# Optimizing a Trainium2 kernel written in Bass

```python
import math
import jax, jax.numpy as jnp
from jax import lax
import numpy as np

D_MODEL = 2048
BATCH = 1
SEQ = 256
DEPTH = 2

CHUNK = 64
N_MIXERS = 3
EPS = 1e-6
DA_HEAD_DIM = 128
DA_HEADS = D_MODEL // (2 * DA_HEAD_DIM)
DA_VALUE_DIM = 2 * DA_HEAD_DIM
Q_BLOCK = 128
S5_GROUP = 16
S5_GROUPS = D_MODEL // S5_GROUP
S5_STATE = 64
S5_DT_MIN = 0.001
S5_DT_MAX = 0.1
RET_QK_DIM = 256
RET_HEADS = D_MODEL // RET_QK_DIM
RET_V_DIM = 2 * RET_QK_DIM
ROPE_BASE = 10000.0
D_FF = 4 * D_MODEL
N_A = (DEPTH + N_MIXERS - 1) // N_MIXERS
N_B = (DEPTH + N_MIXERS - 2) // N_MIXERS
N_C = DEPTH // N_MIXERS


F32 = jnp.float32

def rmsnorm(x, g):
    xf = x.astype(F32)
    y = xf * lax.rsqrt(jnp.mean(xf * xf, axis=-1, keepdims=True) + EPS)
    return (y * g.astype(F32)).astype(x.dtype)

def rotary(t, pos):
    half = t.shape[-1] // 2
    inv = 1.0 / (ROPE_BASE ** jnp.linspace(0.0, 1.0, half, dtype=F32))
    ang = pos[:, None] * inv[None, :]
    cos = jnp.cos(ang)[None, :, None, :]
    sin = jnp.sin(ang)[None, :, None, :]
    t1, t2 = t[..., :half], t[..., half:]
    return jnp.concatenate([t1 * cos - t2 * sin, t1 * sin + t2 * cos], axis=-1)

def diff_attention(h, w_in, lam_p, subln_g, w_out, lambda_init):
    B, S, D = h.shape
    q, k, v = jnp.split(h @ w_in, 3, axis=-1)
    q = q.reshape(B, S, DA_HEADS, 2, DA_HEAD_DIM).astype(F32) * DA_HEAD_DIM ** -0.5
    k = k.reshape(B, S, DA_HEADS, 2, DA_HEAD_DIM).astype(F32)
    v = v.reshape(B, S, DA_HEADS, DA_VALUE_DIM).astype(F32)
    lp = lam_p.astype(F32)
    lam = jnp.exp(jnp.sum(lp[0] * lp[1])) - jnp.exp(jnp.sum(lp[2] * lp[3])) + lambda_init
    n_blk = S // Q_BLOCK
    k_chunk = jnp.arange(S) // CHUNK
    q_blocks = q.reshape(B, n_blk, Q_BLOCK, DA_HEADS, 2, DA_HEAD_DIM).swapaxes(0, 1)

    def block(args):
        qb, bi = args
        q_chunk = (bi * Q_BLOCK + jnp.arange(Q_BLOCK)) // CHUNK
        mask = k_chunk[None, :] <= q_chunk[:, None]
        s = jnp.einsum('bqhtd,bkhtd->bhtqk', qb, k)
        p = jax.nn.softmax(jnp.where(mask, s, -jnp.inf), axis=-1)
        pd = p[:, :, 0] - lam * p[:, :, 1]
        return jnp.einsum('bhqk,bkhe->bqhe', pd, v)

    o = lax.map(block, (q_blocks, jnp.arange(n_blk)))
    o = o.swapaxes(0, 1).reshape(B, S, DA_HEADS, DA_VALUE_DIM)
    o = o * lax.rsqrt(jnp.mean(o * o, axis=-1, keepdims=True) + EPS)
    o = o * subln_g.astype(F32) * (1.0 - lambda_init)
    return o.reshape(B, S, D).astype(h.dtype) @ w_out

def _scan_combine(first, second):
    a1r, a1i, b1r, b1i = first
    a2r, a2i, b2r, b2i = second
    ar = a2r * a1r - a2i * a1i
    ai = a2r * a1i + a2i * a1r
    br = a2r * b1r - a2i * b1i + b2r
    bi = a2r * b1i + a2i * b1r + b2i
    return (ar, ai, br, bi)

def s5_mixer(h, a_re, a_im, log_dt, b_re, b_im, c_re, c_im, d_skip, w_glu):
    B, S, D = h.shape
    lam_re = a_re.astype(F32)
    lam_im = a_im.astype(F32)
    dt = jnp.exp(log_dt.astype(F32))[:, None]
    mag = jnp.exp(lam_re * dt)
    ab_re = mag * jnp.cos(lam_im * dt)
    ab_im = mag * jnp.sin(lam_im * dt)
    den = lam_re * lam_re + lam_im * lam_im
    nr, ni = ab_re - 1.0, ab_im
    coef_re = (nr * lam_re + ni * lam_im) / den
    coef_im = (ni * lam_re - nr * lam_im) / den
    br, bim = b_re.astype(F32), b_im.astype(F32)
    bb_re = coef_re[..., None] * br - coef_im[..., None] * bim
    bb_im = coef_re[..., None] * bim + coef_im[..., None] * br
    cr, ci = c_re.astype(F32), c_im.astype(F32)
    a_seq_re = jnp.broadcast_to(ab_re, (S, S5_GROUPS, S5_STATE))
    a_seq_im = jnp.broadcast_to(ab_im, (S, S5_GROUPS, S5_STATE))
    u = h.astype(F32).reshape(B, S, S5_GROUPS, S5_GROUP)

    def per_sequence(u_s):
        bu_re = jnp.einsum('sgc,gpc->sgp', u_s, bb_re)
        bu_im = jnp.einsum('sgc,gpc->sgp', u_s, bb_im)
        _, _, x_re, x_im = lax.associative_scan(
            _scan_combine, (a_seq_re, a_seq_im, bu_re, bu_im), axis=0)
        return jnp.einsum('sgp,gcp->sgc', x_re, cr) - jnp.einsum('sgp,gcp->sgc', x_im, ci)

    y = lax.map(per_sequence, u).reshape(B, S, D)
    y = y + d_skip.astype(F32) * h.astype(F32)
    g = jax.nn.gelu(y).astype(h.dtype)
    val, gate = jnp.split(g @ w_glu, 2, axis=-1)
    return val * jax.nn.sigmoid(gate)

def retention_mixer(h, w_in, w_out):
    B, S, D = h.shape
    proj = h @ w_in
    q, k, v, g = jnp.split(proj, [D, 2 * D, 4 * D], axis=-1)
    pos = jnp.arange(S, dtype=F32)
    q = rotary(q.reshape(B, S, RET_HEADS, RET_QK_DIM).astype(F32), pos)
    k = rotary(k.reshape(B, S, RET_HEADS, RET_QK_DIM).astype(F32), pos) * RET_QK_DIM ** -0.5
    v = v.reshape(B, S, RET_HEADS, RET_V_DIM).astype(F32)
    log_gamma = jnp.log(1.0 - jnp.exp2(-5.0 - jnp.arange(RET_HEADS, dtype=F32)))
    idx = jnp.arange(CHUNK, dtype=F32)
    intra_decay = jnp.exp(log_gamma[:, None, None] * jnp.abs(idx[:, None] - idx[None, :]))
    q_decay = jnp.exp(log_gamma[None, :] * (idx[:, None] + 1.0))
    k_decay = jnp.exp(log_gamma[None, :] * (CHUNK - 1.0 - idx[:, None]))
    chunk_decay = jnp.exp(log_gamma * CHUNK)
    n_ch = S // CHUNK

    def to_chunks(t):
        return t.reshape(B, n_ch, CHUNK, *t.shape[2:]).swapaxes(0, 1)

    def step(R, inp):
        qc, kc, vc = inp
        s = jnp.einsum('bnhd,bmhd->bhnm', qc, kc) * intra_decay
        o = jnp.einsum('bhnm,bmhe->bnhe', s, vc)
        o = o + jnp.einsum('bnhd,bhde->bnhe', qc * q_decay[..., None], R)
        R = R * chunk_decay[None, :, None, None] + jnp.einsum(
            'bmhd,bmhe->bhde', kc * k_decay[..., None], vc)
        return R, o

    R0 = jnp.zeros((B, RET_HEADS, RET_QK_DIM, RET_V_DIM), F32)
    _, o = lax.scan(step, R0, (to_chunks(q), to_chunks(k), to_chunks(v)))
    o = o.swapaxes(0, 1).reshape(B, S, RET_HEADS, RET_V_DIM)
    o = o * lax.rsqrt(jnp.mean(o * o, axis=-1, keepdims=True) + EPS)
    o = (jax.nn.silu(g.astype(F32)) * o.reshape(B, S, RET_HEADS * RET_V_DIM)).astype(h.dtype)
    return o @ w_out

def sqrelu_mlp(h, w1, w2):
    a = jax.nn.relu(h @ w1)
    return (a * a) @ w2

def first_inputs(seed: int = 0) -> dict:
    key = jax.random.key(seed)
    ks = jax.random.split(key, 24)
    D = D_MODEL

    def w(k, shape, fan_in):
        return jax.random.normal(k, shape, F32) * fan_in ** -0.5

    def gain(k, shape):
        return 1.0 + 0.02 * jax.random.normal(k, shape, F32)

    G, P, C = S5_GROUPS, S5_STATE, S5_GROUP
    return {
        "x": jax.random.normal(ks[0], (BATCH, SEQ, D), F32),
        "norm_mix": gain(ks[1], (DEPTH, D)),
        "norm_mlp": gain(ks[2], (DEPTH, D)),
        "norm_final": gain(ks[3], (D,)),
        "a_w_in": w(ks[4], (N_A, D, 3 * D), D),
        "a_lambda": 0.1 * jax.random.normal(ks[5], (N_A, 4, DA_HEAD_DIM), F32),
        "a_subln": gain(ks[6], (N_A, DA_VALUE_DIM)),
        "a_w_out": w(ks[7], (N_A, D, D), D),
        "b_a_re": -0.5 + 0.01 * jax.random.normal(ks[8], (N_B, G, P), F32),
        "b_a_im": jnp.pi * jnp.arange(P, dtype=F32)[None, None, :]
                  + 0.01 * jax.random.normal(ks[9], (N_B, G, P), F32),
        "b_log_dt": jax.random.uniform(ks[10], (N_B, G), F32,
                                       math.log(S5_DT_MIN), math.log(S5_DT_MAX)),
        "b_b_re": w(ks[11], (N_B, G, P, C), 2 * C),
        "b_b_im": w(ks[12], (N_B, G, P, C), 2 * C),
        "b_c_re": w(ks[13], (N_B, G, C, P), 2 * P),
        "b_c_im": w(ks[14], (N_B, G, C, P), 2 * P),
        "b_d": jax.random.normal(ks[15], (N_B, D), F32),
        "b_w_glu": w(ks[16], (N_B, D, 2 * D), D),
        "c_w_in": w(ks[17], (N_C, D, 6 * D), D),
        "c_w_out": w(ks[18], (N_C, 2 * D, D), 2 * D),
        "mlp_w1": w(ks[19], (DEPTH, D, D_FF), D),
        "mlp_w2": w(ks[20], (DEPTH, D_FF, D), D_FF),
    }

def first_block(x, norm_mix, norm_mlp, norm_final, a_w_in, a_lambda, a_subln, a_w_out,
              b_a_re, b_a_im, b_log_dt, b_b_re, b_b_im, b_c_re, b_c_im, b_d, b_w_glu,
              c_w_in, c_w_out, mlp_w1, mlp_w2):
    for i in range(DEPTH):
        kind = i % N_MIXERS
        j = i // N_MIXERS
        h = rmsnorm(x, norm_mix[i])
        if kind == 0:
            lambda_init = 0.8 - 0.6 * math.exp(-0.3 * i)
            mix = diff_attention(h, a_w_in[j], a_lambda[j], a_subln[j], a_w_out[j], lambda_init)
        elif kind == 1:
            mix = s5_mixer(h, b_a_re[j], b_a_im[j], b_log_dt[j], b_b_re[j], b_b_im[j],
                           b_c_re[j], b_c_im[j], b_d[j], b_w_glu[j])
        else:
            mix = retention_mixer(h, c_w_in[j], c_w_out[j])
        x = x + mix
        x = x + sqrelu_mlp(rmsnorm(x, norm_mlp[i]), mlp_w1[i], mlp_w2[i])
    return rmsnorm(x, norm_final)


DEPTH_2 = 1

FOX_HEAD_DIM = 128
FOX_WIDTH = D_MODEL // 2
FOX_HEADS = FOX_WIDTH // FOX_HEAD_DIM
RWKV_HEAD_DIM = 64
RWKV_WIDTH = D_MODEL // 2
RWKV_HEADS = RWKV_WIDTH // RWKV_HEAD_DIM
DECAY_LORA = max(32, int(round(D_MODEL ** 0.5 * 1.8 / 32)) * 32)
AAA_LORA = max(32, int(round(D_MODEL ** 0.5 * 1.8 / 32)) * 32)
RMS_EPS = 1e-6
GN_EPS = 64e-5
L2_EPS = 1e-12

FOX_SIZES = (FOX_WIDTH, FOX_WIDTH, FOX_WIDTH, FOX_WIDTH, FOX_HEADS)
RWKV_SIZES = (RWKV_WIDTH, RWKV_WIDTH, RWKV_WIDTH, RWKV_WIDTH, DECAY_LORA, AAA_LORA)
FOX_COLS = sum(FOX_SIZES)
RWKV_COLS = sum(RWKV_SIZES)
IN_COLS = FOX_COLS + RWKV_COLS + 2 * D_MODEL


def _split(u, sizes):
    idx = [int(i) for i in np.cumsum(sizes)[:-1]]
    return jnp.split(u, idx, axis=-1)

def _rmsnorm(x, g):
    xf = x.astype(jnp.float32)
    y = xf * lax.rsqrt(jnp.mean(xf * xf, axis=-1, keepdims=True) + RMS_EPS)
    return (y * g.astype(jnp.float32)).astype(x.dtype)

def _token_shift(u, mu):
    prev = jnp.pad(u, ((0, 0), (1, 0), (0, 0)))[:, :-1]
    return u + (prev - u) * mu

def _fox_attention(q, k, v, log_f):
    c = jnp.cumsum(log_f, axis=-1)
    T = q.shape[2]
    scale = FOX_HEAD_DIM ** -0.5
    outs = []
    for i in range(T // Q_BLOCK):
        s0, e = i * Q_BLOCK, (i + 1) * Q_BLOCK
        qb, kb, vb = q[:, :, s0:e], k[:, :, :e], v[:, :, :e]
        logits = (jnp.einsum('bhqd,bhkd->bhqk', qb, kb) * scale
                  + c[:, :, s0:e, None] - c[:, :, None, :e])
        causal = jnp.arange(e)[None, :] <= jnp.arange(s0, e)[:, None]
        logits = jnp.where(causal, logits, -jnp.inf)
        p = jax.nn.softmax(logits, axis=-1)
        outs.append(jnp.einsum('bhqk,bhkd->bhqd', p, vb))
    return jnp.concatenate(outs, axis=2)

def _rwkv7_scan(r, decay, k, v, kk, b):
    B, T, H, N = r.shape
    S0 = jnp.zeros((B, H, N, N), jnp.float32)
    xs = tuple(jnp.moveaxis(t, 1, 0) for t in (r, decay, k, v, kk, b))

    def step(S, inp):
        r_t, w_t, k_t, v_t, kk_t, b_t = inp
        sa = jnp.einsum('bhvk,bhk->bhv', S, -kk_t)
        S = (S * w_t[:, :, None, :] + sa[..., None] * b_t[:, :, None, :]
             + v_t[..., None] * k_t[:, :, None, :])
        y = jnp.einsum('bhvk,bhk->bhv', S, r_t)
        return S, y

    _, ys = lax.scan(step, S0, xs)
    return jnp.moveaxis(ys, 0, 1)

def _hybrid_layer(x, norm_gain, w_in, fox_forget_bias, rwkv_shift_mix, rwkv_w0, rwkv_w2,
                  rwkv_a0, rwkv_a2, rwkv_k_k, rwkv_k_a, rwkv_r_k, rwkv_ln_w, rwkv_ln_b,
                  w_proj_fox, w_proj_rwkv, w_out):
    B, T, _ = x.shape
    f32 = jnp.float32
    h = _rmsnorm(x, norm_gain)
    u = h @ w_in
    u_fox, u_rwkv, g_a, g_b = _split(u, (FOX_COLS, RWKV_COLS, D_MODEL, D_MODEL))

    q, k, v, z_a, f_logit = _split(u_fox.astype(f32), FOX_SIZES)
    to_heads = lambda t: t.reshape(B, T, FOX_HEADS, FOX_HEAD_DIM).transpose(0, 2, 1, 3)
    log_f = jax.nn.log_sigmoid(f_logit + fox_forget_bias.astype(f32)).transpose(0, 2, 1)
    o_a = _fox_attention(to_heads(q), to_heads(k), to_heads(v), log_f)
    o_a = o_a.transpose(0, 2, 1, 3).reshape(B, T, FOX_WIDTH) * jax.nn.silu(z_a)

    u_rwkv = _token_shift(u_rwkv.astype(f32), rwkv_shift_mix.astype(f32))
    r, kr, vr, z_b, w_down, a_down = _split(u_rwkv, RWKV_SIZES)
    w = -jax.nn.softplus(-(rwkv_w0.astype(f32) + jnp.tanh(w_down) @ rwkv_w2.astype(f32))) - 0.5
    decay = jnp.exp(-jnp.exp(w))
    a = jax.nn.sigmoid(rwkv_a0.astype(f32) + a_down @ rwkv_a2.astype(f32))
    heads = lambda t: t.reshape(B, T, RWKV_HEADS, RWKV_HEAD_DIM)
    kk = heads(kr * rwkv_k_k.astype(f32))
    kk = kk / jnp.maximum(jnp.sqrt(jnp.sum(kk * kk, axis=-1, keepdims=True)), L2_EPS)
    kr = kr * (1.0 + (a - 1.0) * rwkv_k_a.astype(f32))
    rh, kh, vh, ah = heads(r), heads(kr), heads(vr), heads(a)
    y = _rwkv7_scan(rh, heads(decay), kh, vh, kk, kk * ah)
    mu = jnp.mean(y, axis=-1, keepdims=True)
    var = jnp.mean(jnp.square(y - mu), axis=-1, keepdims=True)
    y = ((y - mu) * lax.rsqrt(var + GN_EPS)).reshape(B, T, RWKV_WIDTH)
    y = y * rwkv_ln_w.astype(f32) + rwkv_ln_b.astype(f32)
    bonus = jnp.sum(rh * kh * rwkv_r_k.astype(f32), axis=-1, keepdims=True) * vh
    o_b = (y + bonus.reshape(B, T, RWKV_WIDTH)) * jax.nn.silu(z_b)

    o_a = o_a.astype(x.dtype) @ w_proj_fox
    o_b = o_b.astype(x.dtype) @ w_proj_rwkv
    m = jax.nn.sigmoid(g_a) * o_a + jax.nn.sigmoid(g_b) * o_b
    return x + m @ w_out

def second_inputs(seed: int = 0) -> dict:
    key = jax.random.key(seed)
    ks = jax.random.split(key, 20)
    n = jax.random.normal
    L, D = DEPTH_2, D_MODEL
    return {
        "x": n(ks[0], (BATCH, SEQ, D), jnp.float32),
        "norm_gain": 1.0 + 0.05 * n(ks[1], (L, D), jnp.float32),
        "w_in": n(ks[2], (L, D, IN_COLS), jnp.float32) * D ** -0.5,
        "fox_forget_bias": 3.0 + 0.5 * n(ks[3], (L, FOX_HEADS), jnp.float32),
        "rwkv_shift_mix": jax.random.uniform(ks[4], (L, RWKV_COLS), jnp.float32),
        "rwkv_w0": jax.random.uniform(ks[5], (L, RWKV_WIDTH), jnp.float32, -6.5, -1.5),
        "rwkv_w2": n(ks[6], (L, DECAY_LORA, RWKV_WIDTH), jnp.float32) * 0.5 * DECAY_LORA ** -0.5,
        "rwkv_a0": 0.1 * n(ks[7], (L, RWKV_WIDTH), jnp.float32),
        "rwkv_a2": n(ks[8], (L, AAA_LORA, RWKV_WIDTH), jnp.float32) * AAA_LORA ** -0.5,
        "rwkv_k_k": 0.85 + 0.05 * n(ks[9], (L, RWKV_WIDTH), jnp.float32),
        "rwkv_k_a": 1.0 + 0.05 * n(ks[10], (L, RWKV_WIDTH), jnp.float32),
        "rwkv_r_k": -0.04 + 0.02 * n(ks[11], (L, RWKV_HEADS, RWKV_HEAD_DIM), jnp.float32),
        "rwkv_ln_w": 1.0 + 0.05 * n(ks[12], (L, RWKV_WIDTH), jnp.float32),
        "rwkv_ln_b": 0.02 * n(ks[13], (L, RWKV_WIDTH), jnp.float32),
        "w_proj_fox": n(ks[14], (L, FOX_WIDTH, D), jnp.float32) * FOX_WIDTH ** -0.5,
        "w_proj_rwkv": n(ks[15], (L, RWKV_WIDTH, D), jnp.float32) * RWKV_WIDTH ** -0.5,
        "w_out": n(ks[16], (L, D, D), jnp.float32) * D ** -0.5,
        "final_norm_gain": 1.0 + 0.05 * n(ks[17], (D,), jnp.float32),
    }

def second_block(x, norm_gain, w_in, fox_forget_bias, rwkv_shift_mix, rwkv_w0, rwkv_w2,
              rwkv_a0, rwkv_a2, rwkv_k_k, rwkv_k_a, rwkv_r_k, rwkv_ln_w, rwkv_ln_b,
              w_proj_fox, w_proj_rwkv, w_out, final_norm_gain):
    h = x
    for l in range(DEPTH_2):
        h = _hybrid_layer(h, norm_gain[l], w_in[l], fox_forget_bias[l], rwkv_shift_mix[l],
                          rwkv_w0[l], rwkv_w2[l], rwkv_a0[l], rwkv_a2[l], rwkv_k_k[l],
                          rwkv_k_a[l], rwkv_r_k[l], rwkv_ln_w[l], rwkv_ln_b[l],
                          w_proj_fox[l], w_proj_rwkv[l], w_out[l])
    return _rmsnorm(h, final_norm_gain)


def setup_inputs(seed=0):
    out = dict(first_inputs(seed))
    for name, value in second_inputs(seed + 1).items():
        if name != "x":
            out[name + "_2"] = value
    return out


def reference(
    x, norm_mix, norm_mlp, norm_final, a_w_in, a_lambda, a_subln, a_w_out, b_a_re, b_a_im,
    b_log_dt, b_b_re, b_b_im, b_c_re, b_c_im, b_d, b_w_glu, c_w_in, c_w_out, mlp_w1, mlp_w2,
    norm_gain_2, w_in_2, fox_forget_bias_2, rwkv_shift_mix_2, rwkv_w0_2, rwkv_w2_2, rwkv_a0_2,
    rwkv_a2_2, rwkv_k_k_2, rwkv_k_a_2, rwkv_r_k_2, rwkv_ln_w_2, rwkv_ln_b_2, w_proj_fox_2,
    w_proj_rwkv_2, w_out_2, final_norm_gain_2,
):
    x = first_block(
        x, norm_mix, norm_mlp, norm_final, a_w_in, a_lambda, a_subln, a_w_out, b_a_re, b_a_im,
        b_log_dt, b_b_re, b_b_im, b_c_re, b_c_im, b_d, b_w_glu, c_w_in, c_w_out, mlp_w1, mlp_w2,
    )
    return second_block(
        x, norm_gain_2, w_in_2, fox_forget_bias_2, rwkv_shift_mix_2, rwkv_w0_2, rwkv_w2_2,
        rwkv_a0_2, rwkv_a2_2, rwkv_k_k_2, rwkv_k_a_2, rwkv_r_k_2, rwkv_ln_w_2, rwkv_ln_b_2,
        w_proj_fox_2, w_proj_rwkv_2, w_out_2, final_norm_gain_2,
    )


_drawn_inputs = setup_inputs


def setup_inputs(seed=0):
    import zlib

    import numpy as np

    out = dict(_drawn_inputs(seed))
    spreads = {}
    factors = {'a_subln': 3.411,
     'b_a_re': 64.0,
     'b_a_im': 30.12,
     'b_log_dt': 36.576,
     'b_b_re': 41.192,
     'b_b_im': 44.288,
     'b_c_re': 42.984,
     'b_c_im': 45.912,
     'fox_forget_bias_2': 21.92,
     'rwkv_w2_2': 4.965,
     'rwkv_a0_2': 5.784,
     'rwkv_r_k_2': 3.746,
     'rwkv_ln_w_2': 4.389,
     'rwkv_ln_b_2': 8.0}
    for name, (base, spread) in spreads.items():
        noise = np.random.default_rng([zlib.crc32(name.encode()), seed]).standard_normal(out[name].shape)
        drawn = base * np.exp(spread * noise) if base else spread * noise
        out[name] = __import__('jax').numpy.asarray(drawn.astype(out[name].dtype))
    for name, factor in factors.items():
        out[name] = (out[name] * factor).astype(out[name].dtype)
    return out
```

```python
import math
from contextlib import ExitStack

import concourse.bass as bass
from concourse import mybir

F32 = mybir.dt.float32
F32R = mybir.dt.float32r
ALU = mybir.AluOpType
ACT = mybir.ActivationFunctionType
AX = mybir.AxisListType.X

P = 128
S = 256
MT = S // P
D = 2048
KT = D // P
NW = 512
UK = 2
UNITS = KT // UK
HALF = UNITS // 2
RAW = 4
SPLIT = 4
GROUPS = KT // 2
FB = 4
EPS = 1e-6
NEG = -1.0e30

DA_HEADS = 8
DA_HD = 128
DA_VD = 256
DA_ITEMS = DA_HEADS * MT
LAMBDA_INIT = 0.8 - 0.6 * math.exp(-0.3 * 0)

H1 = D // 2
F_HD = 128
F_HEADS = H1 // F_HD
F_ITEMS = F_HEADS * MT
F_SCALE = F_HD ** -0.5
R_HD = 64
R_HEADS = H1 // R_HD
R_PAIRS = R_HEADS // 2
LORA = 96
LC = F_HEADS + 2 * LORA
GN_EPS = 64e-5
L2_EPS = 1e-12
NEG_DECAY = -math.exp(-0.5)
R_LOADS = 7
TC = 64
LEVELS = 5

S5_C = 16
S5_P = 64
S5_GROUPS = D // S5_C
S5_PAIRS = S5_GROUPS // 2
TWO_PI_A = 6.28125
TWO_PI_B = 8117.0 / 2 ** 22
TWO_PI_C = 2 * math.pi - TWO_PI_A - TWO_PI_B
ROUND = 1.5 * 2 ** 23
PI_BELOW = 3.1415925
S5_STEPS = 41
S5_PHASES = 35
TG = 4
S5_START = 4 + 2 * (12 + 4 + 8 * FB)
MASK_STEPS = 63


def masked(i):
    return 3 * (i // 2) + (3 if i % 2 else 1)


class Steps:

    def __init__(self, names):
        self.value = {name: i + 1 for i, name in enumerate(names)}
        assert len(self.value) == len(names)
        self.passed = 0

    def __getitem__(self, name):
        return self.value[name]

    def mark(self, sem, ins, *name):
        self.passed += 1
        assert self.value[name] == self.passed, (name, self.passed, self.value[name])
        ins.then_inc(sem, 1)


def fox_steps():
    pe = [("shift", 0)] + [("lT",), ("cum",)] + [(n, i) for k in range(F_ITEMS + 1) for n, i in
         ([("fs", k)] if k < F_ITEMS else []) + ([("ft", k - 1), ("fv", k - 1)] if k else [])]
    act = [("lo", 0), ("lo", 1), ("tanh",), ("lT",), ("fe",), ("fl",), ("nc",)] + \
          [(n, i) for k in range(F_ITEMS + 1) for n, i in
           ([("fe", k)] if k < F_ITEMS else []) + ([("ft", k - 1), ("fv", k - 1)] if k else [])] + [("sz", 0), ("sz", 1)]
    dve = [("bias", 0), ("bias", 1), ("lmul", 0), ("ladd", 0), ("lmul", 1), ("ladd", 1), ("abs",), ("min",), ("lf",)]
    for k in range(F_ITEMS + 1):
        if k < F_ITEMS:
            dve += ([("fc", k)] if k % 2 else []) + [("fm", k), ("fx", k), ("fn", k)]
        if k:
            dve += [("fr", k - 1), ("fp", k - 1)]
    for m in range(MT):
        dve += [("oz", m), ("og", m)]
    return pe, act, dve


def rwkv_steps():
    pe, act, dve = [], [], []
    for m in range(MT):
        pe += [("lin", m), ("cum", m)]
        act += [("sqrt", m), ("sigw", m), ("siga", m), ("E0", m), ("E1", m), ("E2", m), ("E3", m), ("lam", m)]
        dve += [("kk0", m), ("kk2", m), ("kks", m), ("kkm", m), ("kkr", m), ("kk", m)]
        dve += [("linw", m, q) for q in range(2)] + [("lina", m, q) for q in range(2)]
        dve += [("ka", m), ("k'", m), ("b", m), ("bo0", m), ("bo1", m), ("bon", m)]
        dve += [("kkh", m), ("rh", m), ("bh", m), ("kh", m), ("bt", m), ("kt", m)]
        pe += [("T", m, i) for i in range(8)]
        act += [("T", m, i) for i in range(8)]
        for g in range(2):
            pe += [("A", m, g, h) for h in range(8)]
            dve += [("A", m, g, h) for h in range(8)]
            pe += [("L", m, g), ("AV", m, g)]
            act += [("AV", m, g)]
            dve += [("x0", m, g, e) for e in range(2)] + [("xt0", m, g), ("X", m, g, 0), ("XT", m, g, 0)]
            for lv in range(1, LEVELS + 1):
                pe += [("Q", m, g, lv, k) for k in range(2)] + [("XQ", m, g, lv, k) for k in range(2)]
                dve += [("Q", m, g, lv, k) for k in range(2)]
                for k in range(2):
                    dve += ([("X", m, g, lv, k)] if lv < LEVELS else []) + [("XT", m, g, lv, k)]
            pe += [("U", m, g), ("W", m, g), ("R", m, g), ("Y", m, g)]
            act += [("U", m, g), ("W", m, g), ("Y", m, g)]
            dve += [("R", m, g)]
        pe += [("M", m, c) for c in range(2)] + [("N", m, c) for c in range(2)]
        dve += [("M", m, c, q) for c in range(2) for q in range(2)] + [("N", m, c, q) for c in range(2) for q in range(2)]
        for c in range(2):
            pe += [("S", m, c), ("O", m, c)]
            dve += [("sl", m, c)] + [("sb", m, c, q) for q in range(2)] + [("S", m, c)]
        dve += [("O", m, q) for q in range(2)]
        dve += [("mu", m), ("nm", m), ("yc", m), ("y2", m), ("vs", m)]
        act += [("sd", m), ("sz", m)]
        dve += [("sr", m), ("yn", m), ("yw", m), ("yb", m), ("bv", m), ("yv", m), ("zz", m), ("ob", m)]
    return pe, act, dve


class Tally:

    def __init__(self):
        self.chunk = 0
        self.extra = 0
        self.fill = 0
        self.group = 0
        self.high = 0
        self.norm = 0
        self.square = 0
        self.x_ready = 0


def build(nc, I, out):
    with ExitStack() as ctx:
        def sb(name, shape, dt=F32):
            return ctx.enter_context(nc.sbuf_tensor(name, shape, dt))

        def sem(name):
            return ctx.enter_context(nc.semaphore(name))

        regions = {}

        def area(name, kib):
            base = (nc.sbuf_base + 31) // 32 * 32
            sb(name, [P, kib * 256])
            regions[name] = (base, kib * 1024)

        def at(region, offset_kib, name, shape, dt=F32):
            base, size = regions[region]
            nbytes = 4 * math.prod(shape[1:])
            assert offset_kib * 1024 + nbytes <= size, (name, offset_kib, nbytes, size)
            return nc.alloc_sbuf_tensor_at(name, shape, dt, offset=base + int(offset_kib * 1024))

        X = sb("X", [P, MT, D])
        raw = sb("raw", [P, RAW, UK, NW])
        wH = sb("wH", [P, SPLIT, UK, NW], F32R)
        wL = sb("wL", [P, SPLIT, UK, NW], F32R)
        area("stg", 8)
        area("gain", 8)
        stg = at("stg", 0, "stgs", [P, 2, MT, NW])
        gain = at("gain", 0, "gains", [P, D])
        area("xt", 32)
        area("hid", 32)
        area("mix", 48)
        xH = at("xt", 0, "xH", [P, KT, S], F32R)
        xL = at("xt", 16, "xL", [P, KT, S], F32R)
        hH = at("hid", 0, "hH", [P, KT, S], F32R)
        hL = at("hid", 16, "hL", [P, KT, S], F32R)
        xn = at("mix", 0, "xn", [P, MT, D])
        qT = at("hid", 0, "qT", [P, KT, S])
        kT = at("hid", 16, "kT", [P, KT, S])
        va = at("mix", 0, "va", [P, MT, D])
        oa = at("mix", 16, "oa", [P, MT, D])
        ms = at("mix", 32, "ms", [P, 2, 2, S])
        pd = at("mix", 36, "pd", [P, 2, S])
        pT = at("mix", 38, "pT", [P, 2, MT, P])
        osq = at("mix", 40, "osq", [P, DA_VD])
        subg = at("mix", 41, "subg", [P, DA_VD])
        lamv = at("mix", 42, "lamv", [P, 4, DA_HD])
        lamp = at("mix", 44, "lamp", [P, 2, DA_HD])
        sb_b = at("mix", 0, "sb_b", [P, 2, S5_P, S5_C])
        sb_bb = at("mix", 8, "sb_bb", [P, S5_C, 2, S5_P])
        sb_c = at("mix", 16, "sb_c", [P, 2, KT, 2, S5_P])
        sb_t = at("mix", 32, "sb_t", [P, S5_P, S5_C])
        sv = at("gain", 0, "sv", [P, 22, S5_P])
        pks = at("gain", 5.5, "pks", [P, 3, 2, S5_P])
        cpad = at("mix", 32, "cpad", [P, S5_PAIRS, 2, 2, S5_C])
        powr = at("mix", 0, "powr", [P, 2, 2, S5_PAIRS, 16])
        ptmp = at("gain", 0, "ptmp", [P, 2, S5_PAIRS, 8])
        epow = at("gain", 4, "epow", [P, 4, S5_PAIRS])
        tmul = at("gain", 0, "tmul", [P, 2, TG, S])
        tmade = at("mix", 16, "tmade", [P, 2, TG, 2, S])
        tab = at("xt", 0, "tab", [P, 2, TG, 2, S])
        zz = at("xt", 16, "zz", [P, 2, 2, S])
        zc = at("xt", 20, "zc", [P, 2, 2, S])
        zs5 = at("xt", 24, "zs5", [P, 2, 2, S])
        rot = at("stg", 0, "rot", [P, 2, 2, S])
        vv = at("stg", 4, "vv", [P, 2, S])
        bpad = at("stg", 6, "bpad", [P, 2, 2, 2, S5_P])
        uT = at("hid", 0, "uT", [P, KT, S])
        bbT = at("hid", 16, "bbT", [P, KT, 2, S5_P])
        skip = at("hid", 24, "skip", [P, D])
        fq = at("mix", 0, "fq", [P, F_HEADS, S])
        fk = at("mix", 8, "fk", [P, F_HEADS, S])
        fv = at("mix", 16, "fv", [P, MT, H1])
        fz = at("mix", 24, "fz", [P, MT, H1])
        mixmu = at("mix", 32, "mixmu", [P, 4 * H1])
        fms = at("mix", 32, "fms", [P, 2, S])
        fpd = at("mix", 34, "fpd", [P, 2, S])
        fpT = at("mix", 36, "fpT", [P, 2, MT, P])
        fo = at("mix", 40, "fo", [P, MT, H1])
        rr = at("hid", 0, "rr", [P, MT, H1])
        kr = at("hid", 8, "kr", [P, MT, H1])
        vr = at("hid", 16, "vr", [P, MT, H1])
        zb = at("hid", 24, "zb", [P, MT, H1])
        kkrT = at("mix", 0, "kkrT", [P, R_PAIRS, 2, P])
        bkT = at("mix", 8, "bkT", [P, R_PAIRS, 2, P])
        A4 = at("mix", 16, "A4", [P, 8, 4, P])
        nU = at("mix", 32, "nU", [P, H1])
        nW = at("mix", 36, "nW", [P, H1])
        kkh = at("mix", 40, "kkh", [P, H1])
        bt = at("mix", 44, "bt", [P, H1])
        w0p = at("mix", 0, "w0p", [P, H1])
        a0p = at("mix", 4, "a0p", [P, H1])
        kkp = at("mix", 8, "kkp", [P, H1])
        kap = at("mix", 12, "kap", [P, H1])
        lnw = at("mix", 0, "lnw", [P, H1])
        lnb = at("mix", 4, "lnb", [P, H1])
        sg = at("mix", 16, "sg", [P, H1])
        sa = at("mix", 20, "sa", [P, H1])
        kk = at("mix", 24, "kk", [P, H1])
        bb = at("mix", 28, "bb", [P, H1])
        E0 = at("mix", 32, "E0", [P, H1])
        E1 = at("mix", 36, "E1", [P, H1])
        E2 = at("xt", 8, "E2", [P, H1])
        E3 = at("xt", 12, "E3", [P, H1])
        rkp = at("xt", 24, "rkp", [P, H1])
        tmp = at("xt", 28, "tmp", [P, H1])
        XA = at("xt", 8, "XA", [P, 8, P])
        XT = at("xt", 12, "XT", [P, 8, P])
        QQ = at("xt", 24, "QQ", [P, 8, P])
        AV = at("xt", 28, "AV", [P, 8, R_HD])
        MM = at("xt", 8, "MM", [P, 2, R_PAIRS, P])
        NN = at("xt", 24, "NN", [P, 2, R_PAIRS, P])
        yy = at("stg", 0, "yy", [P, MT, H1])
        ST = at("gain", 0, "ST", [P, 2, R_PAIRS, P])
        y2 = at("mix", 32, "y2", [P, H1])
        zs = at("mix", 36, "zs", [P, H1])
        shtmp = at("gain", 0, "shtmp", [P, MT, NW])
        lo = at("gain", 4, "lo", [P, MT, LC])
        lmu = at("gain", 5.75, "lmu", [P, 2 * LORA])
        fbias = at("gain", 6.5, "fbias", [P, F_HEADS])
        lf = at("gain", 6.75, "lf", [P, 3, MT, F_HEADS])
        ltmp = at("gain", 0, "ltmp", [P, MT, 2 * LORA])
        gg = at("mix", 0, "gg", [P, 2, 2, MT, NW])
        lw2 = at("mix", 40, "lw2", [LORA, 2, H1])
        gates_dram = nc.dram_tensor("gates_scratch", (2, S, D), F32, kind="Internal").ap()
        lT = sb("lT", [LORA, 2, S])
        nct = sb("nct", [F_HEADS, S])
        rsm = sb("rsm", [P, 10, R_HEADS])
        lamT = sb("lamT", [P, R_PAIRS, 2])
        cmask = sb("cmask", [P, P])
        tri = sb("tri", [P, P])
        ones = sb("ones", [P, P])
        same = sb("same", [P, P])
        mask2 = sb("mask2", [P, 2, P])
        decay = sb("decay", [P, 3, P])
        tot = sb("tot", [P, 2])
        shift = sb("shift", [P, P])
        corner = sb("corner", [P, P])
        level = sb("level", [P, LEVELS + 2, P])
        fstat = sb("fstat", [P, 8])
        pe_names, act_names, dve_names = fox_steps()
        rpe_names, ract_names, rdve_names = rwkv_steps()
        FPE, FACT, FDVE = Steps(pe_names), Steps(act_names), Steps(dve_names)
        RPE, RACT, RDVE = Steps(rpe_names), Steps(ract_names), Steps(rdve_names)
        srs = sb("srs", [P, 3, S5_PAIRS])
        pmask = sb("pmask", [P, 8])
        tab_dram = nc.dram_tensor("tab_scratch", (S5_PAIRS // TG, P, TG, 2, S), F32, kind="Internal").ap()
        bb_dram = nc.dram_tensor("bb_scratch", (P, S5_C, 2, S5_P), F32, kind="Internal").ap()
        small = sb("small", [P, 256])
        ss = small[:, 0:2]
        std = small[:, 2:4]
        rstd = small[:, 4:6]
        amx = small[:, 8:12].rearrange("p (b t) -> p b t", b=2)
        anm = small[:, 12:16].rearrange("p (b t) -> p b t", b=2)
        asum = small[:, 16:20].rearrange("p (b t) -> p b t", b=2)
        ars = small[:, 20:24].rearrange("p (b t) -> p b t", b=2)
        ac1 = small[:, 24:26]
        lams = small[:, 26:28]
        lame = small[:, 28:30]
        nlam = small[:, 30:31]
        oss = small[:, 32:48]
        ostd = small[:, 48:64]
        orstd = small[:, 64:80]
        eps = small[:, 80:81]
        gn_eps = small[:, 81:82]
        ident = sb("ident", [P, P])
        dmask = sb("dmask", [P, P])

        acc = [[ctx.enter_context(nc.psum_tensor(f"acc{a}{m}", [P, NW], F32)) for m in range(MT)] for a in range(2)]
        tp = [ctx.enter_context(nc.psum_tensor(f"tp{b}", [P, 2, S], F32)) for b in range(2)]
        wk = [ctx.enter_context(nc.psum_tensor(f"wk{b}", [P, 2, S], F32)) for b in range(2)]

        raw_in = [sem(f"raw_in{j}") for j in range(RAW)]
        high_done = sem("high_done")
        split_done = sem("split_done")
        unit_used = sem("unit_used")
        acc_free = sem("acc_free")
        gain_in = sem("gain_in")
        x_in = sem("x_in")
        sumsq_done = sem("sumsq_done")
        std_done = sem("std_done")
        rstd_done = sem("rstd_done")
        xn_done = sem("xn_done")
        group_done = sem("group_done")
        group_high = sem("group_high")
        group_free = sem("group_free")
        stg_done = sem("stg_done")
        relu_done = sem("relu_done")
        const_a = sem("const_a")
        const_b = sem("const_b")
        mask_step = sem("mask_step")
        lam_in = sem("lam_in")
        lam_step = sem("lam_step")
        lam_exp = sem("lam_exp")
        score_done = sem("score_done")
        mask_done = sem("mask_done")
        max_done = sem("max_done")
        nmax_done = sem("nmax_done")
        exp_done = sem("exp_done")
        coef_step = sem("coef_step")
        prob_done = sem("prob_done")
        pv_done = sem("pv_done")
        o_out = sem("o_out")
        o_norm = sem("o_norm")
        out_done = sem("out_done")
        s5_in = sem("s5_in")
        s5_act = sem("s5_act")
        s5_step = sem("s5_step")
        s5_pool = sem("s5_pool")
        s5_turn = sem("s5_turn")
        s5_back = sem("s5_back")
        s5_out = sem("s5_out")
        pad_turn = sem("pad_turn")
        pad_done = sem("pad_done")
        bu_done = sem("bu_done")
        tab_step = sem("tab_step")
        tab_out = [sem("tab_out0"), sem("tab_out1")]
        tab_turn = sem("tab_turn")
        tab_in = [sem("tab_in0"), sem("tab_in1")]
        s5_cin = sem("s5_cin")
        skip_in = sem("skip_in")
        rot_done = sem("rot_done")
        v_done = sem("v_done")
        scan_done = sem("scan_done")
        zc_done = sem("zc_done")
        zs_done = sem("zs_done")
        xr_done = sem("xr_done")
        y_done = sem("y_done")
        skip_done = sem("skip_done")
        gelu_done = sem("gelu_done")
        gate_done = sem("gate_done")
        glu_done = sem("glu_done")
        glu_added = sem("glu_added")
        shift_done = sem("shift_done")
        shift_out = sem("shift_out")
        shift_mul = sem("shift_mul")
        gate_out = [sem("gate_out0"), sem("gate_out1")]
        f_in = sem("f_in")
        f_pe, f_act, f_dve = sem("f_pe"), sem("f_act"), sem("f_dve")
        r_in = sem("r_in")
        r_in2 = sem("r_in2")
        r_pe, r_act, r_dve = sem("r_pe"), sem("r_act"), sem("r_dve")
        gates_in = [sem("gates_in0"), sem("gates_in1")]
        mix_mul = sem("mix_mul")
        mix_done = sem("mix_done")
        fin_done = sem("fin_done")

        block = ctx.enter_context(nc.Block())

        @block.sync
        def _(sp):
            t = Tally()

            def load(c, j, src):
                sp.wait_ge(split_done, c * UNITS + (j + 1))
                sp.dma_start(raw[:, j % RAW], src).then_inc(raw_in[j % RAW], 16)

            def stream(w, n):
                c0 = t.chunk
                wv = w.rearrange("(u k p) n -> u p k n", k=UK, p=P)
                with sp.Fori(0, n) as i:
                    for j in range(UNITS):
                        load(i + c0, j, wv[j][:, :, bass.ds(i * NW, NW)])
                t.chunk += n

            def stream_mlp(w1, w2):
                c0 = t.chunk
                w1v = w1.rearrange("(u k p) n -> u p k n", k=UK, p=P)
                w2v = w2.rearrange("(b r) n -> b r n", r=D)
                with sp.Fori(0, FB) as b:
                    for c in range(4):
                        for j in range(UNITS):
                            load(b * 8 + (c0 + c), j, w1v[j][:, :, bass.ds(b * D + c * NW, NW)])
                    for c in range(4):
                        for j in range(UNITS):
                            rows = w2[bass.ds(b * D + j * UK * P, UK * P), c * NW:(c + 1) * NW]
                            load(b * 8 + (c0 + 4 + c), j, rows.rearrange("(k p) n -> p k n", p=P))
                t.chunk += 8 * FB

            def s5_tables_back():
                sp.wait_ge(acc_free, S5_START)
                for b in range(2):
                    sp.wait_ge(tab_out[b], 16 * (S5_PAIRS // TG // 2))
                    sp.dma_start(tab[:, b], tab_dram[b]).then_inc(tab_in[b], 16)
                with sp.Fori(1, S5_PAIRS // TG // 2) as i:
                    for b in range(2):
                        sp.wait_ge(y_done, i * (2 * TG) + (TG * b - TG + 2))
                        sp.dma_start(tab[:, b], tab_dram[bass.ds(i * 2 + b, 1)].rearrange("o p a c s -> (o p) a c s")
                                     ).then_inc(tab_in[b], 16)

            sp.dma_start(X[:], I["x"][0].rearrange("(m p) n -> p m n", p=P)).then_inc(x_in, 16)
            stream(I["a_w_in"][0], 12)
            stream(I["a_w_out"][0], 4)
            stream_mlp(I["mlp_w1"][0], I["mlp_w2"][0])
            c0 = t.chunk
            glu = [I["b_w_glu"][0][:, h * D:(h + 1) * D].rearrange("(u k p) n -> u p k n", k=UK, p=P) for h in (1, 0)]
            for c in range(8):
                for j in range(UNITS):
                    load(c0 + c, j, glu[c % 2][j][:, :, (c // 2) * NW:(c // 2 + 1) * NW])
                if c == 0:
                    s5_tables_back()
            t.chunk += 8
            stream_mlp(I["mlp_w1"][1], I["mlp_w2"][1])
            w = I["w_in_2"][0]
            stream(w[:, 0:4 * H1], 8)
            stream(w[:, 4 * H1 + F_HEADS:8 * H1 + F_HEADS], 8)
            stream(w[:, 8 * H1 + LC:], 8)
            c0 = t.chunk
            for j in range(UNITS):
                rows = w[j * UK * P:(j + 1) * UK * P]
                sp.wait_ge(split_done, c0 * UNITS + j + 1)
                sp.dma_start(raw[:, j % RAW, :, 0:F_HEADS],
                             rows[:, 4 * H1:4 * H1 + F_HEADS].rearrange("(k p) n -> p k n", p=P)).then_inc(raw_in[j % RAW], 16)
                sp.dma_start(raw[:, j % RAW, :, F_HEADS:LC],
                             rows[:, 8 * H1 + F_HEADS:8 * H1 + LC].rearrange("(k p) n -> p k n", p=P)).then_inc(raw_in[j % RAW], 16)
            t.chunk += 1
            c0 = t.chunk
            proj = [I[n][0].rearrange("(u k p) n -> u p k n", k=UK, p=P) for n in ("w_proj_fox_2", "w_proj_rwkv_2")]
            with sp.Fori(0, 4) as i:
                for j in range(UNITS):
                    load(i + c0, j, proj[j // HALF][j % HALF][:, :, bass.ds(i * NW, NW)])
            t.chunk += 4
            stream(I["w_out_2"][0], 4)
            for m in range(MT):
                sp.wait_ge(fin_done, m + 1)
                sp.dma_start(out[0, m * P:m * P + P], xn[:, m]).then_inc(out_done, 16)
            sp.wait_ge(out_done, 32)

        @block.gpsimd
        def _(pool):
            norms = [I["norm_mix"][0:1], I["norm_mlp"][0:1], I["norm_mix"][1:2], I["norm_mlp"][1:2],
                     I["norm_final"].unsqueeze(0), I["norm_gain_2"][0:1], I["final_norm_gain_2"].unsqueeze(0)]

            nc.gpsimd.memset(ident[:], 0.0).then_inc(const_a, 1)
            nc.gpsimd.memset(eps, EPS).then_inc(const_a, 1)
            nc.gpsimd.memset(gn_eps, GN_EPS).then_inc(const_b, 1)
            nc.gpsimd.memset(dmask[:], 0.0).then_inc(const_a, 1)
            pool.wait_ge(const_a, 3)
            nc.gpsimd.affine_select(out=ident[:], in_=ident[:], compare_op=ALU.not_equal, fill=1.0, base=0,
                                    pattern=[[-1, P]], channel_multiplier=1).then_inc(const_b, 1)
            nc.gpsimd.memset(dmask[0:64, 64:128], NEG).then_inc(const_b, 1)
            nc.gpsimd.memset(pmask[:], 1.0).then_inc(const_a, 1)
            pool.wait_ge(const_a, 4)
            nc.gpsimd.affine_select(out=pmask[:], in_=pmask[:], compare_op=ALU.is_ge, fill=0.0, base=0,
                                    pattern=[[-S5_C, 8]], channel_multiplier=1).then_inc(const_a, 1)
            pool.wait_ge(const_a, 5)
            nc.gpsimd.affine_select(out=pmask[:], in_=pmask[:], compare_op=ALU.is_ge, fill=0.0, base=S5_C - 1,
                                    pattern=[[S5_C, 8]], channel_multiplier=-1).then_inc(const_b, 1)

            def second_layer_masks():
                mk = [0]

                def mlink(ins):
                    mk[0] += 1
                    ins.then_inc(mask_step, 1)
                    pool.wait_ge(mask_step, mk[0])

                def keep(t, pattern, base, mult, fill=0.0, op=ALU.is_ge):
                    mlink(nc.gpsimd.affine_select(out=t, in_=t, compare_op=op, fill=fill, base=base,
                                                  pattern=pattern, channel_multiplier=mult))

                def blocks(t, v):
                    mlink(nc.gpsimd.memset(t, 0.0))
                    for g in range(2):
                        h = slice(64 * g, 64 * g + 64)
                        mlink(nc.gpsimd.memset(t[h, h], v))

                mlink(nc.gpsimd.memset(cmask[:], 0.0))
                keep(cmask[:], [[-1, P]], 0, 1, NEG)
                mlink(nc.gpsimd.memset(tri[:], 1.0))
                keep(tri[:], [[1, P]], 0, -1)
                mlink(nc.gpsimd.memset(ones[:], 1.0))
                blocks(same[:], 1.0)
                for e in range(2):
                    blocks(mask2[:, e], 1.0)
                    keep(mask2[:, e], [[1, P]], e - 1, -1)
                    blocks(decay[:, e], NEG_DECAY)
                    keep(decay[:, e], [[1, P]], e - 1, -1)
                blocks(decay[:, 2], NEG_DECAY)
                keep(decay[:, 2], [[-1, P]], -1, 1)
                mlink(nc.gpsimd.memset(tot[:], 0.0))
                for g in range(2):
                    mlink(nc.gpsimd.memset(tot[64 * g:64 * g + 64, g:g + 1], NEG_DECAY))
                mlink(nc.gpsimd.memset(shift[:], 0.0))
                keep(shift[:], [[1, P]], -1, -1, 1.0, ALU.not_equal)
                keep(shift[:], [[1, P]], 0, -1, -1.0, ALU.not_equal)
                mlink(nc.gpsimd.memset(corner[:], 0.0))
                keep(corner[:], [[-P, P]], -(P - 1), 1, 1.0, ALU.not_equal)
                for lv in range(LEVELS + 1):
                    w = 1 << lv
                    lm = level[:, lv + 1 if lv else 0].rearrange("p (n e w) -> p n e w", e=2, w=w)
                    mlink(nc.gpsimd.memset(level[:, lv + 1 if lv else 0], 1.0 if lv else -1.0))
                    mlink(nc.gpsimd.memset(lm[:, :, 1], 0.0))
                    keep(lm[:, :, 0], [[-2 * w, P // (2 * w)], [0, w]], -w, 1)
                    keep(lm[:, :, 0], [[2 * w, P // (2 * w)], [0, w]], 2 * w - 1, -1)
                lm = level[:, 1].rearrange("p (n e) -> p n e", e=2)
                mlink(nc.gpsimd.memset(level[:, 1], 0.0))
                keep(lm[:, :, 1], [[-2, P // 2]], 0, 1, -1.0, ALU.not_equal)
                mlink(nc.gpsimd.memset(fstat[:], 0.0))
                assert mk[0] == MASK_STEPS, mk[0]

            def s5_tables():
                n = [0]

                def link(ins):
                    n[0] += 1
                    ins.then_inc(s5_pool, 1)
                    pool.wait_ge(s5_pool, n[0])

                pool.wait_ge(s5_step, S5_STEPS)
                link(nc.gpsimd.memset(cpad[:], 0.0))
                pool.wait_ge(s5_back, 2)
                pool.wait_ge(s5_out, 16)

                def times(dr, di, ar, ai, br, bi, shape):
                    w = shape[-1]
                    ta, tb = ptmp[:, 0, :, 0:w], ptmp[:, 1, :, 0:w]
                    link(nc.gpsimd.tensor_tensor(ta, ar, br, ALU.mult))
                    link(nc.gpsimd.tensor_tensor(tb, ai, bi, ALU.mult))
                    link(nc.gpsimd.tensor_tensor(dr, ta, tb, ALU.subtract))
                    link(nc.gpsimd.tensor_tensor(ta, ar, bi, ALU.mult))
                    link(nc.gpsimd.tensor_tensor(tb, ai, br, ALU.mult))
                    link(nc.gpsimd.tensor_tensor(di, ta, tb, ALU.add))

                er, ei = srs[:, 1], srs[:, 2]
                flip = 0
                for a in range(2):
                    link(nc.gpsimd.memset(powr[:, a, 0, :, 0:1], 1.0))
                    link(nc.gpsimd.memset(powr[:, a, 1, :, 0:1], 0.0))
                    for lvl in range(4):
                        w = 1 << lvl
                        sh = [P, S5_PAIRS, w]
                        times(powr[:, a, 0, :, w:2 * w], powr[:, a, 1, :, w:2 * w],
                              powr[:, a, 0, :, 0:w], powr[:, a, 1, :, 0:w],
                              er.unsqueeze(2).broadcast_to(sh), ei.unsqueeze(2).broadcast_to(sh), sh)
                        nr, ni = epow[:, flip], epow[:, flip + 1]
                        times(nr.unsqueeze(2), ni.unsqueeze(2), er.unsqueeze(2), ei.unsqueeze(2),
                              er.unsqueeze(2), ei.unsqueeze(2), [P, S5_PAIRS, 1])
                        er, ei = nr, ni
                        flip = 2 - flip

                pool.wait_ge(s5_back, 18)
                sh = [P, TG, 16, 16]
                four = lambda t: t.rearrange("p a (h l) -> p a h l", h=16)
                ta, tb = four(tmul[:, 0]), four(tmul[:, 1])

                def pair_tables(i, first=False):
                    for b in range(2):
                        pairs = bass.ds(i * (2 * TG) + TG * b, TG)
                        hi = [powr[:, 1, c, pairs].unsqueeze(3).broadcast_to(sh) for c in range(2)]
                        lo = [powr[:, 0, c, pairs].unsqueeze(2).broadcast_to(sh) for c in range(2)]
                        if not first:
                            pool.wait_ge(tab_out[b], i * 16)
                            nc.gpsimd.sem_inc(tab_turn, 1)
                        for c in range(2):
                            nc.gpsimd.tensor_tensor(ta, hi[0], lo[c], ALU.mult).then_inc(tab_step, 1)
                            nc.gpsimd.tensor_tensor(tb, hi[1], lo[1 - c], ALU.mult).then_inc(tab_step, 1)
                            pool.wait_ge(tab_step, i * 12 + (6 * b + 3 * c + 2))
                            nc.gpsimd.tensor_tensor(four(tmade[:, b, :, c]), ta, tb, ALU.add if c else ALU.subtract
                                                    ).then_inc(tab_step, 1)
                            pool.wait_ge(tab_step, i * 12 + (6 * b + 3 * c + 3))
                            nc.gpsimd.sem_inc(tab_turn, 1)
                        pool.dma_start(tab_dram[bass.ds(i * 2 + b, 1)].rearrange("o p a c s -> (o p) a c s"),
                                       tmade[:, b]).then_inc(tab_out[b], 16)

                pair_tables(0, first=True)
                with pool.Fori(1, S5_PAIRS // TG // 2) as i:
                    pair_tables(i)

            def s5_states():
                nc.gpsimd.sem_inc(zc_done, 2)
                with pool.Fori(0, S5_PAIRS // (2 * TG)) as i:
                    for q in range(2 * TG):
                        b = q % 2
                        cos = tab[:, q // TG, q % TG, 0:1].broadcast_to([P, 2, S])
                        pool.wait_ge(scan_done, i * (4 * TG) + (2 * q + 2))
                        pool.wait_ge(y_done, i * (2 * TG) + (q + 1))
                        nc.gpsimd.tensor_tensor(zc[:, b], zz[:, b], cos, ALU.mult).then_inc(zc_done, 1)
                        pool.wait_ge(zc_done, i * (2 * TG) + (q + 3))
                        pool.wait_ge(zs_done, i * (2 * TG) + (q + 1))
                        nc.gpsimd.tensor_tensor(zc[:, b, 0], zc[:, b, 0], zs5[:, b, 1], ALU.subtract).then_inc(xr_done, 1)

            for n, g in enumerate(norms):
                if n:
                    pool.wait_ge(xn_done, 2 * n)
                if n == 6:
                    pool.wait_ge(mix_done, 2)
                if n == 2:
                    s5_tables()
                pool.dma_start(gain[:], g.broadcast_to([P, D])).then_inc(gain_in, 16)
                if n == 0:
                    second_layer_masks()
                if n == 2:
                    s5_states()

        @block.tensor
        def _(pe):
            t = Tally()

            def product(c, fill, par, aH, aL, mid=None, first=None, n=NW):
                pe.wait_ge(acc_free, fill * 2 + 2)
                for j in range(UNITS):
                    if j == HALF and mid is not None:
                        mid()
                    if first is not None:
                        first(j)
                    pe.wait_ge(split_done, c * UNITS + (j + 1 + RAW))
                    for u in range(UK):
                        k = j * UK + u
                        for m in range(MT):
                            rows = slice(m * P, m * P + P)
                            bank = acc[par][m][:, 0:n]
                            nc.tensor.matmul(bank, aH[:, k, rows], wH[:, j % SPLIT, u, 0:n], start=k == 0, stop=False)
                            nc.tensor.matmul(bank, aH[:, k, rows], wL[:, j % SPLIT, u, 0:n], start=False, stop=False)
                            last = nc.tensor.matmul(bank, aL[:, k, rows], wH[:, j % SPLIT, u, 0:n],
                                                    start=False, stop=k == KT - 1)
                    last.then_inc(unit_used, 1)

            def turn(n, blocks):
                pe.wait_ge(group_free, n + 1)
                for src, dst in blocks:
                    last = nc.tensor.transpose(dst, src, ident[:])
                last.then_inc(group_done, 1)

            def turn_wide(src):
                for g in range(GROUPS):
                    n = t.group + g
                    turn(n, [(src[:, m, (2 * g + k) * P:(2 * g + k + 1) * P], tp[g % 2][:, k, m * P:m * P + P])
                             for k in range(2) for m in range(MT)])
                t.group += GROUPS

            def ready(n0):
                return lambda j: pe.wait_ge(group_free, n0 + j + 3)

            def turn_stg(n, par):
                for g in range(2):
                    turn(n + g, [(stg[:, par, m, (2 * g + k) * P:(2 * g + k + 1) * P],
                                  tp[g][:, k, m * P:m * P + P]) for k in range(2) for m in range(MT)])

            def norm_turn():
                pe.wait_ge(xn_done, 2 * t.norm + 2)
                n0 = t.group
                turn_wide(xn)
                t.norm += 1
                return ready(n0)

            def plain(n, aH, aL, first=None):
                c0, f0 = t.chunk, t.fill
                if first is not None:
                    product(c0, f0, 0, aH, aL, first=first)
                    product(c0 + 1, f0 + 1, 1, aH, aL)
                    done = 2
                else:
                    done = 0
                with pe.Fori(0, n - done, 2) as i:
                    for par in range(2):
                        product(i + (c0 + done + par), i + (f0 + done + par), par, aH, aL)
                t.chunk += n
                t.fill += n

            def mlp(after=None):
                first = norm_turn()
                c0, f0, g0, q0 = t.chunk, t.fill, t.group, t.square

                def block_of(b, first=None, after=None):
                    def turned(c):
                        def mid():
                            pe.wait_ge(stg_done, b * 8 + (q0 + 2 * c + 2))
                            turn_stg(b * 8 + (g0 + 2 * c), c % 2)
                        return mid
                    for c in range(4):
                        product(b * 8 + (c0 + c), b * 8 + (f0 + c), c % 2, xH, xL,
                                mid=turned(c - 1) if c else None, first=first if c == 0 else None)
                        if after:
                            after(c)
                    for c in range(4):
                        product(b * 8 + (c0 + 4 + c), b * 8 + (f0 + 4 + c), c % 2, hH, hL,
                                mid=turned(3) if c == 0 else None,
                                first=(lambda j: pe.wait_ge(group_free, b * 8 + (g0 + j + 3))) if c == 0 else None)
                        if after:
                            after(4 + c)

                block_of(0, first, after)
                with pe.Fori(1, FB) as b:
                    block_of(b)
                t.chunk += 8 * FB
                t.fill += 8 * FB
                t.group += 8 * FB
                t.square += 8 * FB

            nc.tensor.sem_inc(unit_used, SPLIT)
            pe.wait_ge(const_b, 4)
            first = norm_turn()
            c0, f0, g0, q0 = t.chunk, t.fill, t.group, t.square

            def qk_turn(c):
                def mid():
                    pe.wait_ge(acc_free, 2 * (f0 + c) + 6)
                    turn_stg(g0 + 2 * c, c % 2)
                return mid
            for c in range(8):
                product(c0 + c, f0 + c, c % 2, xH, xL, mid=qk_turn(c - 1) if c else None, first=first if c == 0 else None)
            t.chunk += 8
            t.fill += 8
            for c in range(8, 12):
                product(c0 + c, f0 + c, c % 2, xH, xL, mid=qk_turn(7) if c == 8 else None)
            t.chunk += 4
            t.fill += 4
            t.group += 16
            pe.wait_ge(acc_free, 4 + 2 * t.fill)
            pe.wait_ge(group_free, t.group + 2)

            def scores(i):
                h, qt = i // 2, i % 2
                nk = (qt + 1) * P
                if i >= 2:
                    pe.wait_ge(mask_done, masked(i - 2))
                for b in range(2):
                    last = nc.tensor.matmul(wk[i % 2][:, b, 0:nk], qT[:, 2 * h + b, qt * P:qt * P + P],
                                            kT[:, 2 * h + b, 0:nk], start=True, stop=True)
                last.then_inc(score_done, 1)

            def values(i):
                h, qt = i // 2, i % 2
                pe.wait_ge(prob_done, i + 1)
                turn(t.group, [(pd[:, i % 2, k * P:k * P + P], tp[t.group % 2][:, 0, k * P:k * P + P])
                               for k in range(qt + 1)])
                pe.wait_ge(group_free, t.group + 3)
                if i >= 2:
                    pe.wait_ge(o_out, i - 1)
                for k in range(qt + 1):
                    last = nc.tensor.matmul(acc[i % 2][0][:, 0:DA_VD], pT[:, i % 2, k],
                                            va[:, k, h * DA_VD:(h + 1) * DA_VD], start=k == 0, stop=k == qt)
                last.then_inc(pv_done, 1)
                t.group += 1

            for i in range(DA_ITEMS + 1):
                if i < DA_ITEMS:
                    scores(i)
                if i:
                    values(i - 1)
            pe.wait_ge(o_norm, DA_ITEMS)
            n0 = t.group
            turn_wide(oa)
            plain(4, xH, xL, first=ready(n0))

            def s5_turns(c):
                if c == 2:
                    pe.wait_ge(s5_step, S5_PHASES)
                    for j in range(3):
                        last = nc.tensor.transpose(wk[0][:].rearrange("p a s -> p (a s)")[:, j * P:j * P + P],
                                                   pks[:, j].rearrange("p a s -> p (a s)"), ident[:])
                    last.then_inc(s5_turn, 1)
                if c < 4:
                    return
                pe.wait_ge(s5_cin, 64)
                pe.wait_ge(s5_back, 2 + 4 * (c - 4))
                for b in range(2 * (c - 4), 2 * (c - 4) + 2):
                    bank = wk[b % 2][:].rearrange("p a s -> p (a s)")
                    for k in range(4):
                        last = nc.tensor.transpose(bank[:, k * P:k * P + P],
                                                   sb_c[:, b // 4, (b % 4) * 4 + k].rearrange("p a s -> p (a s)"), ident[:])
                    last.then_inc(s5_turn, 1)

            mlp(after=s5_turns)
            norm_turn()
            nc.tensor.sem_inc(bu_done, 2)
            nc.tensor.sem_inc(y_done, 2)
            pe.wait_ge(group_free, 2 + t.group)

            def inputs_of(s, k, b):
                pe.wait_ge(pad_done, s * 2 + 2)
                pe.wait_ge(rot_done, s * 2 + 2)
                for c in range(2):
                    last = nc.tensor.matmul(wk[b][:, c], bpad[:, b, c].rearrange("p a s -> p (a s)"),
                                            uT[:, bass.ds(k, 1)].rearrange("p o s -> p (o s)"), start=True, stop=True)
                last.then_inc(bu_done, 1)

            def outputs_of(s, s_ds, col, r, b):
                pe.wait_ge(xr_done, s + 1)
                for m in range(MT):
                    cols = slice(m * P, m * P + P)
                    for n, (z, c) in enumerate(((zc[:, b, 0, cols], 0), (zc[:, b, 1, cols], 1), (zs5[:, b, 0, cols], 1))):
                        last = nc.tensor.matmul(acc[r][m][:, col], z, cpad[:, s_ds, c].rearrange("p o g c -> p (o g c)"),
                                                start=n == 0, stop=n == 2)
                last.then_inc(y_done, 1)

            def pairs_of(r, i, final=False):
                for q in range(2 * TG):
                    if not (final and q >= 2 * TG - 2):
                        k = i * 2 + (4 * r + (q + 2) // 4)
                        inputs_of(i * (2 * TG) + (16 * r + q + 2), k, q % 2)
                    s = i * (2 * TG) + (16 * r + q)
                    outputs_of(s, bass.ds(s, 1), bass.ds(i * (64 * TG) + 32 * q, 32), r % 2, q % 2)

            inputs_of(0, 0, 0)
            inputs_of(1, 0, 1)
            for r in range(4):
                pe.wait_ge(acc_free, 2 * (t.fill + r) + 2)
                if r < 3:
                    with pe.Fori(0, 2) as i:
                        pairs_of(r, i)
                else:
                    pairs_of(r, 0)
                    pairs_of(r, 1, final=True)
            t.fill += 4
            n0 = t.group
            for r in range(4):
                pe.wait_ge(gelu_done, 2 * r + 2)
                for g in range(2 * r, 2 * r + 2):
                    turn(t.group + g, [(xn[:, m, (2 * g + k) * P:(2 * g + k + 1) * P], tp[g % 2][:, k, m * P:m * P + P])
                                       for k in range(2) for m in range(MT)])
            t.group += GROUPS
            plain(8, xH, xL, first=ready(n0))
            mlp()
            pe.wait_ge(mask_step, MASK_STEPS)
            t.norm += 1
            first = norm_turn()
            c0, f0, g0 = t.chunk, t.fill, t.group

            def stg_turn(c):
                def mid():
                    pe.wait_ge(acc_free, 2 * (f0 + c) + 6)
                    turn_stg(g0 + 2 * c, c % 2)
                return mid

            def shifted(c):
                def mid():
                    pe.wait_ge(acc_free, 2 * (f0 + c) + 6)
                    if c > 8:
                        pe.wait_ge(shift_out, 2 * (c - 8))
                    for m in range(MT):
                        bank = wk[m][:].rearrange("p a s -> p (a s)")
                        last = nc.tensor.matmul(bank, shift[:], stg[:, c % 2, m], start=True, stop=m == 0)
                        if m:
                            last = nc.tensor.matmul(bank, corner[:], stg[:, c % 2, 0], start=False, stop=True)
                    last.then_inc(shift_done, 1)
                return mid

            def mid_of(c):
                if 1 <= c <= 4:
                    return stg_turn(c - 1)
                if 9 <= c <= 16:
                    return shifted(c - 1)
            for c in range(18):
                product(c0 + c, f0 + c, c % 2, xH, xL, mid=mid_of(c), first=first if c == 0 else None)
            t.chunk += 18
            t.fill += 18
            t.group += 8
            plain(6, xH, xL)
            product(t.chunk, t.fill, 0, xH, xL, n=LC)
            t.chunk += 1

            pe.wait_ge(f_act, FACT["lo", 1])
            pe.wait_ge(shift_out, 16)
            for m in range(MT):
                bank = wk[m][:].rearrange("p a s -> p (a s)")[:, 0:2 * LORA]
                last = nc.tensor.matmul(bank, shift[:], lo[:, m, F_HEADS:], start=True, stop=m == 0)
                if m:
                    last = nc.tensor.matmul(bank, corner[:], lo[:, 0, F_HEADS:], start=False, stop=True)
            FPE.mark(f_pe, last, "shift", 0)
            pe.wait_ge(f_act, FACT["tanh",])
            bank = acc[1][0][0:LORA].rearrange("p (v s) -> p v s", v=2)
            for v in range(2):
                for m in range(MT):
                    last = nc.tensor.transpose(bank[:, v, m * P:m * P + P],
                                               lo[:, m, F_HEADS + v * LORA:F_HEADS + (v + 1) * LORA], ident[:])
            FPE.mark(f_pe, last, "lT")
            pe.wait_ge(f_dve, FDVE["lf",])
            cbank = acc[1][1][0:F_HEADS]
            nc.tensor.matmul(cbank[:, 0:P], lf[:, 2, 0], tri[:], start=True, stop=True)
            nc.tensor.matmul(cbank[:, P:S], lf[:, 2, 0], ones[:], start=True, stop=False)
            FPE.mark(f_pe, nc.tensor.matmul(cbank[:, P:S], lf[:, 2, 1], tri[:], start=False, stop=True), "cum")

            def fox_scores(i):
                h, qt = i // 2, i % 2
                nk = (qt + 1) * P
                pe.wait_ge(f_act, FACT["nc",])
                if i >= 2:
                    pe.wait_ge(f_dve, FDVE["fm", i - 2])
                bank = wk[i % 2][:, 0, 0:nk]
                nc.tensor.matmul(bank, fq[:, h, qt * P:qt * P + P], fk[:, h, 0:nk], start=True, stop=False)
                FPE.mark(f_pe, nc.tensor.matmul(bank, ident[0:F_HEADS, h:h + 1].broadcast_to([F_HEADS, P]), nct[:, 0:nk],
                                                start=False, stop=True), "fs", i)

            def fox_values(i):
                h, qt = i // 2, i % 2
                pe.wait_ge(f_dve, FDVE["fp", i])
                if i >= 2:
                    pe.wait_ge(f_act, FACT["ft", i - 2])
                for k in range(qt + 1):
                    last = nc.tensor.transpose(tp[i % 2][:, 0, k * P:k * P + P], fpd[:, i % 2, k * P:k * P + P], ident[:])
                FPE.mark(f_pe, last, "ft", i)
                pe.wait_ge(f_act, FACT["ft", i])
                if i >= 2:
                    pe.wait_ge(f_act, FACT["fv", i - 2])
                for k in range(qt + 1):
                    last = nc.tensor.matmul(acc[i % 2][0][:, 0:F_HD], fpT[:, i % 2, k],
                                            fv[:, k, h * F_HD:(h + 1) * F_HD], start=k == 0, stop=k == qt)
                FPE.mark(f_pe, last, "fv", i)

            for i in range(F_ITEMS + 1):
                if i < F_ITEMS:
                    fox_scores(i)
                if i:
                    fox_values(i - 1)

            def turn_half(src, ready):
                for g in range(4):
                    turn(t.group + g, [(src[:, m, (2 * g + k) * P:(2 * g + k + 1) * P], tp[g % 2][:, k, m * P:m * P + P])
                                       for k in range(2) for m in range(MT)])
                t.group += 4

            pe.wait_ge(f_dve, FDVE["og", 1])
            turn_half(fo, None)
            pe.wait_ge(group_free, t.group + 2)

            B = [acc[0][0], acc[0][1], acc[1][0], acc[1][1], tp[0], tp[1], wk[0], wk[1]]
            B = [b[:] if n < 4 else b[:].rearrange("p a s -> p (a s)") for n, b in enumerate(B)]

            def wait(name_act=None, name_dve=None):
                if name_act:
                    pe.wait_ge(r_act, RACT[name_act])
                if name_dve:
                    pe.wait_ge(r_dve, RDVE[name_dve])

            for m in range(MT):
                pe.wait_ge(r_in, R_LOADS * 16 * (m + 1))
                if m:
                    wait(name_dve=("ob", m - 1))
                for v in range(2):
                    for q in range(2):
                        last = nc.tensor.matmul(B[2 * v + q], lT[:, v, m * P:m * P + P], lw2[:, v, q * NW:(q + 1) * NW],
                                                start=True, stop=True)
                RPE.mark(r_pe, last, "lin", m)
                wait(("sigw", m), ("lina", m, 1))
                for e in range(3):
                    for q in range(2):
                        nc.tensor.matmul(B[2 * e + q], decay[:, e], sg[:, q * NW:(q + 1) * NW], start=True, stop=True)
                for p in range(R_PAIRS):
                    last = nc.tensor.matmul(B[6][:, 2 * p:2 * p + 2], sg[:, p * P:p * P + P], tot[:], start=True, stop=True)
                RPE.mark(r_pe, last, "cum", m)
                for i, (src, name) in enumerate(((kkh[:], "kkh"), (rr[:, m], "rh"), (kk[:], "bh"), (sg[:], "kh"))):
                    wait(("lam", m), (name, m))
                    for q in range(2):
                        for p in range(4):
                            c = 4 * q + p
                            last = nc.tensor.transpose(B[2 * i + q][:, p * P:p * P + P], src[:, c * P:c * P + P], ident[:])
                        RPE.mark(r_pe, last, "T", m, 2 * i + q)
                for g in range(2):
                    for h in range(8):
                        p, e = 4 * g + h // 2, h % 2
                        rows = slice(64 * e, 64 * e + 64)
                        if g == 0:
                            wait(("T", m, 7))
                        else:
                            wait(("Y", m, 0), ("R", m, 0))
                        for v in range(2):
                            last = nc.tensor.matmul(B[h][:, v * S:(v + 1) * S], bkT[rows, p, v],
                                                    kkrT[rows, p].rearrange("k v t -> k (v t)"), start=True, stop=True)
                        RPE.mark(r_pe, last, "A", m, g, h)
                    wait(name_dve=("A", m, g, 1))
                    for h in range(8):
                        p, e = 4 * g + h // 2, h % 2
                        rows = slice(64 * e, 64 * e + 64)
                        last = nc.tensor.matmul(B[e][:, (h // 2) * P:(h // 2 + 1) * P], kkrT[rows, p, 0], bkT[rows, p, 0],
                                                start=True, stop=True)
                    RPE.mark(r_pe, last, "L", m, g)
                    wait(name_dve=("A", m, g, 7))
                    for h in range(8):
                        hh = 8 * g + h
                        last = nc.tensor.matmul(B[6][:, h * R_HD:(h + 1) * R_HD], A4[:, h, 2], vr[:, m, hh * R_HD:(hh + 1) * R_HD],
                                                start=True, stop=True)
                    RPE.mark(r_pe, last, "AV", m, g)
                    for lv in range(1, LEVELS + 1):
                        for k in range(2):
                            wait(name_dve=("X", m, g, lv - 1, k) if lv > 1 else ("XT", m, g, 0))
                            for h in range(4 * k, 4 * k + 4):
                                last = nc.tensor.matmul(B[k][:, (h % 4) * P:(h % 4 + 1) * P], A4[:, h, 0], XA[:, h],
                                                        start=True, stop=True)
                            RPE.mark(r_pe, last, "Q", m, g, lv, k)
                        for k in range(2):
                            wait(name_dve=("Q", m, g, lv, k))
                            for h in range(4 * k, 4 * k + 4):
                                cols = slice((h % 4) * P, (h % 4 + 1) * P)
                                if lv < LEVELS:
                                    nc.tensor.matmul(B[2 + k][:, cols], XT[:, h], QQ[:, h], start=True, stop=True)
                                last = nc.tensor.matmul(B[4 + k][:, cols], QQ[:, h], XT[:, h], start=True, stop=True)
                            RPE.mark(r_pe, last, "XQ", m, g, lv, k)
                    wait(("AV", m, g), ("XT", m, g, LEVELS, 1))
                    for name, bank in (("U", 7), ("W", 6)):
                        for h in range(8):
                            hh = 8 * g + h
                            src = kkh[:, hh * R_HD:(hh + 1) * R_HD] if name == "U" else AV[:, h]
                            last = nc.tensor.matmul(B[bank][:, h * R_HD:(h + 1) * R_HD], XT[:, h], src, start=True, stop=True)
                        RPE.mark(r_pe, last, name, m, g)
                    wait(("W", m, g))
                    for h in range(8):
                        hh = 8 * g + h
                        e = h % 2
                        last = nc.tensor.matmul(B[0][64 * e:64 * e + 64, (h // 2) * P:(h // 2 + 1) * P],
                                                nU[:, hh * R_HD:(hh + 1) * R_HD], A4[:, h, 1], start=True, stop=True)
                    RPE.mark(r_pe, last, "R", m, g)
                    for h in range(8):
                        hh = 8 * g + h
                        cols = slice(hh * R_HD, (hh + 1) * R_HD)
                        o = B[1][:, h * R_HD:(h + 1) * R_HD]
                        nc.tensor.matmul(o, A4[:, h, 1], nW[:, cols], start=True, stop=False)
                        last = nc.tensor.matmul(o, A4[:, h, 3], vr[:, m, cols], start=False, stop=True)
                    RPE.mark(r_pe, last, "Y", m, g)
                wait(("Y", m, 1), ("R", m, 1))
                for c in range(2):
                    rows = slice(TC * c, TC * c + TC)
                    for p in range(R_PAIRS):
                        cols = slice(p * P, p * P + P)
                        last = nc.tensor.matmul(B[4 * c + p // 4][:, (p % 4) * P:(p % 4 + 1) * P], nU[rows, cols], bt[rows, cols],
                                                start=True, stop=True)
                    RPE.mark(r_pe, last, "M", m, c)
                for c in range(2):
                    rows = slice(TC * c, TC * c + TC)
                    for p in range(R_PAIRS):
                        cols = slice(p * P, p * P + P)
                        o = B[4 * c + 2 + p // 4][:, (p % 4) * P:(p % 4 + 1) * P]
                        nc.tensor.matmul(o, kr[rows, m, cols], vr[rows, m, cols], start=True, stop=False)
                        last = nc.tensor.matmul(o, bt[rows, cols], nW[rows, cols], start=False, stop=True)
                    RPE.mark(r_pe, last, "N", m, c)
                for c in range(2):
                    wait(name_dve=("N", m, 1, 1))
                    if c:
                        wait(name_dve=("S", m, 0))
                    elif m:
                        wait(name_dve=("S", m - 1, 1))
                    for p in range(R_PAIRS):
                        last = nc.tensor.matmul(B[p // 4][:, (p % 4) * P:(p % 4 + 1) * P], MM[:, c, p], ST[:, c, p],
                                                start=True, stop=True)
                    RPE.mark(r_pe, last, "S", m, c)
                    for p in range(R_PAIRS):
                        last = nc.tensor.matmul(B[2 + p // 4][TC * c:TC * c + TC, (p % 4) * P:(p % 4 + 1) * P],
                                                kkrT[:, p, 1, TC * c:TC * c + TC], ST[:, c, p], start=True, stop=True)
                    RPE.mark(r_pe, last, "O", m, c)
            pe.wait_ge(r_dve, RDVE["ob", 1])
            turn_half(zb, None)

            pe.wait_ge(group_free, t.group + 2)
            c0, f0, g0 = t.chunk, t.fill, t.group

            def mixed_turn(c):
                pe.wait_ge(mix_done, 2 * c + 2)
                turn_stg(g0 + 2 * c, c % 2)
            for c in range(4):
                for j in range(UNITS):
                    par = j // HALF
                    if j % HALF == 0:
                        pe.wait_ge(acc_free, (f0 + 2 * c + par) * 2 + 2)
                        if par and c:
                            mixed_turn(c - 1)
                    pe.wait_ge(split_done, (c0 + c) * UNITS + (j + 1 + RAW))
                    for u in range(UK):
                        k = j * UK + u
                        for m in range(MT):
                            rows = slice(m * P, m * P + P)
                            bank = acc[par][m][:]
                            nc.tensor.matmul(bank, xH[:, k, rows], wH[:, j % SPLIT, u], start=k % 8 == 0, stop=False)
                            nc.tensor.matmul(bank, xH[:, k, rows], wL[:, j % SPLIT, u], start=False, stop=False)
                            last = nc.tensor.matmul(bank, xL[:, k, rows], wH[:, j % SPLIT, u], start=False, stop=k % 8 == 7)
                    last.then_inc(unit_used, 1)
            t.chunk += 4
            t.fill += 8
            t.group += 8

            def last_turn(j):
                if j == 6:
                    mixed_turn(3)
                pe.wait_ge(group_free, g0 + j + 3)
            product(t.chunk, t.fill, 0, hH, hL, first=last_turn)
            for c in range(1, 4):
                product(t.chunk + c, t.fill + c, c % 2, hH, hL)

        @block.scalar
        def _(act):
            t = Tally()

            def split(c, half, small=False):
                for j in range(half * HALF, half * HALF + HALF):
                    loads = j // RAW + 1
                    act.wait_ge(raw_in[j % RAW], c * (16 * UNITS // RAW) + (16 * loads * (2 if small else 1) + t.extra))
                    act.wait_ge(unit_used, c * UNITS + (j + 1))
                    n = LC if small else NW
                    nc.scalar.copy(wH[:, j % SPLIT, :, 0:n], raw[:, j % RAW, :, 0:n]).then_inc(high_done, 1)

            def steps(n, evac, turned=None, small=None):
                c0 = t.chunk
                for k in range(n):
                    split(c0 + k, 1, k == small)
                    if k == small:
                        t.extra = 16 * UNITS // RAW
                    if turned is not None and k:
                        turned(k - 1)
                    split(c0 + k + 1, 0, k + 1 == small)
                    evac(k)
                t.chunk += n

            def done(c):
                act.wait_ge(unit_used, c * UNITS + (UNITS + SPLIT))

            def high(n, nh, bank, dst):
                act.wait_ge(group_done, n + 1)
                nc.scalar.copy(dst, tp[bank][:]).then_inc(group_high, 1)

            def high_wide(dH):
                for g in range(GROUPS):
                    high(t.group + g, None, g % 2, dH[:, 2 * g:2 * g + 2])
                t.group += GROUPS

            def norm():
                for m in range(MT):
                    nc.scalar.activation(xn[:, m], X[:, m], ACT.Square, accum_out=ss[:, m:m + 1]).then_inc(sumsq_done, 1)
                act.wait_ge(sumsq_done, 2 * t.norm + 2)
                nc.scalar.activation(std, ss, ACT.Sqrt, bias=eps, scale=1.0 / D).then_inc(std_done, 1)
                t.norm += 1

            def mlp(before=None, after=None):
                act.wait_ge(acc_free, t.x_ready)
                norm()
                high_wide(xH)
                if before:
                    before()
                c0, f0, g0, q0 = t.chunk, t.fill, t.group, t.square

                def block_of(b, after=None):
                    def turned(c):
                        for g in range(2):
                            high(b * 8 + (g0 + 2 * c + g), None, g, hH[:, 4 * c + 2 * g:4 * c + 2 * g + 2])
                    for c in range(8):
                        split(b * 8 + (c0 + c), 1)
                        if 1 <= c <= 4:
                            turned(c - 1)
                        split(b * 8 + (c0 + c + 1), 0)
                        if c < 4:
                            done(b * 8 + (c0 + c))
                            if c == 0:
                                act.wait_ge(acc_free, b * 16 + (2 * f0 + 4))
                            if c >= 2:
                                act.wait_ge(group_done, b * 8 + (g0 + 2 * (c - 1)))
                            for m in range(MT):
                                nc.scalar.activation(stg[:, c % 2, m], acc[c % 2][m][:], ACT.Relu).then_inc(acc_free, 1)
                        if after:
                            after(c)

                block_of(0, after)
                with act.Fori(1, FB) as b:
                    block_of(b)
                t.chunk += 8 * FB
                t.fill += 8 * FB
                t.group += 8 * FB
                t.square += 8 * FB
                t.x_ready = 4 + 2 * t.fill

            act.wait_ge(const_b, 4)
            act.dma_start(lamv[:], I["a_lambda"].rearrange("o a d -> o (a d)").broadcast_to([P, 4 * DA_HD])).then_inc(lam_in, 16)
            act.dma_start(subg[:], I["a_subln"].broadcast_to([P, DA_VD])).then_inc(lam_in, 16)
            split(0, 0)
            act.wait_ge(x_in, 16)
            norm()
            high_wide(xH)
            act.wait_ge(lam_step, 4)
            nc.scalar.activation(lame, lams, ACT.Exp).then_inc(lam_exp, 1)
            g0 = t.group

            def qk_turned(c):
                for g in range(2):
                    act.wait_ge(group_done, g0 + 2 * c + g + 1)
                    dst = qT if c < 4 else kT
                    k = 4 * (c % 4) + 2 * g
                    nc.scalar.copy(dst[:, k:k + 2], tp[g][:]).then_inc(group_free, 1)

            def qk_out(c):
                done(c)
                if c >= 8:
                    for m in range(MT):
                        nc.scalar.copy(va[:, m, (c - 8) * NW:(c - 7) * NW], acc[c % 2][m][:]).then_inc(acc_free, 1)
                    return
                if c >= 2:
                    act.wait_ge(group_done, g0 + 2 * (c - 1))
                for m in range(MT):
                    nc.scalar.copy(stg[:, c % 2, m], acc[c % 2][m][:]).then_inc(acc_free, 1)

            steps(12, qk_out, turned=lambda c: qk_turned(c) if c < 8 else None)
            t.fill += 12
            t.group += 16

            def exps(i):
                nk = (i % 2 + 1) * P
                act.wait_ge(nmax_done, i + 1)
                for b in range(2):
                    e = ms[:, i % 2, b, 0:nk]
                    nc.scalar.activation(e, e, ACT.Exp, bias=anm[:, i % 2, b:b + 1], scale=DA_HD ** -0.5,
                                         accum_out=asum[:, i % 2, b:b + 1]).then_inc(exp_done, 1)

            def outs(i):
                h, qt = i // 2, i % 2
                act.wait_ge(group_done, t.group + 1)
                if i >= 2:
                    act.wait_ge(pv_done, i - 1)
                nk = (qt + 1) * P
                nc.scalar.copy(pT[:, i % 2].rearrange("p k q -> p (k q)")[:, 0:nk],
                               tp[t.group % 2][:, 0, 0:nk]).then_inc(group_free, 1)
                t.group += 1
                act.wait_ge(pv_done, i + 1)
                o = acc[i % 2][0][:, 0:DA_VD]
                nc.scalar.copy(oa[:, qt, h * DA_VD:(h + 1) * DA_VD], o).then_inc(o_out, 1)

            for i in range(DA_ITEMS + 1):
                if i < DA_ITEMS:
                    exps(i)
                if i:
                    outs(i - 1)
            for i in range(DA_ITEMS):
                h, qt = i // 2, i % 2
                act.wait_ge(o_out, i + 1)
                if i:
                    act.wait_ge(lam_exp, 1 + i)
                nc.scalar.activation(osq[:], oa[:, qt, h * DA_VD:(h + 1) * DA_VD], ACT.Square,
                                     accum_out=oss[:, i:i + 1]).then_inc(lam_exp, 1)
            act.wait_ge(lam_exp, 1 + DA_ITEMS)
            nc.scalar.activation(ostd, oss, ACT.Sqrt, bias=eps, scale=1.0 / DA_VD).then_inc(lam_exp, 1)
            high_wide(xH)
            steps(4, lambda c: None)
            t.fill += 4
            t.x_ready = 4 + 2 * t.fill

            def s5_load():
                act.dma_start(sv[:, 0], I["b_a_re"][0]).then_inc(s5_in, 16)
                act.dma_start(sv[:, 1], I["b_a_im"][0]).then_inc(s5_in, 16)
                act.dma_start(sv[:, 2, 0:1], I["b_log_dt"].rearrange("o g -> g o")).then_inc(s5_in, 16)
                for c, name in enumerate(("b_b_re", "b_b_im")):
                    act.dma_start(sb_b[:, c], I[name][0]).then_inc(s5_in, 16)
                for c, name in enumerate(("b_c_re", "b_c_im")):
                    for twice in range(2):
                        act.dma_start(sb_c[:, c, :, twice], I[name][0].rearrange("(k e) c p -> (e c) k p", e=8)).then_inc(s5_cin, 16)

            def s5_scalars(c):
                if c == 0:
                    act.wait_ge(s5_in, 80)
                    nc.scalar.activation(sv[:, 2, 1:2], sv[:, 2, 0:1], ACT.Exp).then_inc(s5_act, 1)
                if c == 1:
                    act.wait_ge(s5_step, 8)
                    nc.scalar.activation(sv[:, 5], sv[:, 3], ACT.Exp).then_inc(s5_act, 1)
                    nc.scalar.activation(sv[:, 6], sv[:, 7], ACT.Sin).then_inc(s5_act, 1)
                    nc.scalar.activation(sv[:, 8], sv[:, 7], ACT.Sin, scale=0.5).then_inc(s5_act, 1)
                if c == 5:
                    act.wait_ge(s5_step, S5_STEPS)
                    act.dma_start(bb_dram, sb_bb[:]).then_inc(s5_out, 16)

            mlp(before=s5_load, after=s5_scalars)
            act.wait_ge(acc_free, t.x_ready)
            act.wait_ge(s5_out, 16)
            act.dma_start(bbT[:].rearrange("p k c s -> p k (c s)"),
                          bb_dram.rearrange("(k e) c r s -> (e c) k (r s)", e=8)).then_inc(s5_out, 16)
            act.dma_start(skip[:], I["b_d"].broadcast_to([P, D])).then_inc(skip_in, 16)
            for b in range(2):
                act.wait_ge(tab_out[b], 16 * (S5_PAIRS // TG // 2))
            norm()
            for g in range(GROUPS):
                act.wait_ge(group_done, t.group + g + 1)
                nc.scalar.copy(uT[:, 2 * g:2 * g + 2], tp[g % 2][:]).then_inc(group_free, 1)
            t.group += GROUPS
            act.wait_ge(s5_out, 32)

            def gelus(r):
                for m in range(MT):
                    act.wait_ge(acc_free, 2 * (t.fill + r) + 4 + m + 1)
                    y = xn[:, m, r * NW:(r + 1) * NW]
                    nc.scalar.activation(y, y, ACT.Gelu_apprx_tanh).then_inc(gelu_done, 1)

            for r in range(4):
                with act.Fori(0, 4) as k:
                    for q in range(4):
                        act.wait_ge(bu_done, k * 4 + (16 * r + q + 1))
                        act.sem_inc(pad_turn, 1)
                        for g in range(2):
                            nc.scalar.activation(bpad[:, q % 2, :, g], bbT[:, bass.ds(k + 4 * r, 1)].rearrange("p o c s -> p (o c) s"),
                                                 ACT.Copy, scale=pmask[:, 2 * q + g:2 * q + g + 1]).then_inc(pad_done, 1)
                if r >= 2:
                    gelus(r - 2)
            gelus(2)
            gelus(3)
            t.fill += 4
            high_wide(xH)

            c0, f0 = t.chunk, t.fill

            def gate(c):
                if c % 2:
                    return
                done(c0 + c)
                if c:
                    act.wait_ge(glu_added, c)
                for m in range(MT):
                    nc.scalar.activation(stg[:, (c // 2) % 2, m], acc[0][m][:], ACT.Sigmoid).then_inc(acc_free, 1)

            steps(8, gate)
            t.fill += 8
            t.x_ready = 4 + 2 * t.fill
            act.wait_ge(glu_added, 8)
            mlp()
            act.wait_ge(acc_free, t.x_ready)
            norm()
            act.wait_ge(xn_done, 2 * t.norm)
            norm()
            high_wide(xH)
            act.dma_start(mixmu[:], I["rwkv_shift_mix_2"][:, 0:4 * H1].broadcast_to([P, 4 * H1])).then_inc(f_in, 16)
            act.dma_start(lmu[:], I["rwkv_shift_mix_2"][:, 4 * H1:].broadcast_to([P, 2 * LORA])).then_inc(f_in, 16)
            act.dma_start(fbias[:], I["fox_forget_bias_2"].broadcast_to([P, F_HEADS])).then_inc(f_in, 16)
            c0, f0, g0 = t.chunk, t.fill, t.group
            gates = gates_dram.rearrange("g (m p) n -> g p m n", p=P)

            def second_turned(c):
                if c < 4:
                    for g in range(2):
                        act.wait_ge(group_done, g0 + 2 * c + g + 1)
                        dst = fq if c < 2 else fk
                        k = 4 * (c % 2) + 2 * g
                        nc.scalar.copy(dst[:, k:k + 2], tp[g][:]).then_inc(group_free, 1)

            def second_out(c):
                done(c0 + c)
                for m in range(MT):
                    src = acc[c % 2][m][:]
                    if c < 4 or 8 <= c < 16:
                        dst = stg[:, c % 2, m]
                    elif c < 8:
                        dst = (fv if c < 6 else fz)[:, m, (c % 2) * NW:(c % 2 + 1) * NW]
                    elif c < 24:
                        dst = stg[:, c % 2, m]
                    if m == 0:
                        if 2 <= c < 4:
                            act.wait_ge(group_done, g0 + 2 * (c - 1))
                        if 10 <= c < 18:
                            act.wait_ge(shift_out, 2 * (c - 9))
                        if 18 <= c < 24:
                            act.wait_ge(gate_out[c % 2], 16 * ((c - 18) // 2 + 1))
                    if c == 24:
                        FACT.mark(f_act, nc.scalar.copy(lo[:, m], src[:, 0:LC]), "lo", m)
                    elif c >= 16:
                        nc.scalar.activation(dst, src, ACT.Sigmoid).then_inc(acc_free, 1)
                    else:
                        nc.scalar.copy(dst, src).then_inc(acc_free, 1)
                if 16 <= c < 24:
                    act.wait_ge(acc_free, 2 * (f0 + c) + 6)
                    n = c - 16
                    act.dma_start(gates[n // 4][:, :, (n % 4) * NW:(n % 4 + 1) * NW], stg[:, c % 2]).then_inc(gate_out[c % 2], 16)

            steps(25, second_out, turned=second_turned, small=24)
            t.fill += 24
            t.group += 8

            act.wait_ge(f_dve, FDVE["ladd", 1])
            FACT.mark(f_act, nc.scalar.activation(lo[:, :, F_HEADS:F_HEADS + LORA], lo[:, :, F_HEADS:F_HEADS + LORA], ACT.Tanh), "tanh")
            act.wait_ge(f_pe, FPE["lT",])
            FACT.mark(f_act, nc.scalar.copy(lT[:].rearrange("p v s -> p (v s)"), acc[1][0][0:LORA]), "lT")
            act.wait_ge(f_dve, FDVE["abs",])
            FACT.mark(f_act, nc.scalar.activation(lf[:, 1], lf[:, 1], ACT.Exp, scale=-1.0), "fe")
            act.wait_ge(f_act, FACT["fe",])
            FACT.mark(f_act, nc.scalar.activation(lf[:, 1], lf[:, 1], ACT.Ln, bias=1.0), "fl")
            act.wait_ge(f_pe, FPE["cum",])
            FACT.mark(f_act, nc.scalar.activation(nct[:], acc[1][1][0:F_HEADS, 0:S], ACT.Copy, scale=-1.0 / F_SCALE), "nc")

            def fox_exp(i):
                nk = (i % 2 + 1) * P
                act.wait_ge(f_dve, FDVE["fn", i])
                e = fms[:, i % 2, 0:nk]
                FACT.mark(f_act, nc.scalar.activation(e, e, ACT.Exp, bias=fstat[:, 2 + i % 2:3 + i % 2], scale=F_SCALE,
                                                      accum_out=fstat[:, 4 + i % 2:5 + i % 2]), "fe", i)

            def fox_out(i):
                h, qt = i // 2, i % 2
                nk = (qt + 1) * P
                act.wait_ge(f_pe, FPE["ft", i])
                if i >= 2:
                    act.wait_ge(f_pe, FPE["fv", i - 2])
                FACT.mark(f_act, nc.scalar.copy(fpT[:, i % 2].rearrange("p k q -> p (k q)")[:, 0:nk], tp[i % 2][:, 0, 0:nk]), "ft", i)
                act.wait_ge(f_pe, FPE["fv", i])
                FACT.mark(f_act, nc.scalar.copy(fo[:, qt, h * F_HD:(h + 1) * F_HD], acc[i % 2][0][:, 0:F_HD]), "fv", i)

            for i in range(F_ITEMS + 1):
                if i < F_ITEMS:
                    fox_exp(i)
                if i:
                    fox_out(i - 1)
            for m in range(MT):
                FACT.mark(f_act, nc.scalar.activation(fk[:, 4 * m:4 * m + 4].rearrange("p a s -> p (a s)"), fz[:, m], ACT.Sigmoid), "sz", m)

            def high_half(k0):
                for g in range(4):
                    high(t.group + g, None, g % 2, xH[:, k0 + 2 * g:k0 + 2 * g + 2])
                t.group += 4
            high_half(0)

            B = [acc[0][0], acc[0][1], acc[1][0], acc[1][1], tp[0], tp[1], wk[0], wk[1]]
            B = [b[:] if n < 4 else b[:].rearrange("p a s -> p (a s)") for n, b in enumerate(B)]

            def bcast(name, dst, s):
                act.dma_start(dst, I[name].broadcast_to([P, H1])).then_inc(s, 16)

            act.wait_ge(group_free, t.group + 2)
            for m in range(MT):
                if m:
                    act.wait_ge(r_dve, RDVE["ob", m - 1])
                bcast("rwkv_w0_2", w0p[:], r_in)
                bcast("rwkv_a0_2", a0p[:], r_in)
                act.dma_start(lw2[:, 0], I["rwkv_w2_2"][0]).then_inc(r_in, 16)
                act.dma_start(lw2[:, 1], I["rwkv_a2_2"][0]).then_inc(r_in, 16)
                bcast("rwkv_k_k_2", kkp[:], r_in)
                bcast("rwkv_k_a_2", kap[:], r_in)
                act.dma_start(rkp[:], I["rwkv_r_k_2"].rearrange("o h n -> o (h n)").broadcast_to([P, H1])).then_inc(r_in, 16)
                act.wait_ge(r_dve, RDVE["kks", m])
                RACT.mark(r_act, nc.scalar.activation(rsm[:, 1], rsm[:, 0], ACT.Sqrt), "sqrt", m)
                act.wait_ge(r_dve, RDVE["linw", m, 1])
                RACT.mark(r_act, nc.scalar.activation(sg[:], sg[:], ACT.Sigmoid), "sigw", m)
                act.wait_ge(r_dve, RDVE["lina", m, 1])
                RACT.mark(r_act, nc.scalar.activation(sa[:], sa[:], ACT.Sigmoid), "siga", m)
                act.wait_ge(r_pe, RPE["cum", m])
                for name, dst, bank, sc in (("E0", E0, 0, 1.0), ("E1", E1, 2, 1.0), ("E2", E2, 2, -1.0), ("E3", E3, 4, 1.0)):
                    nc.scalar.activation(dst[:, 0:NW], B[bank], ACT.Exp, scale=sc)
                    RACT.mark(r_act, nc.scalar.activation(dst[:, NW:], B[bank + 1], ACT.Exp, scale=sc), name, m)
                RACT.mark(r_act, nc.scalar.activation(lamT[:].rearrange("p a c -> p (a c)"), B[6][:, 0:2 * R_PAIRS], ACT.Exp), "lam", m)
                for i in range(8):
                    dst = (kkrT if i < 4 else bkT)[:, 4 * (i % 2):4 * (i % 2) + 4, (i // 2) % 2]
                    act.wait_ge(r_pe, RPE["T", m, i])
                    RACT.mark(r_act, nc.scalar.copy(dst, B[i].rearrange("p (a t) -> p a t", a=4)), "T", m, i)
                for g in range(2):
                    half = slice(g * NW, (g + 1) * NW)
                    act.wait_ge(r_pe, RPE["AV", m, g])
                    RACT.mark(r_act, nc.scalar.copy(AV[:].rearrange("p a s -> p (a s)"), B[6]), "AV", m, g)
                    act.wait_ge(r_pe, RPE["U", m, g])
                    RACT.mark(r_act, nc.scalar.mul(nU[:, half], B[7], -1.0), "U", m, g)
                    act.wait_ge(r_pe, RPE["W", m, g])
                    RACT.mark(r_act, nc.scalar.mul(nW[:, half], B[6], -1.0), "W", m, g)
                    act.wait_ge(r_pe, RPE["Y", m, g])
                    RACT.mark(r_act, nc.scalar.copy(yy[:, m, half], B[1]), "Y", m, g)
                act.wait_ge(r_pe, RPE["O", m, 1])
                bcast("rwkv_ln_w_2", lnw[:], r_in2)
                bcast("rwkv_ln_b_2", lnb[:], r_in2)
                act.wait_ge(r_dve, RDVE["vs", m])
                RACT.mark(r_act, nc.scalar.activation(rsm[:, 5], rsm[:, 4], ACT.Sqrt, bias=gn_eps, scale=1.0 / R_HD), "sd", m)
                RACT.mark(r_act, nc.scalar.activation(zs[:], zb[:, m], ACT.Sigmoid), "sz", m)
            high_half(8)

            for par in range(2):
                act.wait_ge(gate_out[par], 64)
            act.wait_ge(r_dve, RDVE["ob", 1])
            t0 = t.fill

            def load_gates(c):
                if c >= 2:
                    act.wait_ge(mix_done, 2 * (c - 1))
                for g in range(2):
                    act.dma_start(gg[:, c % 2, g], gates[g][:, :, c * NW:(c + 1) * NW]).then_inc(gates_in[c % 2], 16)

            load_gates(0)
            g0 = t.group

            def mixed_high(c):
                for g in range(2):
                    high(g0 + 2 * c + g, None, g, hH[:, 4 * c + 2 * g:4 * c + 2 * g + 2])

            steps(4, lambda c: load_gates(c + 1) if c < 3 else None, turned=mixed_high)
            t.fill += 8
            c0 = t.chunk
            split(c0, 1)
            mixed_high(3)
            for c in range(1, 4):
                split(c0 + c, 0)
                split(c0 + c, 1)
            t.fill += 4
            act.wait_ge(acc_free, 4 + 2 * t.fill)
            norm()

        @block.vector
        def _(dve):
            t = Tally()

            def split(c, half, small=False):
                for j in range(half * HALF, half * HALF + HALF):
                    dve.wait_ge(high_done, c * UNITS + (j + 1))
                    n = LC if small else NW
                    nc.vector.tensor_tensor(wL[:, j % SPLIT, :, 0:n], raw[:, j % RAW, :, 0:n],
                                            wH[:, j % SPLIT, :, 0:n].bitcast(F32), ALU.subtract).then_inc(split_done, 1)

            def steps(n, evac, turned=None, small=None):
                c0 = t.chunk
                for k in range(n):
                    split(c0 + k, 1, k == small)
                    if k == small:
                        t.extra = 16 * UNITS // RAW
                    if turned is not None and k:
                        turned(k - 1)
                    split(c0 + k + 1, 0, k + 1 == small)
                    evac(k)
                t.chunk += n

            def done(c):
                dve.wait_ge(unit_used, c * UNITS + (UNITS + SPLIT))

            def low(nh, bank, dH, dL):
                dve.wait_ge(group_high, nh + 1)
                nc.vector.tensor_tensor(dL, tp[bank][:], dH.bitcast(F32), ALU.subtract).then_inc(group_free, 1)

            def low_wide(dH, dL):
                for g in range(GROUPS):
                    low(t.high + g, g % 2, dH[:, 2 * g:2 * g + 2], dL[:, 2 * g:2 * g + 2])
                t.high += GROUPS
                t.group += GROUPS

            def norm(dst=xn, out_sem=None):
                dve.wait_ge(std_done, t.norm + 1)
                nc.vector.reciprocal(rstd, std).then_inc(rstd_done, 1)
                dve.wait_ge(rstd_done, t.norm + 1)
                dve.wait_ge(gain_in, 16 * (t.norm + 1))
                for m in range(MT):
                    nc.vector.scalar_tensor_tensor(dst[:, m], X[:, m], rstd[:, m:m + 1], gain[:], ALU.mult,
                                                   ALU.mult).then_inc(out_sem or xn_done, 1)
                t.norm += 1

            def add_to_x(c, par, cols):
                done(c)
                for m in range(MT):
                    nc.vector.tensor_tensor(X[:, m, cols], X[:, m, cols], acc[par][m][:], ALU.add).then_inc(acc_free, 1)

            def mlp(after=None):
                norm()
                low_wide(xH, xL)
                c0, f0, h0, q0 = t.chunk, t.fill, t.high, t.square

                def block_of(b, after=None):
                    def turned(c):
                        for g in range(2):
                            k = 4 * c + 2 * g
                            low(b * 8 + (h0 + 2 * c + g), g, hH[:, k:k + 2], hL[:, k:k + 2])
                    for c in range(8):
                        split(b * 8 + (c0 + c), 1)
                        if 1 <= c <= 4:
                            turned(c - 1)
                        split(b * 8 + (c0 + c + 1), 0)
                        if c < 4:
                            for m in range(MT):
                                dve.wait_ge(acc_free, b * 16 + (2 * (f0 + c) + 4 + m + 1))
                                r = stg[:, c % 2, m]
                                nc.vector.tensor_tensor(r, r, r, ALU.mult).then_inc(stg_done, 1)
                        else:
                            add_to_x(b * 8 + (c0 + c), c % 2, slice((c - 4) * NW, (c - 3) * NW))
                        if after:
                            after(c)

                block_of(0, after)
                with dve.Fori(1, FB) as b:
                    block_of(b)
                t.chunk += 8 * FB
                t.fill += 8 * FB
                t.high += 8 * FB
                t.group += 8 * FB
                t.square += 8 * FB

            nc.vector.sem_inc(split_done, RAW)
            nc.vector.sem_inc(acc_free, 4)
            nc.vector.sem_inc(group_free, 2)
            dve.wait_ge(const_b, 4)
            dve.wait_ge(lam_in, 32)
            lv = lamv[:].rearrange("p (a b) d -> p a b d", b=2)
            nc.vector.tensor_tensor(lamp[:], lv[:, :, 0], lv[:, :, 1], ALU.mult).then_inc(lam_step, 1)
            nc.vector.tensor_scalar(subg[:], subg[:], 1.0 - LAMBDA_INIT, None, ALU.mult).then_inc(lam_step, 1)
            dve.wait_ge(lam_step, 2)
            nc.vector.tensor_reduce(lams, lamp[:], AX, ALU.add).then_inc(lam_step, 1)
            nc.vector.memset(ac1, 0.0).then_inc(lam_step, 1)
            split(0, 0)
            norm()
            low_wide(xH, xL)
            dve.wait_ge(lam_exp, 1)
            nc.vector.tensor_tensor(nlam, lame[:, 1:2], lame[:, 0:1], ALU.subtract).then_inc(lam_step, 1)
            dve.wait_ge(lam_step, 5)
            nc.vector.tensor_scalar(nlam, nlam, -LAMBDA_INIT, None, ALU.add).then_inc(lam_step, 1)
            steps(12, lambda c: None)
            t.fill += 12
            t.group += 16 + DA_ITEMS

            def masks(i):
                nk = (i % 2 + 1) * P
                m = ms[:, i % 2, :, 0:nk]
                dve.wait_ge(score_done, i + 1)
                if i >= 2:
                    dve.wait_ge(prob_done, i - 1)
                if nk > P:
                    nc.vector.tensor_copy(ms[:, i % 2, :, 0:P], wk[i % 2][:, :, 0:P]).then_inc(mask_done, 1)
                nc.vector.tensor_tensor(ms[:, i % 2, :, nk - P:nk], wk[i % 2][:, :, nk - P:nk],
                                        dmask[:].unsqueeze(1).broadcast_to([P, 2, P]), ALU.add).then_inc(mask_done, 1)
                dve.wait_ge(mask_done, masked(i))
                nc.vector.tensor_reduce(amx[:, i % 2], m, AX, ALU.max).then_inc(max_done, 1)
                dve.wait_ge(max_done, i + 1)
                nc.vector.tensor_scalar(anm[:, i % 2], amx[:, i % 2], -DA_HD ** -0.5, None, ALU.mult).then_inc(nmax_done, 1)

            def probs(i):
                nk = (i % 2 + 1) * P
                e = ms[:, i % 2]
                n = 3 * i
                dve.wait_ge(exp_done, 2 * i + 2)
                nc.vector.reciprocal(ars[:, i % 2], asum[:, i % 2]).then_inc(coef_step, 1)
                dve.wait_ge(coef_step, n + 1)
                nc.vector.tensor_tensor(ac1[:, i % 2:i % 2 + 1], ars[:, i % 2, 1:2], nlam, ALU.mult).then_inc(coef_step, 1)
                dve.wait_ge(coef_step, n + 2)
                nc.vector.tensor_scalar(e[:, 1, 0:nk], e[:, 1, 0:nk], ac1[:, i % 2:i % 2 + 1], None, ALU.mult).then_inc(coef_step, 1)
                dve.wait_ge(coef_step, n + 3)
                if i >= 2:
                    dve.wait_ge(pv_done, i - 1)
                nc.vector.scalar_tensor_tensor(pd[:, i % 2, 0:nk], e[:, 0, 0:nk], ars[:, i % 2, 0:1], e[:, 1, 0:nk],
                                               ALU.mult, ALU.add).then_inc(prob_done, 1)

            for i in range(DA_ITEMS + 1):
                if i < DA_ITEMS:
                    masks(i)
                if i:
                    probs(i - 1)
            dve.wait_ge(lam_exp, DA_ITEMS + 2)
            nc.vector.reciprocal(orstd, ostd).then_inc(lam_step, 1)
            dve.wait_ge(lam_step, 7)
            for i in range(DA_ITEMS):
                h, qt = i // 2, i % 2
                o = oa[:, qt, h * DA_VD:(h + 1) * DA_VD]
                nc.vector.scalar_tensor_tensor(o, o, orstd[:, i:i + 1], subg[:], ALU.mult, ALU.mult).then_inc(o_norm, 1)
            low_wide(xH, xL)
            c0 = t.chunk
            steps(4, lambda c: add_to_x(c0 + c, c % 2, slice(c * NW, (c + 1) * NW)))
            t.fill += 4

            n = [0]

            def link(ins):
                n[0] += 1
                ins.then_inc(s5_step, 1)
                dve.wait_ge(s5_step, n[0])

            are, aim, dt = sv[:, 0], sv[:, 1], sv[:, 2, 1:2]

            def angles():
                dve.wait_ge(s5_act, 1)
                link(nc.vector.tensor_scalar(sv[:, 3], are, dt, None, ALU.mult))
                link(nc.vector.tensor_scalar(sv[:, 4], aim, dt, None, ALU.mult))
                link(nc.vector.tensor_scalar(sv[:, 7], sv[:, 4], 1 / (2 * math.pi), ROUND, ALU.mult, ALU.add))
                link(nc.vector.tensor_scalar(sv[:, 9], sv[:, 7], -ROUND, None, ALU.add))
                link(nc.vector.scalar_tensor_tensor(sv[:, 4], sv[:, 9], -TWO_PI_A, sv[:, 4], ALU.mult, ALU.add))
                link(nc.vector.scalar_tensor_tensor(sv[:, 4], sv[:, 9], -TWO_PI_B, sv[:, 4], ALU.mult, ALU.add))
                link(nc.vector.scalar_tensor_tensor(sv[:, 4], sv[:, 9], -TWO_PI_C, sv[:, 4], ALU.mult, ALU.add))
                link(nc.vector.tensor_scalar(sv[:, 7], sv[:, 4], PI_BELOW, -PI_BELOW, ALU.min, ALU.max))

            def factors():
                dve.wait_ge(s5_act, 4)
                sn, cs, mag = sv[:, 6], sv[:, 10], sv[:, 5]
                link(nc.vector.tensor_tensor(sv[:, 9], sv[:, 8], sv[:, 8], ALU.mult))
                link(nc.vector.tensor_scalar(cs, sv[:, 9], -2.0, 1.0, ALU.mult, ALU.add))
                link(nc.vector.tensor_tensor(sv[:, 11], mag, cs, ALU.mult))
                link(nc.vector.tensor_scalar(sv[:, 11], sv[:, 11], -1.0, None, ALU.add))
                link(nc.vector.tensor_tensor(sv[:, 12], mag, sn, ALU.mult))
                link(nc.vector.tensor_tensor(sv[:, 13], are, are, ALU.mult))
                link(nc.vector.tensor_tensor(sv[:, 14], aim, aim, ALU.mult))
                link(nc.vector.tensor_tensor(sv[:, 13], sv[:, 13], sv[:, 14], ALU.add))
                link(nc.vector.reciprocal(sv[:, 14], sv[:, 13]))
                for o, op, p0, q0 in ((15, ALU.add, (11, 0), (12, 1)), (16, ALU.subtract, (12, 0), (11, 1))):
                    link(nc.vector.tensor_tensor(sv[:, 17], sv[:, p0[0]], sv[:, p0[1]], ALU.mult))
                    link(nc.vector.tensor_tensor(sv[:, 18], sv[:, q0[0]], sv[:, q0[1]], ALU.mult))
                    link(nc.vector.tensor_tensor(sv[:, o], sv[:, 17], sv[:, 18], op))
                    link(nc.vector.tensor_tensor(sv[:, o], sv[:, o], sv[:, 14], ALU.mult))
                link(nc.vector.tensor_tensor(sv[:, 17], cs, cs, ALU.mult))
                link(nc.vector.tensor_tensor(sv[:, 18], sn, sn, ALU.mult))
                link(nc.vector.tensor_tensor(sv[:, 17], sv[:, 17], sv[:, 18], ALU.add))
                link(nc.vector.tensor_scalar(sv[:, 17], sv[:, 17], -0.5, 1.5, ALU.mult, ALU.add))
                for twice in range(2):
                    link(nc.vector.tensor_copy(pks[:, 0, twice], mag))
                    link(nc.vector.tensor_tensor(pks[:, 1, twice], cs, sv[:, 17], ALU.mult))
                    link(nc.vector.tensor_tensor(pks[:, 2, twice], sn, sv[:, 17], ALU.mult))
                assert n[0] == S5_PHASES

            def input_matrices(c):
                wide = [P, S5_P, S5_C]
                cr, ci = sv[:, 15].unsqueeze(2).broadcast_to(wide), sv[:, 16].unsqueeze(2).broadcast_to(wide)
                o = sb_bb[:, :, c].rearrange("p c s -> p s c")
                link(nc.vector.tensor_tensor(o, cr, sb_b[:, c], ALU.mult))
                link(nc.vector.tensor_tensor(sb_t[:], ci, sb_b[:, 1 - c], ALU.mult))
                link(nc.vector.tensor_tensor(o, o, sb_t[:], ALU.add if c else ALU.subtract))

            def phases():
                dve.wait_ge(s5_turn, 1)
                for g in range(2):
                    half = slice(64 * g, 64 * g + 64)
                    src = wk[0][half].rearrange("p a s -> p (a s)")[:, 0:3 * P].rearrange("p (v s g) -> p v s g", v=3, g=2)
                    nc.vector.tensor_copy(srs[half], src[:, :, :, g]).then_inc(s5_back, 1)

            def output_matrices(b):
                dve.wait_ge(s5_pool, 1)
                dve.wait_ge(s5_turn, b + 2)
                for g in range(2):
                    half = slice(64 * g, 64 * g + 64)
                    src = wk[b % 2][half].rearrange("p a s -> p (a s)").rearrange("p (s g c) -> p s g c", g=2, c=S5_C)
                    s0 = (b % 4) * 16
                    nc.vector.tensor_scalar(cpad[half, s0:s0 + 16, b // 4, g], src[:, :, g], -1.0 if b >= 4 else 1.0,
                                            None, ALU.mult).then_inc(s5_back, 1)

            def s5_vectors(c):
                if c == 0:
                    angles()
                if c == 1:
                    factors()
                if c == 2:
                    input_matrices(0)
                if c == 3:
                    input_matrices(1)
                    phases()
                if c >= 4:
                    for b in range(2 * (c - 4), 2 * (c - 4) + 2):
                        output_matrices(b)

            mlp(after=s5_vectors)
            norm()
            dve.wait_ge(xn_done, 2 * t.norm)
            dve.wait_ge(group_done, t.group + GROUPS)
            t.group += GROUPS
            nc.vector.sem_inc(rot_done, 4)

            def recurrence(s, one, q):
                b = q % 2
                tables = tab[:, q // TG, q % TG]
                dve.wait_ge(bu_done, s + 3)
                for c in range(2):
                    nc.vector.tensor_tensor(rot[:, c], wk[b][:], tables[:, c:c + 1].broadcast_to([P, 2, S]),
                                            ALU.mult).then_inc(rot_done, 1)
                dve.wait_ge(rot_done, s * 2 + 6)
                nc.vector.tensor_tensor(vv[:, 0], rot[:, 0, 0], rot[:, 1, 1], ALU.add).then_inc(v_done, 1)
                nc.vector.tensor_tensor(vv[:, 1], rot[:, 0, 1], rot[:, 1, 0], ALU.subtract).then_inc(v_done, 1)
                dve.wait_ge(zc_done, s + 1)
                for c in range(2):
                    dve.wait_ge(v_done, s * 2 + (c + 1))
                    nc.vector.tensor_tensor_scan(zz[:, b, c], srs[:, 0, one].broadcast_to([P, S]), vv[:, c],
                                                 0.0, ALU.mult, ALU.add).then_inc(scan_done, 1)
                dve.wait_ge(scan_done, s * 2 + 2)
                dve.wait_ge(y_done, s + 1)
                nc.vector.tensor_tensor(zs5[:, b], zz[:, b], tables[:, 1:2].broadcast_to([P, 2, S]), ALU.mult).then_inc(zs_done, 1)

            def add_outputs(r):
                dve.wait_ge(y_done, 16 * (r + 1) + 2)
                for m in range(MT):
                    y = xn[:, m, r * NW:(r + 1) * NW]
                    nc.vector.tensor_tensor(y, y, acc[r % 2][m][:], ALU.add).then_inc(acc_free, 1)

            for r in range(4):
                with dve.Fori(0, 2) as i:
                    for q in range(2 * TG):
                        if q % TG == 0:
                            dve.wait_ge(tab_in[q // TG], i * 16 + (32 * r + 16))
                        s = i * (2 * TG) + (16 * r + q)
                        recurrence(s, bass.ds(s, 1), q)
                if r == 0:
                    dve.wait_ge(skip_in, 16)
                    for m in range(MT):
                        nc.vector.tensor_tensor(xn[:, m], xn[:, m], skip[:], ALU.mult).then_inc(skip_done, 1)
                    dve.wait_ge(skip_done, 2)
                else:
                    add_outputs(r - 1)
            add_outputs(3)
            t.fill += 4
            low_wide(xH, xL)
            c0, f0 = t.chunk, t.fill

            def glu(c):
                if not c % 2:
                    return
                done(c0 + c)
                for m in range(MT):
                    g = stg[:, (c // 2) % 2, m]
                    cols = slice((c // 2) * NW, (c // 2 + 1) * NW)
                    dve.wait_ge(acc_free, 2 * (f0 + c - 1) + 6 + m)
                    nc.vector.tensor_tensor(g, g, acc[1][m][:], ALU.mult).then_inc(acc_free, 1)
                    dve.wait_ge(acc_free, 2 * (f0 + c) + 4 + m + 1)
                    nc.vector.tensor_tensor(X[:, m, cols], X[:, m, cols], g, ALU.add).then_inc(glu_added, 1)

            steps(8, glu)
            t.fill += 8
            mlp()
            dve.wait_ge(mask_step, MASK_STEPS)
            norm(X)
            norm()
            low_wide(xH, xL)
            c0, f0 = t.chunk, t.fill
            dve.wait_ge(f_in, 48)

            def second_turned(c):
                if not 8 <= c < 16:
                    return
                n = c - 8
                dst = (rr, kr, vr, zb)[n // 2]
                dve.wait_ge(shift_done, n + 1)
                if n:
                    dve.wait_ge(shift_out, 2 * n)
                for m in range(MT):
                    nc.vector.tensor_tensor(shtmp[:, m], wk[m][:].rearrange("p a s -> p (a s)"), mixmu[:, n * NW:(n + 1) * NW],
                                            ALU.mult).then_inc(shift_mul, 1)
                for m in range(MT):
                    dve.wait_ge(shift_mul, 2 * n + m + 1)
                    nc.vector.tensor_tensor(dst[:, m, (n % 2) * NW:(n % 2 + 1) * NW], shtmp[:, m], stg[:, c % 2, m],
                                            ALU.add).then_inc(shift_out, 1)

            steps(25, lambda c: None, turned=second_turned, small=24)
            t.fill += 24
            t.group += 8

            for m in range(MT):
                dve.wait_ge(f_act, FACT["lo", m])
                FDVE.mark(f_dve, nc.vector.tensor_tensor(lf[:, 0, m], lo[:, m, 0:F_HEADS], fbias[:], ALU.add), "bias", m)
            dve.wait_ge(f_pe, FPE["shift", 0])
            for m in range(MT):
                bank = wk[m][:].rearrange("p a s -> p (a s)")[:, 0:2 * LORA]
                FDVE.mark(f_dve, nc.vector.tensor_tensor(ltmp[:, m], bank, lmu[:], ALU.mult), "lmul", m)
                dve.wait_ge(f_dve, FDVE["lmul", m])
                u = lo[:, m, F_HEADS:]
                FDVE.mark(f_dve, nc.vector.tensor_tensor(u, ltmp[:, m], u, ALU.add), "ladd", m)
            FDVE.mark(f_dve, nc.vector.scalar_tensor_tensor(lf[:, 1], lf[:, 0], -1.0, lf[:, 0], ALU.mult, ALU.max), "abs")
            FDVE.mark(f_dve, nc.vector.tensor_scalar(lf[:, 2], lf[:, 0], 0.0, None, ALU.min), "min")
            dve.wait_ge(f_act, FACT["fl",])
            dve.wait_ge(f_dve, FDVE["min",])
            FDVE.mark(f_dve, nc.vector.tensor_tensor(lf[:, 2], lf[:, 2], lf[:, 1], ALU.subtract), "lf")

            def fox_mask(i):
                nk = (i % 2 + 1) * P
                dve.wait_ge(f_pe, FPE["fs", i])
                if i >= 2:
                    dve.wait_ge(f_dve, FDVE["fp", i - 2])
                if nk > P:
                    FDVE.mark(f_dve, nc.vector.tensor_copy(fms[:, i % 2, 0:P], wk[i % 2][:, 0, 0:P]), "fc", i)
                FDVE.mark(f_dve, nc.vector.tensor_tensor(fms[:, i % 2, nk - P:nk], wk[i % 2][:, 0, nk - P:nk], cmask[:], ALU.add), "fm", i)
                dve.wait_ge(f_dve, FDVE["fm", i])
                FDVE.mark(f_dve, nc.vector.tensor_reduce(fstat[:, i % 2:i % 2 + 1], fms[:, i % 2, 0:nk], AX, ALU.max), "fx", i)
                dve.wait_ge(f_dve, FDVE["fx", i])
                FDVE.mark(f_dve, nc.vector.tensor_scalar(fstat[:, 2 + i % 2:3 + i % 2], fstat[:, i % 2:i % 2 + 1], -F_SCALE, None,
                                                         ALU.mult), "fn", i)

            def fox_prob(i):
                nk = (i % 2 + 1) * P
                dve.wait_ge(f_act, FACT["fe", i])
                FDVE.mark(f_dve, nc.vector.reciprocal(fstat[:, 6 + i % 2:7 + i % 2], fstat[:, 4 + i % 2:5 + i % 2]), "fr", i)
                dve.wait_ge(f_dve, FDVE["fr", i])
                if i >= 2:
                    dve.wait_ge(f_pe, FPE["ft", i - 2])
                FDVE.mark(f_dve, nc.vector.tensor_scalar(fpd[:, i % 2, 0:nk], fms[:, i % 2, 0:nk], fstat[:, 6 + i % 2:7 + i % 2], None,
                                                         ALU.mult), "fp", i)

            for i in range(F_ITEMS + 1):
                if i < F_ITEMS:
                    fox_mask(i)
                if i:
                    fox_prob(i - 1)
            for m in range(MT):
                sz = fk[:, 4 * m:4 * m + 4].rearrange("p a s -> p (a s)")
                dve.wait_ge(f_act, FACT["sz", m])
                FDVE.mark(f_dve, nc.vector.tensor_tensor(sz, sz, fz[:, m], ALU.mult), "oz", m)
                dve.wait_ge(f_dve, FDVE["oz", m])
                FDVE.mark(f_dve, nc.vector.tensor_tensor(fo[:, m], fo[:, m], sz, ALU.mult), "og", m)

            def low_half(k0):
                for g in range(4):
                    low(t.high + g, g % 2, xH[:, k0 + 2 * g:k0 + 2 * g + 2], xL[:, k0 + 2 * g:k0 + 2 * g + 2])
                t.high += 4
                t.group += 4
            low_half(0)

            B = [acc[0][0], acc[0][1], acc[1][0], acc[1][1], tp[0], tp[1], wk[0], wk[1]]
            B = [b[:] if n < 4 else b[:].rearrange("p a s -> p (a s)") for n, b in enumerate(B)]
            hd = lambda t: t.rearrange("p (h n) -> p h n", n=R_HD)
            wide = lambda t: t.unsqueeze(2).broadcast_to([P, R_HEADS, R_HD])
            over = lambda t, n: t.unsqueeze(1).broadcast_to([P, n, P])
            four = lambda b: b.rearrange("p (a t) -> p a t", a=4)
            TT = nc.vector.tensor_tensor

            def step(ins, *name):
                RDVE.mark(r_dve, ins, *name)

            def own(*name):
                dve.wait_ge(r_dve, RDVE[name])

            nc.vector.memset(ST[:, 0], 0.0).then_inc(shift_mul, 1)
            for m in range(MT):
                dve.wait_ge(r_in, R_LOADS * 16 * (m + 1))
                step(TT(kk[:], kr[:, m], kkp[:], ALU.mult), "kk0", m)
                own("kk0", m)
                step(TT(tmp[:], kk[:], kk[:], ALU.mult), "kk2", m)
                own("kk2", m)
                step(nc.vector.tensor_reduce(rsm[:, 0], hd(tmp[:]), AX, ALU.add), "kks", m)
                dve.wait_ge(r_act, RACT["sqrt", m])
                step(nc.vector.tensor_scalar(rsm[:, 1], rsm[:, 1], L2_EPS, None, ALU.max), "kkm", m)
                own("kkm", m)
                step(nc.vector.reciprocal(rsm[:, 2], rsm[:, 1]), "kkr", m)
                own("kkr", m)
                step(TT(hd(kk[:]), hd(kk[:]), wide(rsm[:, 2]), ALU.mult), "kk", m)
                dve.wait_ge(r_pe, RPE["lin", m])
                for name, dst, par, b0 in (("linw", sg, w0p, 0), ("lina", sa, a0p, 2)):
                    for q in range(2):
                        cols = slice(q * NW, (q + 1) * NW)
                        step(TT(dst[:, cols], B[b0 + q], par[:, cols], ALU.add), name, m, q)
                dve.wait_ge(r_act, RACT["siga", m])
                step(nc.vector.scalar_tensor_tensor(tmp[:], sa[:], -1.0, kap[:], ALU.add, ALU.mult), "ka", m)
                own("ka", m)
                step(nc.vector.scalar_tensor_tensor(kr[:, m], tmp[:], 1.0, kr[:, m], ALU.add, ALU.mult), "k'", m)
                step(TT(bb[:], kk[:], sa[:], ALU.mult), "b", m)
                own("b", m)
                step(TT(tmp[:], rr[:, m], kr[:, m], ALU.mult), "bo0", m)
                own("bo0", m)
                step(TT(tmp[:], tmp[:], rkp[:], ALU.mult), "bo1", m)
                own("bo1", m)
                step(nc.vector.tensor_reduce(rsm[:, 6], hd(tmp[:]), AX, ALU.add), "bon", m)
                dve.wait_ge(r_act, RACT["E3", m])
                step(TT(kkh[:], kk[:], E0[:], ALU.mult), "kkh", m)
                step(TT(rr[:, m], rr[:, m], E1[:], ALU.mult), "rh", m)
                own("kkh", m)
                step(TT(kk[:], bb[:], E2[:], ALU.mult), "bh", m)
                step(TT(sg[:], kr[:, m], E2[:], ALU.mult), "kh", m)
                step(TT(bt[:], bb[:], E3[:], ALU.mult), "bt", m)
                own("kh", m)
                step(TT(kr[:, m], kr[:, m], E3[:], ALU.mult), "kt", m)
                own("kt", m)
                for g in range(2):
                    dve.wait_ge(r_pe, RPE["T", m, 7])
                    for h in range(8):
                        dve.wait_ge(r_pe, RPE["A", m, g, h])
                        step(TT(A4[:, h].rearrange("p (v e) t -> p v e t", v=2), B[h].rearrange("p (v e t) -> p v e t", v=2, e=2),
                                mask2[:].unsqueeze(1).broadcast_to([P, 2, 2, P]), ALU.mult), "A", m, g, h)
                    dve.wait_ge(r_pe, RPE["L", m, g])
                    X4 = XA[:].rearrange("p (a e) s -> p a e s", e=2)
                    for e in range(2):
                        step(TT(X4[:, :, e], four(B[e]), over(level[:, 0], 4), ALU.mult), "x0", m, g, e)
                    own("A", m, g, 7)
                    step(TT(XT[:], A4[:, :, 0], over(level[:, 1], 8), ALU.mult), "xt0", m, g)
                    own("xt0", m, g)
                    step(TT(XA[:], XA[:], over(ident[:], 8), ALU.add), "X", m, g, 0)
                    step(TT(XT[:], XT[:], over(ident[:], 8), ALU.add), "XT", m, g, 0)
                    for lv in range(1, LEVELS + 1):
                        for k in range(2):
                            h4 = slice(4 * k, 4 * k + 4)
                            dve.wait_ge(r_pe, RPE["Q", m, g, lv, k])
                            step(TT(QQ[:, h4], four(B[k]), over(level[:, lv + 1], 4), ALU.mult), "Q", m, g, lv, k)
                        for k in range(2):
                            h4 = slice(4 * k, 4 * k + 4)
                            dve.wait_ge(r_pe, RPE["XQ", m, g, lv, k])
                            if lv < LEVELS:
                                step(TT(XA[:, h4], XA[:, h4], four(B[2 + k]), ALU.subtract), "X", m, g, lv, k)
                            step(TT(XT[:, h4], XT[:, h4], four(B[4 + k]), ALU.subtract), "XT", m, g, lv, k)
                    dve.wait_ge(r_pe, RPE["R", m, g])
                    dst = kkrT[:, 4 * g:4 * g + 4, 1]
                    step(TT(dst, dst, four(B[0]), ALU.add), "R", m, g)
                for name, dst, b0 in (("M", MM, 0), ("N", NN, 2)):
                    for c in range(2):
                        dve.wait_ge(r_pe, RPE[name, m, c])
                        for q in range(2):
                            step(TT(dst[:, c, 4 * q:4 * q + 4], four(B[4 * c + b0 + q]), over(same[:], 4), ALU.mult), name, m, c, q)
                for c in range(2):
                    new = ST[:, 1 - c]
                    if c:
                        own("S", m, 0)
                    if c or m:
                        dve.wait_ge(r_pe, RPE["O", m, 0] if c else RPE["O", m - 1, 1])
                    else:
                        dve.wait_ge(shift_mul, 17)
                    step(TT(new, ST[:, c], lamT[:, :, c:c + 1].broadcast_to([P, R_PAIRS, P]), ALU.mult), "sl", m, c)
                    dve.wait_ge(r_pe, RPE["S", m, c])
                    own("sl", m, c)
                    for q in range(2):
                        part = ST[:, 1 - c, 4 * q:4 * q + 4]
                        step(TT(part, part, four(B[q]), ALU.add), "sb", m, c, q)
                    own("sb", m, c, 1)
                    step(TT(new, new, NN[:, c], ALU.add), "S", m, c)
                dve.wait_ge(r_pe, RPE["O", m, 1])
                dve.wait_ge(r_act, RACT["Y", m, 1])
                for q in range(2):
                    cols = slice(q * NW, (q + 1) * NW)
                    step(TT(yy[:, m, cols], yy[:, m, cols], B[2 + q], ALU.add), "O", m, q)
                y = yy[:, m]
                own("O", m, 1)
                step(nc.vector.tensor_reduce(rsm[:, 3], hd(y), AX, ALU.add), "mu", m)
                own("mu", m)
                step(nc.vector.tensor_scalar(rsm[:, 3], rsm[:, 3], -1.0 / R_HD, None, ALU.mult), "nm", m)
                own("nm", m)
                step(TT(hd(y), hd(y), wide(rsm[:, 3]), ALU.add), "yc", m)
                own("yc", m)
                step(TT(y2[:], y, y, ALU.mult), "y2", m)
                own("y2", m)
                step(nc.vector.tensor_reduce(rsm[:, 4], hd(y2[:]), AX, ALU.add), "vs", m)
                dve.wait_ge(r_act, RACT["sd", m])
                step(nc.vector.reciprocal(rsm[:, 7], rsm[:, 5]), "sr", m)
                own("sr", m)
                step(TT(hd(y), hd(y), wide(rsm[:, 7]), ALU.mult), "yn", m)
                dve.wait_ge(r_in2, 32 * (m + 1))
                own("yn", m)
                step(TT(y, y, lnw[:], ALU.mult), "yw", m)
                own("yw", m)
                step(TT(y, y, lnb[:], ALU.add), "yb", m)
                step(TT(hd(y2[:]), hd(vr[:, m]), wide(rsm[:, 6]), ALU.mult), "bv", m)
                own("bv", m)
                step(TT(y, y, y2[:], ALU.add), "yv", m)
                dve.wait_ge(r_act, RACT["sz", m])
                step(TT(zb[:, m], zb[:, m], zs[:], ALU.mult), "zz", m)
                own("zz", m)
                step(TT(zb[:, m], zb[:, m], y, ALU.mult), "ob", m)
            low_half(8)

            c0, f0, h0 = t.chunk, t.fill, t.high

            def mixed_low(c):
                for g in range(2):
                    k = 4 * c + 2 * g
                    low(h0 + 2 * c + g, g, hH[:, k:k + 2], hL[:, k:k + 2])

            def mixed(c):
                done(c0 + c)
                dve.wait_ge(gates_in[c % 2], 32 * (c // 2 + 1))
                if c >= 2:
                    dve.wait_ge(group_done, t.group + 2 * (c - 1))
                for g in range(2):
                    for m in range(MT):
                        v = gg[:, c % 2, g, m]
                        TT(v, v, acc[g][m][:], ALU.mult).then_inc(acc_free, 1)
                dve.wait_ge(acc_free, 2 * (f0 + 2 * c) + 8)
                for m in range(MT):
                    TT(stg[:, c % 2, m], gg[:, c % 2, 0, m], gg[:, c % 2, 1, m], ALU.add).then_inc(mix_done, 1)

            steps(4, mixed, turned=mixed_low)
            t.fill += 8
            t.high += 8
            t.group += 8
            c0 = t.chunk
            split(c0, 1)
            mixed_low(3)
            for c in range(4):
                if c < 3:
                    split(c0 + c + 1, 0)
                add_to_x(c0 + c, c % 2, slice(c * NW, (c + 1) * NW))
                if c < 3:
                    split(c0 + c + 1, 1)
            norm(out_sem=fin_done)


_INS = ['x', 'norm_mix', 'norm_mlp', 'norm_final', 'a_w_in', 'a_lambda', 'a_subln', 'a_w_out',
        'b_a_re', 'b_a_im', 'b_log_dt', 'b_b_re', 'b_b_im', 'b_c_re', 'b_c_im', 'b_d', 'b_w_glu',
        'mlp_w1', 'mlp_w2', 'norm_gain_2', 'w_in_2', 'fox_forget_bias_2', 'rwkv_shift_mix_2',
        'rwkv_w0_2', 'rwkv_w2_2', 'rwkv_a0_2', 'rwkv_a2_2', 'rwkv_k_k_2', 'rwkv_k_a_2',
        'rwkv_r_k_2', 'rwkv_ln_w_2', 'rwkv_ln_b_2', 'w_proj_fox_2', 'w_proj_rwkv_2', 'w_out_2',
        'final_norm_gain_2']


def kernel(**inputs):
    import numpy as _np
    import concourse.bacc as _bacc
    from concourse import mybir as _mybir
    from concourse.bass_utils import run_bass_kernel_spmd as _run

    nc = _bacc.Bacc("TRN2", target_bir_lowering=False, num_devices=1)
    arrays, args = {}, {}
    for name in _INS:
        a = _np.ascontiguousarray(inputs[name])
        arrays[f"in_{name}_dram"] = a
        args[name] = nc.dram_tensor(f"in_{name}_dram", a.shape, _mybir.dt.from_np(a.dtype), kind="ExternalInput").ap()
    out = nc.dram_tensor("out_0_dram", (1, S, D), F32, kind="ExternalOutput").ap()
    build(nc, args, out)
    r = _run(nc, [arrays], core_ids=[0])
    return r.results[0]["out_0_dram"]
```

```python
import math
from contextlib import ExitStack

import concourse.bass as bass
from concourse import mybir

F32 = mybir.dt.float32
F32R = mybir.dt.float32r
ALU = mybir.AluOpType
ACT = mybir.ActivationFunctionType
AX = mybir.AxisListType.X

P = 128
S = 256
MT = S // P
D = 2048
KT = D // P
NW = 512
UK = 2
UNITS = KT // UK
HALF = UNITS // 2
SLOTS = (3, 6, 8)
DA_SLOTS = (2, 4, 6, 8)
DA_FIRST = 2
RAW = 4
SPLIT = 4
QT = D // NW
GROUPS = KT // 2
FB = 4
EPS = 1e-6
NEG = -1.0e30

DA_HEADS = 8
DA_HD = 128
DA_VD = 256
DA_ITEMS = DA_HEADS * MT
LAMBDA_INIT = 0.8 - 0.6 * math.exp(-0.3 * 0)

H1 = D // 2
F_HD = 128
F_HEADS = H1 // F_HD
F_ITEMS = F_HEADS * MT
F_SCALE = F_HD ** -0.5
R_HD = 64
R_HEADS = H1 // R_HD
R_PAIRS = R_HEADS // 2
LORA = 96
LC = F_HEADS + 2 * LORA
GN_EPS = 64e-5
L2_EPS = 1e-12
NEG_DECAY = -math.exp(-0.5)
TC = 64
LEVELS = 5

S5_C = 16
S5_P = 64
S5_GROUPS = D // S5_C
S5_PAIRS = S5_GROUPS // 2
TWO_PI_A = 6.28125
TWO_PI_B = 8117.0 / 2 ** 22
TWO_PI_C = 2 * math.pi - TWO_PI_A - TWO_PI_B
ROUND = 1.5 * 2 ** 23
PI_BELOW = 3.1415925
S5_STEPS = 41
S5_PHASES = 35
TG = 4
S5_START = 4 + 2 * (12 + 4 + 8 * FB)
MASK_STEPS = 63


def masked(i):
    return 3 * (i // 2) + (3 if i % 2 else 1)


class Steps:

    def __init__(self, names):
        self.value = {name: i + 1 for i, name in enumerate(names)}
        assert len(self.value) == len(names)
        self.passed = 0

    def __getitem__(self, name):
        return self.value[name]

    def mark(self, sem, ins, *name):
        self.passed += 1
        assert self.value[name] == self.passed, (name, self.passed, self.value[name])
        ins.then_inc(sem, 1)


def fox_steps():
    pe = [("shift", 0), ("lT",), ("cum",)]
    act = [("lo", 0), ("lo", 1), ("tanh",), ("fe",), ("fl",), ("lT",), ("nc",)]
    dve = [("bias", 0), ("bias", 1), ("lmul", 0), ("ladd", 0), ("lmul", 1), ("ladd", 1), ("abs",), ("min",), ("lf",)]
    for n in range(F_ITEMS + 3):
        sums, turns, probs, scores = n >= 3, 2 <= n <= F_ITEMS + 1, 1 <= n <= F_ITEMS, n < F_ITEMS
        pe += [("fv", n - 3)] * sums + [("ft", n - 2)] * turns + [("fs", n)] * scores
        act += [("fv", n - 3)] * sums + [("ft", n - 2)] * turns + [("fe", n)] * scores
        dve += [("fr", n - 1), ("fp", n - 1)] * probs
        dve += ([("fc", n)] * (n % 2) + [("fm", n), ("fx", n), ("fn", n)]) * scores
    act += [("sz", 0), ("sz", 1)]
    for m in range(MT):
        dve += [("oz", m), ("og", m)]
    return pe, act, dve


def rwkv_steps():
    pe, act, dve = [], [], []

    def end(m):
        nonlocal act, dve
        dve += [("mu", m), ("nm", m), ("yc", m), ("y2", m), ("vs", m)]
        act += [("sd", m), ("sz", m)]
        dve += [("sr", m), ("yn", m), ("yw", m), ("yb", m), ("bv", m), ("yv", m), ("zz", m), ("ob", m)]

    for m in range(MT):
        pe += [("lin", m), ("cum", m)]
        act += [("sqrt", m), ("sigw", m), ("siga", m)]
        dve += [("kk0", m), ("kk2", m), ("kks", m), ("kkm", m), ("kkr", m), ("kk", m)]
        dve += [("linw", m, q) for q in range(2)] + [("lina", m, q) for q in range(2)]
        if m:
            end(m - 1)
        act += [("E0", m), ("E1", m), ("E2", m), ("E3", m), ("lam", m)]
        dve += [("ka", m), ("k'", m), ("b", m), ("bo0", m), ("bo1", m), ("bon", m)]
        dve += [("kkh", m), ("rh", m), ("bh", m), ("kh", m), ("bt", m), ("kt", m)]
        pe += [("T", m, i) for i in range(8)]
        act += [("T", m, i) for i in range(8)]
        for g in range(2):
            pe += [("A", m, g, h) for h in range(8)]
            dve += [("A", m, g, h) for h in range(8)]
            pe += [("L", m, g), ("AV", m, g)]
            act += [("AV", m, g)]
            dve += [("x0", m, g, e) for e in range(2)] + [("xt0", m, g), ("X", m, g, 0), ("XT", m, g, 0)]
            for lv in range(1, LEVELS + 1):
                pe += [("Q", m, g, lv, k) for k in range(2)] + [("XQ", m, g, lv, k) for k in range(2)]
                dve += [("Q", m, g, lv, k) for k in range(2)]
                for k in range(2):
                    dve += ([("X", m, g, lv, k)] if lv < LEVELS else []) + [("XT", m, g, lv, k)]
            pe += [("U", m, g), ("W", m, g), ("R", m, g), ("Y", m, g)]
            act += [("U", m, g), ("W", m, g), ("Y", m, g)]
            dve += [("R", m, g)]
        pe += [("M", m, c) for c in range(2)] + [("N", m, c) for c in range(2)]
        dve += [("M", m, c, q) for c in range(2) for q in range(2)] + [("N", m, c, q) for c in range(2) for q in range(2)]
        for c in range(2):
            pe += [("S", m, c), ("O", m, c)]
            dve += [("sl", m, c)] + [("sb", m, c, q) for q in range(2)] + [("S", m, c)]
        dve += [("O", m, q) for q in range(2)]
    end(MT - 1)
    return pe, act, dve


class Tally:

    def __init__(self):
        self.chunk = 0
        self.extra = 0
        self.fill = 0
        self.group = 0
        self.high = 0
        self.norm = 0
        self.square = 0
        self.x_ready = 0


def build(nc, I, out):
    with ExitStack() as ctx:
        def sb(name, shape, dt=F32):
            return ctx.enter_context(nc.sbuf_tensor(name, shape, dt))

        def sem(name):
            return ctx.enter_context(nc.semaphore(name))

        regions = {}

        def area(name, kib):
            base = (nc.sbuf_base + 31) // 32 * 32
            sb(name, [P, kib * 256])
            regions[name] = (base, kib * 1024)

        def at(region, offset_kib, name, shape, dt=F32):
            base, size = regions[region]
            nbytes = 4 * math.prod(shape[1:])
            assert offset_kib * 1024 + nbytes <= size, (name, offset_kib, nbytes, size)
            return nc.alloc_sbuf_tensor_at(name, shape, dt, offset=base + int(offset_kib * 1024))

        X = sb("X", [P, MT, D])
        raw = sb("raw", [P, RAW, UK, NW])
        wH = sb("wH", [P, SPLIT, UK, NW], F32R)
        wL = sb("wL", [P, SPLIT, UK, NW], F32R)
        area("stg", 8)
        area("low", 2)
        area("gain", 8)
        stg = at("stg", 0, "stgs", [P, 2, MT, NW])
        gain = at("gain", 0, "gains", [P, D])
        area("xt", 32)
        area("hid", 32)
        area("mix", 48)
        xH = at("xt", 0, "xH", [P, KT, S], F32R)
        xL = at("xt", 16, "xL", [P, KT, S], F32R)
        hH = at("hid", 0, "hH", [P, KT, S], F32R)
        hL = at("hid", 16, "hL", [P, KT, S], F32R)
        xn = at("mix", 0, "xn", [P, MT, D])
        qT = at("hid", 0, "qT", [P, KT, S])
        kT = at("hid", 16, "kT", [P, KT, S])
        va = at("mix", 0, "va", [P, MT, D])
        oa = at("mix", 16, "oa", [P, MT, D])
        ms = at("mix", 32, "ms", [P, 2, 2, S])
        pd = at("mix", 36, "pd", [P, 2, S])
        pT = at("mix", 38, "pT", [P, 2, MT, P])
        osq = at("mix", 40, "osq", [P, DA_VD])
        subg = at("mix", 41, "subg", [P, DA_VD])
        lamv = at("mix", 42, "lamv", [P, 4, DA_HD])
        lamp = at("mix", 44, "lamp", [P, 2, DA_HD])
        sb_b = at("mix", 0, "sb_b", [P, 2, S5_P, S5_C])
        sb_bb = at("mix", 8, "sb_bb", [P, S5_C, 2, S5_P])
        sb_c = at("mix", 16, "sb_c", [P, 2, KT, 2, S5_P])
        sb_t = at("mix", 32, "sb_t", [P, S5_P, S5_C])
        sv = at("gain", 0, "sv", [P, 22, S5_P])
        pks = at("gain", 5.5, "pks", [P, 3, 2, S5_P])
        cpad = at("mix", 32, "cpad", [P, S5_PAIRS, 2, 2, S5_C])
        powr = at("mix", 0, "powr", [P, 2, 2, S5_PAIRS, 16])
        ptmp = at("gain", 0, "ptmp", [P, 2, S5_PAIRS, 8])
        epow = at("gain", 4, "epow", [P, 4, S5_PAIRS])
        tmul = at("gain", 0, "tmul", [P, 2, TG, S])
        tmade = at("mix", 16, "tmade", [P, 2, TG, 2, S])
        tab = at("xt", 0, "tab", [P, 2, TG, 2, S])
        zz = at("xt", 16, "zz", [P, 2, 2, S])
        zc = at("xt", 20, "zc", [P, 2, 2, S])
        zs5 = at("xt", 24, "zs5", [P, 2, 2, S])
        rot = [at("stg", 0, "rot0", [P, 2, 2, S]), at("xt", 28, "rot1", [P, 2, 2, S])]
        vv = at("stg", 4, "vv", [P, 2, 2, S])
        bpad = at("low", 0, "bpad", [P, 2, 2, 2, S5_P])
        uT = at("hid", 0, "uT", [P, KT, S])
        bbT = at("hid", 16, "bbT", [P, KT, 2, S5_P])
        skip = at("hid", 24, "skip", [P, D])
        fq = at("mix", 0, "fq", [P, F_HEADS, S])
        fk = at("mix", 8, "fk", [P, F_HEADS, S])
        fv = at("mix", 16, "fv", [P, MT, H1])
        fz = at("mix", 24, "fz", [P, MT, H1])
        mixmu = at("mix", 32, "mixmu", [P, 4 * H1])
        fms = at("mix", 32, "fms", [P, 2, S])
        fpd = at("mix", 34, "fpd", [P, 2, S])
        fpT = at("mix", 36, "fpT", [P, 2, MT, P])
        fo = at("mix", 40, "fo", [P, MT, H1])
        rr = at("hid", 0, "rr", [P, MT, H1])
        kr = at("hid", 8, "kr", [P, MT, H1])
        vr = at("hid", 16, "vr", [P, MT, H1])
        zb = at("hid", 24, "zb", [P, MT, H1])
        kkrT = at("mix", 0, "kkrT", [P, R_PAIRS, 2, P])
        bkT = at("mix", 8, "bkT", [P, R_PAIRS, 2, P])
        A4 = at("mix", 16, "A4", [P, 8, 4, P])
        nU = at("mix", 32, "nU", [P, H1])
        nW = at("mix", 36, "nW", [P, H1])
        kkh = at("mix", 40, "kkh", [P, H1])
        bt = at("mix", 44, "bt", [P, H1])
        w0p = at("mix", 0, "w0p", [P, H1])
        a0p = at("mix", 4, "a0p", [P, H1])
        kkp = at("mix", 8, "kkp", [P, H1])
        kap = at("mix", 12, "kap", [P, H1])
        lnw = at("xt", 8, "lnw", [P, H1])
        lnb = at("xt", 12, "lnb", [P, H1])
        sg = at("mix", 16, "sg", [P, H1])
        sa = at("mix", 20, "sa", [P, H1])
        kk = at("mix", 24, "kk", [P, H1])
        bb = at("mix", 28, "bb", [P, H1])
        E0 = at("mix", 32, "E0", [P, H1])
        E1 = at("mix", 36, "E1", [P, H1])
        E2 = at("xt", 8, "E2", [P, H1])
        E3 = at("xt", 12, "E3", [P, H1])
        rkp = at("xt", 24, "rkp", [P, H1])
        tmp = at("xt", 28, "tmp", [P, H1])
        XA = at("xt", 8, "XA", [P, 8, P])
        XT = at("xt", 12, "XT", [P, 8, P])
        QQ = at("xt", 24, "QQ", [P, 8, P])
        AV = at("xt", 28, "AV", [P, 8, R_HD])
        MM = at("xt", 8, "MM", [P, 2, R_PAIRS, P])
        NN = at("xt", 24, "NN", [P, 2, R_PAIRS, P])
        yy = at("stg", 0, "yy", [P, MT, H1])
        ST = at("gain", 0, "ST", [P, 2, R_PAIRS, P])
        y2 = at("mix", 32, "y2", [P, H1])
        zs = at("mix", 36, "zs", [P, H1])
        shtmp = at("gain", 0, "shtmp", [P, MT, NW])
        lo = at("gain", 4, "lo", [P, MT, LC])
        lmu = at("gain", 5.75, "lmu", [P, 2 * LORA])
        fbias = at("gain", 6.5, "fbias", [P, F_HEADS])
        lf = at("gain", 6.75, "lf", [P, 3, MT, F_HEADS])
        ltmp = at("gain", 0, "ltmp", [P, MT, 2 * LORA])
        gg = at("mix", 0, "gg", [P, 2, 2, MT, NW])
        lw2 = at("mix", 40, "lw2", [LORA, 2, H1])
        gates_dram = nc.dram_tensor("gates_scratch", (2, S, D), F32, kind="Internal").ap()
        lT = at("low", 0, "lT", [LORA, 2, S])
        nct = sb("nct", [F_HEADS, S])
        rsm = sb("rsm", [P, 10, R_HEADS])
        lamT = sb("lamT", [P, R_PAIRS, 2])
        cmask = sb("cmask", [P, P])
        tri = sb("tri", [P, P])
        ones = sb("ones", [P, P])
        same = sb("same", [P, P])
        mask2 = sb("mask2", [P, 2, P])
        decay = sb("decay", [P, 3, P])
        tot = sb("tot", [P, 2])
        shift = sb("shift", [P, P])
        corner = sb("corner", [P, P])
        level = sb("level", [P, LEVELS + 2, P])
        fstat = sb("fstat", [P, 8])
        pe_names, act_names, dve_names = fox_steps()
        rpe_names, ract_names, rdve_names = rwkv_steps()
        FPE, FACT, FDVE = Steps(pe_names), Steps(act_names), Steps(dve_names)
        RPE, RACT, RDVE = Steps(rpe_names), Steps(ract_names), Steps(rdve_names)
        srs = sb("srs", [P, 3, S5_PAIRS])
        pmask = sb("pmask", [P, 8])
        tab_dram = nc.dram_tensor("tab_scratch", (S5_PAIRS // TG, P, TG, 2, S), F32, kind="Internal").ap()
        bb_dram = nc.dram_tensor("bb_scratch", (P, S5_C, 2, S5_P), F32, kind="Internal").ap()
        small = sb("small", [P, 256])
        ss = small[:, 0:2]
        ssq = small[:, 96:96 + MT * QT].rearrange("p (m q) -> p m q", m=MT)
        std = small[:, 2:4]
        rstd = small[:, 4:6]
        amx = small[:, 8:12].rearrange("p (b t) -> p b t", b=2)
        anm = small[:, 12:16].rearrange("p (b t) -> p b t", b=2)
        asum = small[:, 16:20].rearrange("p (b t) -> p b t", b=2)
        ars = small[:, 20:24].rearrange("p (b t) -> p b t", b=2)
        ac1 = small[:, 24:26]
        lams = small[:, 26:28]
        lame = small[:, 28:30]
        nlam = small[:, 30:31]
        oss = small[:, 32:48]
        ostd = small[:, 48:64]
        orstd = small[:, 64:80]
        eps = small[:, 80:81]
        gn_eps = small[:, 81:82]
        ident = sb("ident", [P, P])
        dmask = sb("dmask", [P, P])

        acc = [[ctx.enter_context(nc.psum_tensor(f"acc{a}{m}", [P, NW], F32)) for m in range(MT)] for a in range(2)]
        tp = [ctx.enter_context(nc.psum_tensor(f"tp{b}", [P, 2, S], F32)) for b in range(2)]
        wk = [ctx.enter_context(nc.psum_tensor(f"wk{b}", [P, 2, S], F32)) for b in range(2)]

        raw_in = [sem(f"raw_in{j}") for j in range(RAW)]
        high_done = sem("high_done")
        split_done = sem("split_done")
        unit_used = sem("unit_used")
        acc_free = sem("acc_free")
        gain_first = sem("gain_first")
        gain_in = sem("gain_in")
        x_in = [sem(f"x_in{q}") for q in range(QT)]
        ssum_done = sem("ssum_done")
        sumsq_done = sem("sumsq_done")
        std_done = sem("std_done")
        rstd_done = sem("rstd_done")
        xn_done = sem("xn_done")
        group_done = sem("group_done")
        group_high = sem("group_high")
        group_free = sem("group_free")
        stg_done = sem("stg_done")
        const_a = sem("const_a")
        const_b = sem("const_b")
        mask_step = sem("mask_step")
        lam_in = sem("lam_in")
        lam_step = sem("lam_step")
        lam_exp = sem("lam_exp")
        score_done = sem("score_done")
        mask_done = sem("mask_done")
        max_done = sem("max_done")
        nmax_done = sem("nmax_done")
        exp_done = sem("exp_done")
        coef_step = sem("coef_step")
        prob_done = sem("prob_done")
        pv_done = sem("pv_done")
        o_out = sem("o_out")
        o_norm = sem("o_norm")
        out_done = sem("out_done")
        s5_in = sem("s5_in")
        s5_act = sem("s5_act")
        s5_step = sem("s5_step")
        s5_pool = sem("s5_pool")
        s5_turn = sem("s5_turn")
        s5_back = sem("s5_back")
        s5_out = sem("s5_out")
        pad_turn = sem("pad_turn")
        pad_done = sem("pad_done")
        bu_done = sem("bu_done")
        tab_step = sem("tab_step")
        tab_out = [sem("tab_out0"), sem("tab_out1")]
        tab_turn = sem("tab_turn")
        tab_in = [sem("tab_in0"), sem("tab_in1")]
        s5_cin = sem("s5_cin")
        skip_in = sem("skip_in")
        rot_done = sem("rot_done")
        v_done = sem("v_done")
        scan_done = sem("scan_done")
        zc_done = sem("zc_done")
        zs_done = sem("zs_done")
        x_done = sem("x_done")
        y_done = sem("y_done")
        skip_done = sem("skip_done")
        gelu_done = sem("gelu_done")
        glu_added = sem("glu_added")
        shift_done = sem("shift_done")
        shift_out = sem("shift_out")
        shift_mul = sem("shift_mul")
        gate_out = [sem("gate_out0"), sem("gate_out1")]
        f_in = sem("f_in")
        f_pe, f_act, f_dve = sem("f_pe"), sem("f_act"), sem("f_dve")
        r_kk_in = sem("r_kk_in")
        r_low_in = sem("r_low_in")
        r_in = sem("r_in")
        r_in2 = sem("r_in2")
        r_pe, r_act, r_dve = sem("r_pe"), sem("r_act"), sem("r_dve")
        gates_in = [sem("gates_in0"), sem("gates_in1")]
        mix_done = sem("mix_done")
        fin_done = sem("fin_done")

        block = ctx.enter_context(nc.Block())

        @block.sync
        def _(sp):
            t = Tally()

            def load(c, j, src):
                sp.wait_ge(split_done, c * UNITS + (j + 1))
                sp.dma_start(raw[:, j % RAW], src).then_inc(raw_in[j % RAW], 16)

            def stream(w, n):
                c0 = t.chunk
                wv = w.rearrange("(u k p) n -> u p k n", k=UK, p=P)
                with sp.Fori(0, n) as i:
                    for j in range(UNITS):
                        load(i + c0, j, wv[j][:, :, bass.ds(i * NW, NW)])
                t.chunk += n

            def stream_mlp(w1, w2):
                c0 = t.chunk
                w1v = w1.rearrange("(u k p) n -> u p k n", k=UK, p=P)
                w2v = w2.rearrange("(b r) n -> b r n", r=D)
                with sp.Fori(0, FB) as b:
                    for c in range(4):
                        for j in range(UNITS):
                            load(b * 8 + (c0 + c), j, w1v[j][:, :, bass.ds(b * D + c * NW, NW)])
                    for c in range(4):
                        for j in range(UNITS):
                            rows = w2[bass.ds(b * D + j * UK * P, UK * P), c * NW:(c + 1) * NW]
                            load(b * 8 + (c0 + 4 + c), j, rows.rearrange("(k p) n -> p k n", p=P))
                t.chunk += 8 * FB

            def s5_tables_back():
                sp.wait_ge(acc_free, S5_START)
                for b in range(2):
                    sp.wait_ge(tab_out[b], 16 * (S5_PAIRS // TG // 2))
                    sp.dma_start(tab[:, b], tab_dram[b]).then_inc(tab_in[b], 16)
                with sp.Fori(1, S5_PAIRS // TG // 2) as i:
                    for b in range(2):
                        sp.wait_ge(y_done, i * (2 * TG) + (TG * b - TG + 2))
                        sp.dma_start(tab[:, b], tab_dram[bass.ds(i * 2 + b, 1)].rearrange("o p a c s -> (o p) a c s")
                                     ).then_inc(tab_in[b], 16)

            for q in range(QT):
                cols = slice(q * NW, (q + 1) * NW)
                sp.dma_start(X[:, :, cols], I["x"][0].rearrange("(m p) n -> p m n", p=P)[:, :, cols]).then_inc(x_in[q], 16)
            sp.dma_start(gain[:], I["norm_mix"][0:1].broadcast_to([P, D])).then_inc(gain_first, 16)
            stream(I["a_w_in"][0], 12)
            stream(I["a_w_out"][0], 4)
            stream_mlp(I["mlp_w1"][0], I["mlp_w2"][0])
            c0 = t.chunk
            glu = [I["b_w_glu"][0][:, h * D:(h + 1) * D].rearrange("(u k p) n -> u p k n", k=UK, p=P) for h in (1, 0)]
            for c in range(8):
                for j in range(UNITS):
                    load(c0 + c, j, glu[c % 2][j][:, :, (c // 2) * NW:(c // 2 + 1) * NW])
                if c == 0:
                    s5_tables_back()
            t.chunk += 8
            stream_mlp(I["mlp_w1"][1], I["mlp_w2"][1])
            w = I["w_in_2"][0]
            stream(w[:, 0:4 * H1], 8)
            stream(w[:, 4 * H1 + F_HEADS:8 * H1 + F_HEADS], 8)
            c0 = t.chunk
            for j in range(UNITS):
                rows = w[j * UK * P:(j + 1) * UK * P]
                sp.wait_ge(split_done, c0 * UNITS + j + 1)
                sp.dma_start(raw[:, j % RAW, :, 0:F_HEADS],
                             rows[:, 4 * H1:4 * H1 + F_HEADS].rearrange("(k p) n -> p k n", p=P)).then_inc(raw_in[j % RAW], 16)
                sp.dma_start(raw[:, j % RAW, :, F_HEADS:LC],
                             rows[:, 8 * H1 + F_HEADS:8 * H1 + LC].rearrange("(k p) n -> p k n", p=P)).then_inc(raw_in[j % RAW], 16)
            t.chunk += 1
            stream(w[:, 8 * H1 + LC:], 8)
            c0 = t.chunk
            proj = [I[n][0].rearrange("(u k p) n -> u p k n", k=UK, p=P) for n in ("w_proj_fox_2", "w_proj_rwkv_2")]
            with sp.Fori(0, 4) as i:
                for j in range(UNITS):
                    load(i + c0, j, proj[j // HALF][j % HALF][:, :, bass.ds(i * NW, NW)])
            t.chunk += 4
            stream(I["w_out_2"][0], 4)
            for q in range(QT):
                cols = slice(q * NW, (q + 1) * NW)
                sp.wait_ge(fin_done, MT * q + MT)
                sp.dma_start(out[0].rearrange("(m p) n -> p m n", p=P)[:, :, cols], xn[:, :, cols]).then_inc(out_done, 16)
            sp.wait_ge(out_done, 16 * QT)

        @block.gpsimd
        def _(pool):
            norms = [I["norm_mix"][0:1], I["norm_mlp"][0:1], I["norm_mix"][1:2], I["norm_mlp"][1:2],
                     I["norm_final"].unsqueeze(0), I["norm_gain_2"][0:1], I["final_norm_gain_2"].unsqueeze(0)]

            nc.gpsimd.memset(ident[:], 0.0).then_inc(const_a, 1)
            nc.gpsimd.memset(eps, EPS).then_inc(const_a, 1)
            nc.gpsimd.memset(gn_eps, GN_EPS).then_inc(const_b, 1)
            nc.gpsimd.memset(dmask[:], 0.0).then_inc(const_a, 1)
            pool.wait_ge(const_a, 3)
            nc.gpsimd.affine_select(out=ident[:], in_=ident[:], compare_op=ALU.not_equal, fill=1.0, base=0,
                                    pattern=[[-1, P]], channel_multiplier=1).then_inc(const_b, 1)
            nc.gpsimd.memset(dmask[0:64, 64:128], NEG).then_inc(const_b, 1)
            nc.gpsimd.memset(pmask[:], 1.0).then_inc(const_a, 1)
            pool.wait_ge(const_a, 4)
            nc.gpsimd.affine_select(out=pmask[:], in_=pmask[:], compare_op=ALU.is_ge, fill=0.0, base=0,
                                    pattern=[[-S5_C, 8]], channel_multiplier=1).then_inc(const_a, 1)
            pool.wait_ge(const_a, 5)
            nc.gpsimd.affine_select(out=pmask[:], in_=pmask[:], compare_op=ALU.is_ge, fill=0.0, base=S5_C - 1,
                                    pattern=[[S5_C, 8]], channel_multiplier=-1).then_inc(const_b, 1)

            def second_layer_masks():
                mk = [0]

                def mlink(ins):
                    mk[0] += 1
                    ins.then_inc(mask_step, 1)
                    pool.wait_ge(mask_step, mk[0])

                def keep(t, pattern, base, mult, fill=0.0, op=ALU.is_ge):
                    mlink(nc.gpsimd.affine_select(out=t, in_=t, compare_op=op, fill=fill, base=base,
                                                  pattern=pattern, channel_multiplier=mult))

                def blocks(t, v):
                    mlink(nc.gpsimd.memset(t, 0.0))
                    for g in range(2):
                        h = slice(64 * g, 64 * g + 64)
                        mlink(nc.gpsimd.memset(t[h, h], v))

                mlink(nc.gpsimd.memset(cmask[:], 0.0))
                keep(cmask[:], [[-1, P]], 0, 1, NEG)
                mlink(nc.gpsimd.memset(tri[:], 1.0))
                keep(tri[:], [[1, P]], 0, -1)
                mlink(nc.gpsimd.memset(ones[:], 1.0))
                blocks(same[:], 1.0)
                for e in range(2):
                    blocks(mask2[:, e], 1.0)
                    keep(mask2[:, e], [[1, P]], e - 1, -1)
                    blocks(decay[:, e], NEG_DECAY)
                    keep(decay[:, e], [[1, P]], e - 1, -1)
                blocks(decay[:, 2], NEG_DECAY)
                keep(decay[:, 2], [[-1, P]], -1, 1)
                mlink(nc.gpsimd.memset(tot[:], 0.0))
                for g in range(2):
                    mlink(nc.gpsimd.memset(tot[64 * g:64 * g + 64, g:g + 1], NEG_DECAY))
                mlink(nc.gpsimd.memset(shift[:], 0.0))
                keep(shift[:], [[1, P]], -1, -1, 1.0, ALU.not_equal)
                keep(shift[:], [[1, P]], 0, -1, -1.0, ALU.not_equal)
                mlink(nc.gpsimd.memset(corner[:], 0.0))
                keep(corner[:], [[-P, P]], -(P - 1), 1, 1.0, ALU.not_equal)
                for lv in range(LEVELS + 1):
                    w = 1 << lv
                    lm = level[:, lv + 1 if lv else 0].rearrange("p (n e w) -> p n e w", e=2, w=w)
                    mlink(nc.gpsimd.memset(level[:, lv + 1 if lv else 0], 1.0 if lv else -1.0))
                    mlink(nc.gpsimd.memset(lm[:, :, 1], 0.0))
                    keep(lm[:, :, 0], [[-2 * w, P // (2 * w)], [0, w]], -w, 1)
                    keep(lm[:, :, 0], [[2 * w, P // (2 * w)], [0, w]], 2 * w - 1, -1)
                lm = level[:, 1].rearrange("p (n e) -> p n e", e=2)
                mlink(nc.gpsimd.memset(level[:, 1], 0.0))
                keep(lm[:, :, 1], [[-2, P // 2]], 0, 1, -1.0, ALU.not_equal)
                mlink(nc.gpsimd.memset(fstat[:], 0.0))
                assert mk[0] == MASK_STEPS, mk[0]

            def s5_tables():
                n = [0]

                def link(ins):
                    n[0] += 1
                    ins.then_inc(s5_pool, 1)
                    pool.wait_ge(s5_pool, n[0])

                pool.wait_ge(s5_step, S5_STEPS)
                link(nc.gpsimd.memset(cpad[:], 0.0))
                pool.wait_ge(s5_back, 2)
                pool.wait_ge(s5_out, 16)

                def times(dr, di, ar, ai, br, bi, shape):
                    w = shape[-1]
                    ta, tb = ptmp[:, 0, :, 0:w], ptmp[:, 1, :, 0:w]
                    link(nc.gpsimd.tensor_tensor(ta, ar, br, ALU.mult))
                    link(nc.gpsimd.tensor_tensor(tb, ai, bi, ALU.mult))
                    link(nc.gpsimd.tensor_tensor(dr, ta, tb, ALU.subtract))
                    link(nc.gpsimd.tensor_tensor(ta, ar, bi, ALU.mult))
                    link(nc.gpsimd.tensor_tensor(tb, ai, br, ALU.mult))
                    link(nc.gpsimd.tensor_tensor(di, ta, tb, ALU.add))

                er, ei = srs[:, 1], srs[:, 2]
                flip = 0
                for a in range(2):
                    link(nc.gpsimd.memset(powr[:, a, 0, :, 0:1], 1.0))
                    link(nc.gpsimd.memset(powr[:, a, 1, :, 0:1], 0.0))
                    for lvl in range(4):
                        w = 1 << lvl
                        sh = [P, S5_PAIRS, w]
                        times(powr[:, a, 0, :, w:2 * w], powr[:, a, 1, :, w:2 * w],
                              powr[:, a, 0, :, 0:w], powr[:, a, 1, :, 0:w],
                              er.unsqueeze(2).broadcast_to(sh), ei.unsqueeze(2).broadcast_to(sh), sh)
                        nr, ni = epow[:, flip], epow[:, flip + 1]
                        times(nr.unsqueeze(2), ni.unsqueeze(2), er.unsqueeze(2), ei.unsqueeze(2),
                              er.unsqueeze(2), ei.unsqueeze(2), [P, S5_PAIRS, 1])
                        er, ei = nr, ni
                        flip = 2 - flip

                pool.wait_ge(s5_back, 18)
                sh = [P, TG, 16, 16]
                four = lambda t: t.rearrange("p a (h l) -> p a h l", h=16)
                ta, tb = four(tmul[:, 0]), four(tmul[:, 1])

                def pair_tables(i, first=False):
                    for b in range(2):
                        pairs = bass.ds(i * (2 * TG) + TG * b, TG)
                        hi = [powr[:, 1, c, pairs].unsqueeze(3).broadcast_to(sh) for c in range(2)]
                        lo = [powr[:, 0, c, pairs].unsqueeze(2).broadcast_to(sh) for c in range(2)]
                        if not first:
                            pool.wait_ge(tab_out[b], i * 16)
                            nc.gpsimd.sem_inc(tab_turn, 1)
                        for c in range(2):
                            nc.gpsimd.tensor_tensor(ta, hi[0], lo[c], ALU.mult).then_inc(tab_step, 1)
                            nc.gpsimd.tensor_tensor(tb, hi[1], lo[1 - c], ALU.mult).then_inc(tab_step, 1)
                            pool.wait_ge(tab_step, i * 12 + (6 * b + 3 * c + 2))
                            nc.gpsimd.tensor_tensor(four(tmade[:, b, :, c]), ta, tb, ALU.add if c else ALU.subtract
                                                    ).then_inc(tab_step, 1)
                            pool.wait_ge(tab_step, i * 12 + (6 * b + 3 * c + 3))
                            nc.gpsimd.sem_inc(tab_turn, 1)
                        pool.dma_start(tab_dram[bass.ds(i * 2 + b, 1)].rearrange("o p a c s -> (o p) a c s"),
                                       tmade[:, b]).then_inc(tab_out[b], 16)

                pair_tables(0, first=True)
                with pool.Fori(1, S5_PAIRS // TG // 2) as i:
                    pair_tables(i)

            def s5_states():
                nc.gpsimd.sem_inc(zc_done, 2)
                with pool.Fori(0, S5_PAIRS // (2 * TG)) as i:
                    for q in range(2 * TG):
                        b = q % 2
                        cos = tab[:, q // TG, q % TG, 0:1].broadcast_to([P, 2, S])
                        pool.wait_ge(scan_done, i * (4 * TG) + (2 * q + 2))
                        pool.wait_ge(y_done, i * (2 * TG) + (q + 1))
                        nc.gpsimd.tensor_tensor(zc[:, b], zz[:, b], cos, ALU.mult).then_inc(zc_done, 1)
                        pool.wait_ge(zc_done, i * (2 * TG) + (q + 3))
                        pool.wait_ge(zs_done, i * (2 * TG) + (q + 1))
                        nc.gpsimd.tensor_tensor(zc[:, b, 0], zc[:, b, 0], zs5[:, b, 1], ALU.subtract).then_inc(x_done, 1)
                        nc.gpsimd.tensor_tensor(zc[:, b, 1], zc[:, b, 1], zs5[:, b, 0], ALU.add).then_inc(x_done, 1)

            for n, g in enumerate(norms):
                if n:
                    pool.wait_ge(xn_done, MT * QT * n)
                if n == 6:
                    pool.wait_ge(mix_done, 2)
                if n == 2:
                    s5_tables()
                if n:
                    pool.dma_start(gain[:], g.broadcast_to([P, D])).then_inc(gain_in, 16)
                if n == 0:
                    second_layer_masks()
                if n == 2:
                    s5_states()

        @block.tensor
        def _(pe):
            t = Tally()

            def product(c, fill, par, aH, aL, mid=None, first=None, n=NW, between=None, slots=SLOTS):
                pe.wait_ge(acc_free, fill * 2 + 2)
                for j in range(UNITS):
                    if j == HALF and mid is not None:
                        mid()
                    if first is not None:
                        first(j)
                    if between is not None and j in slots:
                        between(slots.index(j))
                    pe.wait_ge(split_done, c * UNITS + (j + 1 + RAW))
                    for u in range(UK):
                        k = j * UK + u
                        for m in range(MT):
                            rows = slice(m * P, m * P + P)
                            bank = acc[par][m][:, 0:n]
                            nc.tensor.matmul(bank, aH[:, k, rows], wH[:, j % SPLIT, u, 0:n], start=k == 0, stop=False)
                            nc.tensor.matmul(bank, aH[:, k, rows], wL[:, j % SPLIT, u, 0:n], start=False, stop=False)
                            last = nc.tensor.matmul(bank, aL[:, k, rows], wH[:, j % SPLIT, u, 0:n],
                                                    start=False, stop=k == KT - 1)
                    last.then_inc(unit_used, 1)

            def turn(n, blocks):
                pe.wait_ge(group_free, n + 1)
                for src, dst in blocks:
                    last = nc.tensor.transpose(dst, src, ident[:])
                last.then_inc(group_done, 1)

            def turn_wide(src, ready=None):
                for g in range(GROUPS):
                    if ready:
                        ready(g)
                    n = t.group + g
                    turn(n, [(src[:, m, (2 * g + k) * P:(2 * g + k + 1) * P], tp[g % 2][:, k, m * P:m * P + P])
                             for k in range(2) for m in range(MT)])
                t.group += GROUPS

            def ready(n0):
                return lambda j: pe.wait_ge(group_free, n0 + j + 3)

            def turn_stg(n, par):
                for g in range(2):
                    turn(n + g, [(stg[:, par, m, (2 * g + k) * P:(2 * g + k + 1) * P],
                                  tp[g][:, k, m * P:m * P + P]) for k in range(2) for m in range(MT)])

            def norm_turn():
                n0 = t.group
                turn_wide(xn, lambda g: pe.wait_ge(xn_done, MT * (QT * t.norm + g // 2 + 1)))
                t.norm += 1
                return ready(n0)

            def plain(n, aH, aL, first=None):
                c0, f0 = t.chunk, t.fill
                if first is not None:
                    product(c0, f0, 0, aH, aL, first=first)
                    product(c0 + 1, f0 + 1, 1, aH, aL)
                    done = 2
                else:
                    done = 0
                with pe.Fori(0, n - done, 2) as i:
                    for par in range(2):
                        product(i + (c0 + done + par), i + (f0 + done + par), par, aH, aL)
                t.chunk += n
                t.fill += n

            def mlp(after=None):
                first = norm_turn()
                c0, f0, g0, q0 = t.chunk, t.fill, t.group, t.square

                def block_of(b, first=None, after=None):
                    def turned(c):
                        def mid():
                            pe.wait_ge(stg_done, b * 8 + (q0 + 2 * c + 2))
                            turn_stg(b * 8 + (g0 + 2 * c), c % 2)
                        return mid
                    for c in range(4):
                        product(b * 8 + (c0 + c), b * 8 + (f0 + c), c % 2, xH, xL,
                                mid=turned(c - 1) if c else None, first=first if c == 0 else None)
                        if after:
                            after(c)
                    for c in range(4):
                        product(b * 8 + (c0 + 4 + c), b * 8 + (f0 + 4 + c), c % 2, hH, hL,
                                mid=turned(3) if c == 0 else None,
                                first=(lambda j: pe.wait_ge(group_free, b * 8 + (g0 + j + 3))) if c == 0 else None)
                        if after:
                            after(4 + c)

                block_of(0, first, after)
                with pe.Fori(1, FB) as b:
                    block_of(b)
                t.chunk += 8 * FB
                t.fill += 8 * FB
                t.group += 8 * FB
                t.square += 8 * FB

            nc.tensor.sem_inc(unit_used, SPLIT)
            pe.wait_ge(const_b, 4)
            first = norm_turn()
            c0, f0, g0, q0 = t.chunk, t.fill, t.group, t.square

            def qk_turn(c):
                def mid():
                    pe.wait_ge(acc_free, 2 * (f0 + c) + 6)
                    turn_stg(g0 + 2 * c, c % 2)
                return mid
            for c in range(8):
                product(c0 + c, f0 + c, c % 2, xH, xL, mid=qk_turn(c - 1) if c else None, first=first if c == 0 else None)
            t.chunk += 8
            t.fill += 8
            t.group += 16

            def scores(i):
                h, qt = i // 2, i % 2
                nk = (qt + 1) * P
                if i == 0:
                    pe.wait_ge(group_free, t.group + 2)
                if i >= 2:
                    pe.wait_ge(mask_done, masked(i - 2))
                for b in range(2):
                    last = nc.tensor.matmul(wk[i % 2][:, b, 0:nk], qT[:, 2 * h + b, qt * P:qt * P + P],
                                            kT[:, 2 * h + b, 0:nk], start=True, stop=True)
                last.then_inc(score_done, 1)

            def turn_probs(i):
                pe.wait_ge(prob_done, i + 1)
                if i >= 2:
                    pe.wait_ge(o_out, i - 1)
                turn(t.group + i, [(pd[:, i % 2, k * P:k * P + P], tp[i % 2][:, 0, k * P:k * P + P]) for k in range(i % 2 + 1)])

            def sums(i):
                h, qt = i // 2, i % 2
                pe.wait_ge(acc_free, 4 + 2 * (f0 + 9 + h // 2))
                pe.wait_ge(group_free, t.group + i + 3)
                for k in range(qt + 1):
                    last = nc.tensor.matmul(tp[i % 2][:, 1], pT[:, i % 2, k],
                                            va[:, k, h * DA_VD:(h + 1) * DA_VD], start=k == 0, stop=k == qt)
                last.then_inc(pv_done, 1)

            def slot(p):
                n = p - DA_FIRST
                if 3 <= n < DA_ITEMS + 3:
                    sums(n - 3)
                if 2 <= n < DA_ITEMS + 2:
                    turn_probs(n - 2)
                if 0 <= n < DA_ITEMS:
                    scores(n)

            for c in range(8, 12):
                product(c0 + c, f0 + c, c % 2, xH, xL, mid=qk_turn(7) if c == 8 else None,
                        between=lambda i: slot(4 * (c - 8) + i), slots=DA_SLOTS)
                slot(4 * (c - 8) + 3)
            t.chunk += 4
            t.fill += 4
            for p in range(16, DA_FIRST + DA_ITEMS + 3):
                slot(p)
            t.group += DA_ITEMS
            n0 = t.group
            turn_wide(oa, lambda g: pe.wait_ge(o_norm, 2 * g + 2))
            plain(4, xH, xL, first=ready(n0))

            def s5_turns(c):
                if c == 2:
                    pe.wait_ge(s5_step, S5_PHASES)
                    for j in range(3):
                        last = nc.tensor.transpose(wk[0][:].rearrange("p a s -> p (a s)")[:, j * P:j * P + P],
                                                   pks[:, j].rearrange("p a s -> p (a s)"), ident[:])
                    last.then_inc(s5_turn, 1)
                if c < 4:
                    return
                pe.wait_ge(s5_cin, 64)
                pe.wait_ge(s5_back, 2 + 4 * (c - 4))
                for b in range(2 * (c - 4), 2 * (c - 4) + 2):
                    bank = wk[b % 2][:].rearrange("p a s -> p (a s)")
                    for k in range(4):
                        last = nc.tensor.transpose(bank[:, k * P:k * P + P],
                                                   sb_c[:, b // 4, (b % 4) * 4 + k].rearrange("p a s -> p (a s)"), ident[:])
                    last.then_inc(s5_turn, 1)

            mlp(after=s5_turns)
            norm_turn()
            nc.tensor.sem_inc(bu_done, 2)
            nc.tensor.sem_inc(y_done, 2)
            pe.wait_ge(group_free, 2 + t.group)

            def inputs_of(s, k, b):
                pe.wait_ge(pad_done, s * 2 + 2)
                pe.wait_ge(rot_done, s * 2 + 2)
                for c in range(2):
                    last = nc.tensor.matmul(wk[b][:, c], bpad[:, b, c].rearrange("p a s -> p (a s)"),
                                            uT[:, bass.ds(k, 1)].rearrange("p o s -> p (o s)"), start=True, stop=True)
                last.then_inc(bu_done, 1)

            def outputs_of(s, s_ds, col, r, b):
                pe.wait_ge(x_done, s * 2 + 2)
                for m in range(MT):
                    for c in range(2):
                        last = nc.tensor.matmul(acc[r][m][:, col], zc[:, b, c, m * P:m * P + P],
                                                cpad[:, s_ds, c].rearrange("p o g c -> p (o g c)"), start=c == 0, stop=c == 1)
                last.then_inc(y_done, 1)

            def pairs_of(r, i, final=False):
                for q in range(2 * TG):
                    if not (final and q >= 2 * TG - 3):
                        inputs_of(i * (2 * TG) + (16 * r + q + 3), i * 2 + (4 * r + (q + 3) // 4), (q + 3) % 2)
                    s = i * (2 * TG) + (16 * r + q)
                    outputs_of(s, bass.ds(s, 1), bass.ds(i * (64 * TG) + 32 * q, 32), r % 2, q % 2)

            for q in range(3):
                inputs_of(q, 0, q % 2)
            for r in range(4):
                pe.wait_ge(acc_free, 2 * (t.fill + r) + 2)
                if r < 3:
                    with pe.Fori(0, 2) as i:
                        pairs_of(r, i)
                else:
                    pairs_of(r, 0)
                    pairs_of(r, 1, final=True)
            t.fill += 4
            n0 = t.group
            for r in range(4):
                pe.wait_ge(gelu_done, 2 * r + 2)
                for g in range(2 * r, 2 * r + 2):
                    turn(t.group + g, [(xn[:, m, (2 * g + k) * P:(2 * g + k + 1) * P], tp[g % 2][:, k, m * P:m * P + P])
                                       for k in range(2) for m in range(MT)])
            t.group += GROUPS
            plain(8, xH, xL, first=ready(n0))
            mlp()
            pe.wait_ge(mask_step, MASK_STEPS)
            t.norm += 1
            first = norm_turn()
            c0, f0, g0 = t.chunk, t.fill, t.group

            def stg_turn(c):
                def mid():
                    pe.wait_ge(acc_free, 2 * (f0 + c) + 6)
                    turn_stg(g0 + 2 * c, c % 2)
                return mid

            def shifted(c):
                def mid():
                    pe.wait_ge(acc_free, 2 * (f0 + c) + 6)
                    if c > 8:
                        pe.wait_ge(shift_out, 2 * (c - 8))
                    for m in range(MT):
                        bank = wk[m][:].rearrange("p a s -> p (a s)")
                        last = nc.tensor.matmul(bank, shift[:], stg[:, c % 2, m], start=True, stop=m == 0)
                        if m:
                            last = nc.tensor.matmul(bank, corner[:], stg[:, c % 2, 0], start=False, stop=True)
                    last.then_inc(shift_done, 1)
                return mid

            def mid_of(c):
                if 1 <= c <= 4:
                    return stg_turn(c - 1)
                if 9 <= c <= 16:
                    return shifted(c - 1)
            for c in range(17):
                product(c0 + c, f0 + c, c % 2, xH, xL, mid=mid_of(c), first=first if c == 0 else None,
                        n=LC if c == 16 else NW)
            t.chunk += 17
            t.fill += 16
            t.group += 8

            def small_shift():
                pe.wait_ge(f_act, FACT["lo", 1])
                pe.wait_ge(shift_out, 16)
                for m in range(MT):
                    bank = wk[m][:].rearrange("p a s -> p (a s)")[:, 0:2 * LORA]
                    last = nc.tensor.matmul(bank, shift[:], lo[:, m, F_HEADS:], start=True, stop=m == 0)
                    if m:
                        last = nc.tensor.matmul(bank, corner[:], lo[:, 0, F_HEADS:], start=False, stop=True)
                FPE.mark(f_pe, last, "shift", 0)

            def small_turn():
                pe.wait_ge(f_act, FACT["tanh",])
                bank = tp[0][0:LORA]
                for v in range(2):
                    for m in range(MT):
                        last = nc.tensor.transpose(bank[:, v, m * P:m * P + P],
                                                   lo[:, m, F_HEADS + v * LORA:F_HEADS + (v + 1) * LORA], ident[:])
                FPE.mark(f_pe, last, "lT")

            def running_sums():
                pe.wait_ge(f_dve, FDVE["lf",])
                cbank = tp[1][0:F_HEADS, 0]
                nc.tensor.matmul(cbank[:, 0:P], lf[:, 2, 0], tri[:], start=True, stop=True)
                nc.tensor.matmul(cbank[:, P:S], lf[:, 2, 0], ones[:], start=True, stop=False)
                FPE.mark(f_pe, nc.tensor.matmul(cbank[:, P:S], lf[:, 2, 1], tri[:], start=False, stop=True), "cum")

            def fox_scores(i):
                h, qt = i // 2, i % 2
                nk = (qt + 1) * P
                pe.wait_ge(f_act, FACT["nc",])
                pe.wait_ge(f_dve, FDVE["fm", i - 2] if i >= 2 else FDVE["ladd", 1])
                bank = wk[i % 2][:, 0, 0:nk]
                nc.tensor.matmul(bank, fq[:, h, qt * P:qt * P + P], fk[:, h, 0:nk], start=True, stop=False)
                FPE.mark(f_pe, nc.tensor.matmul(bank, ident[0:F_HEADS, h:h + 1].broadcast_to([F_HEADS, P]), nct[:, 0:nk],
                                                start=False, stop=True), "fs", i)

            def fox_turn(i):
                qt = i % 2
                pe.wait_ge(f_dve, FDVE["fp", i])
                pe.wait_ge(f_act, FACT["fv", i - 2] if i >= 2 else FACT["nc",])
                for k in range(qt + 1):
                    last = nc.tensor.transpose(tp[i % 2][:, 0, k * P:k * P + P], fpd[:, i % 2, k * P:k * P + P], ident[:])
                FPE.mark(f_pe, last, "ft", i)

            def fox_sums(i):
                h, qt = i // 2, i % 2
                pe.wait_ge(f_act, FACT["ft", i])
                for k in range(qt + 1):
                    last = nc.tensor.matmul(tp[i % 2][:, 1, 0:F_HD], fpT[:, i % 2, k],
                                            fv[:, k, h * F_HD:(h + 1) * F_HD], start=k == 0, stop=k == qt)
                FPE.mark(f_pe, last, "fv", i)

            def slot(p):
                if p < 3:
                    (small_shift, small_turn, running_sums)[p]()
                    return
                n = p - 3
                if 3 <= n < F_ITEMS + 3:
                    fox_sums(n - 3)
                if 2 <= n < F_ITEMS + 2:
                    fox_turn(n - 2)
                if n < F_ITEMS:
                    fox_scores(n)

            for k in range(8):
                fill = t.fill + k + (1 if k == 0 else 0)
                if k == 1:
                    pe.wait_ge(f_act, FACT["lo", 1])
                product(t.chunk + k, fill, (k + 1) % 2, xH, xL, between=lambda i: slot(3 * k + i))
                slot(3 * k + 2)
            t.chunk += 8
            t.fill += 8

            def turn_half(src, ready):
                for g in range(4):
                    turn(t.group + g, [(src[:, m, (2 * g + k) * P:(2 * g + k + 1) * P], tp[g % 2][:, k, m * P:m * P + P])
                                       for k in range(2) for m in range(MT)])
                t.group += 4

            pe.wait_ge(f_dve, FDVE["og", 1])
            turn_half(fo, None)
            pe.wait_ge(group_free, t.group + 2)

            B = [acc[0][0], acc[0][1], acc[1][0], acc[1][1], tp[0], tp[1], wk[0], wk[1]]
            B = [b[:] if n < 4 else b[:].rearrange("p a s -> p (a s)") for n, b in enumerate(B)]

            def wait(name_act=None, name_dve=None):
                if name_act:
                    pe.wait_ge(r_act, RACT[name_act])
                if name_dve:
                    pe.wait_ge(r_dve, RDVE[name_dve])

            for m in range(MT):
                pe.wait_ge(r_low_in, 32 * (m + 1))
                if m:
                    wait(name_dve=("O", m - 1, 1))
                for v in range(2):
                    for q in range(2):
                        last = nc.tensor.matmul(B[2 * v + q], lT[:, v, m * P:m * P + P], lw2[:, v, q * NW:(q + 1) * NW],
                                                start=True, stop=True)
                RPE.mark(r_pe, last, "lin", m)
                wait(("sigw", m), ("lina", m, 1))
                for e in range(3):
                    for q in range(2):
                        nc.tensor.matmul(B[2 * e + q], decay[:, e], sg[:, q * NW:(q + 1) * NW], start=True, stop=True)
                for p in range(R_PAIRS):
                    last = nc.tensor.matmul(B[6][:, 2 * p:2 * p + 2], sg[:, p * P:p * P + P], tot[:], start=True, stop=True)
                RPE.mark(r_pe, last, "cum", m)
                for i, (src, name) in enumerate(((kkh[:], "kkh"), (rr[:, m], "rh"), (kk[:], "bh"), (sg[:], "kh"))):
                    wait(("lam", m), (name, m))
                    for q in range(2):
                        for p in range(4):
                            c = 4 * q + p
                            last = nc.tensor.transpose(B[2 * i + q][:, p * P:p * P + P], src[:, c * P:c * P + P], ident[:])
                        RPE.mark(r_pe, last, "T", m, 2 * i + q)
                for g in range(2):
                    for h in range(8):
                        p, e = 4 * g + h // 2, h % 2
                        rows = slice(64 * e, 64 * e + 64)
                        if g == 0:
                            wait(("T", m, 7))
                        else:
                            wait(("Y", m, 0), ("R", m, 0))
                        for v in range(2):
                            last = nc.tensor.matmul(B[h][:, v * S:(v + 1) * S], bkT[rows, p, v],
                                                    kkrT[rows, p].rearrange("k v t -> k (v t)"), start=True, stop=True)
                        RPE.mark(r_pe, last, "A", m, g, h)
                    wait(name_dve=("A", m, g, 1))
                    for h in range(8):
                        p, e = 4 * g + h // 2, h % 2
                        rows = slice(64 * e, 64 * e + 64)
                        last = nc.tensor.matmul(B[e][:, (h // 2) * P:(h // 2 + 1) * P], kkrT[rows, p, 0], bkT[rows, p, 0],
                                                start=True, stop=True)
                    RPE.mark(r_pe, last, "L", m, g)
                    wait(name_dve=("A", m, g, 7))
                    for h in range(8):
                        hh = 8 * g + h
                        last = nc.tensor.matmul(B[6][:, h * R_HD:(h + 1) * R_HD], A4[:, h, 2], vr[:, m, hh * R_HD:(hh + 1) * R_HD],
                                                start=True, stop=True)
                    RPE.mark(r_pe, last, "AV", m, g)
                    for lv in range(1, LEVELS + 1):
                        for k in range(2):
                            wait(name_dve=("X", m, g, lv - 1, k) if lv > 1 else ("XT", m, g, 0))
                            for h in range(4 * k, 4 * k + 4):
                                last = nc.tensor.matmul(B[k][:, (h % 4) * P:(h % 4 + 1) * P], A4[:, h, 0], XA[:, h],
                                                        start=True, stop=True)
                            RPE.mark(r_pe, last, "Q", m, g, lv, k)
                        for k in range(2):
                            wait(name_dve=("Q", m, g, lv, k))
                            for h in range(4 * k, 4 * k + 4):
                                cols = slice((h % 4) * P, (h % 4 + 1) * P)
                                if lv < LEVELS:
                                    nc.tensor.matmul(B[2 + k][:, cols], XT[:, h], QQ[:, h], start=True, stop=True)
                                last = nc.tensor.matmul(B[4 + k][:, cols], QQ[:, h], XT[:, h], start=True, stop=True)
                            RPE.mark(r_pe, last, "XQ", m, g, lv, k)
                    wait(("AV", m, g), ("XT", m, g, LEVELS, 1))
                    for name, bank in (("U", 7), ("W", 6)):
                        for h in range(8):
                            hh = 8 * g + h
                            src = kkh[:, hh * R_HD:(hh + 1) * R_HD] if name == "U" else AV[:, h]
                            last = nc.tensor.matmul(B[bank][:, h * R_HD:(h + 1) * R_HD], XT[:, h], src, start=True, stop=True)
                        RPE.mark(r_pe, last, name, m, g)
                    wait(("W", m, g))
                    for h in range(8):
                        hh = 8 * g + h
                        e = h % 2
                        last = nc.tensor.matmul(B[0][64 * e:64 * e + 64, (h // 2) * P:(h // 2 + 1) * P],
                                                nU[:, hh * R_HD:(hh + 1) * R_HD], A4[:, h, 1], start=True, stop=True)
                    RPE.mark(r_pe, last, "R", m, g)
                    for h in range(8):
                        hh = 8 * g + h
                        cols = slice(hh * R_HD, (hh + 1) * R_HD)
                        o = B[1][:, h * R_HD:(h + 1) * R_HD]
                        nc.tensor.matmul(o, A4[:, h, 1], nW[:, cols], start=True, stop=False)
                        last = nc.tensor.matmul(o, A4[:, h, 3], vr[:, m, cols], start=False, stop=True)
                    RPE.mark(r_pe, last, "Y", m, g)
                wait(("Y", m, 1), ("R", m, 1))
                for c in range(2):
                    rows = slice(TC * c, TC * c + TC)
                    for p in range(R_PAIRS):
                        cols = slice(p * P, p * P + P)
                        last = nc.tensor.matmul(B[4 * c + p // 4][:, (p % 4) * P:(p % 4 + 1) * P], nU[rows, cols], bt[rows, cols],
                                                start=True, stop=True)
                    RPE.mark(r_pe, last, "M", m, c)
                for c in range(2):
                    rows = slice(TC * c, TC * c + TC)
                    for p in range(R_PAIRS):
                        cols = slice(p * P, p * P + P)
                        o = B[4 * c + 2 + p // 4][:, (p % 4) * P:(p % 4 + 1) * P]
                        nc.tensor.matmul(o, kr[rows, m, cols], vr[rows, m, cols], start=True, stop=False)
                        last = nc.tensor.matmul(o, bt[rows, cols], nW[rows, cols], start=False, stop=True)
                    RPE.mark(r_pe, last, "N", m, c)
                for c in range(2):
                    wait(name_dve=("N", m, 1, 1))
                    if c:
                        wait(name_dve=("S", m, 0))
                    elif m:
                        wait(name_dve=("S", m - 1, 1))
                    for p in range(R_PAIRS):
                        last = nc.tensor.matmul(B[p // 4][:, (p % 4) * P:(p % 4 + 1) * P], MM[:, c, p], ST[:, c, p],
                                                start=True, stop=True)
                    RPE.mark(r_pe, last, "S", m, c)
                    for p in range(R_PAIRS):
                        last = nc.tensor.matmul(B[2 + p // 4][TC * c:TC * c + TC, (p % 4) * P:(p % 4 + 1) * P],
                                                kkrT[:, p, 1, TC * c:TC * c + TC], ST[:, c, p], start=True, stop=True)
                    RPE.mark(r_pe, last, "O", m, c)
            pe.wait_ge(r_dve, RDVE["O", 1, 1])
            pe.wait_ge(group_free, t.group + 2)
            c0, f0, g0 = t.chunk, t.fill, t.group + 4

            def mixed_turn(c):
                pe.wait_ge(mix_done, 2 * c + 2)
                turn_stg(g0 + 2 * c, c % 2)
            for c in range(4):
                for j in range(UNITS):
                    par = j // HALF
                    if j % HALF == 0:
                        pe.wait_ge(acc_free, (f0 + 2 * c + par) * 2 + 2)
                        if par and c:
                            mixed_turn(c - 1)
                        elif par:
                            pe.wait_ge(r_dve, RDVE["ob", 1])
                            turn_half(zb, None)
                            pe.wait_ge(group_free, t.group + 2)
                    pe.wait_ge(split_done, (c0 + c) * UNITS + (j + 1 + RAW))
                    for u in range(UK):
                        k = j * UK + u
                        for m in range(MT):
                            rows = slice(m * P, m * P + P)
                            bank = acc[par][m][:]
                            nc.tensor.matmul(bank, xH[:, k, rows], wH[:, j % SPLIT, u], start=k % 8 == 0, stop=False)
                            nc.tensor.matmul(bank, xH[:, k, rows], wL[:, j % SPLIT, u], start=False, stop=False)
                            last = nc.tensor.matmul(bank, xL[:, k, rows], wH[:, j % SPLIT, u], start=False, stop=k % 8 == 7)
                    last.then_inc(unit_used, 1)
            t.chunk += 4
            t.fill += 8
            t.group += 8

            def last_turn(j):
                if j == 6:
                    mixed_turn(3)
                pe.wait_ge(group_free, g0 + j + 3)
            product(t.chunk, t.fill, 0, hH, hL, first=last_turn)
            for c in range(1, 4):
                product(t.chunk + c, t.fill + c, c % 2, hH, hL)

        @block.scalar
        def _(act):
            t = Tally()

            def split(c, half, small=False, units=None):
                for j in units or range(half * HALF, half * HALF + HALF):
                    loads = j // RAW + 1
                    act.wait_ge(raw_in[j % RAW], c * (16 * UNITS // RAW) + (16 * loads * (2 if small else 1) + t.extra))
                    act.wait_ge(unit_used, c * UNITS + (j + 1))
                    n = LC if small else NW
                    nc.scalar.copy(wH[:, j % SPLIT, :, 0:n], raw[:, j % RAW, :, 0:n]).then_inc(high_done, 1)

            def steps(n, evac, turned=None, small=None):
                c0 = t.chunk
                for k in range(n):
                    split(c0 + k, 1, k == small)
                    if k == small:
                        t.extra = 16 * UNITS // RAW
                    if turned is not None and k:
                        turned(k - 1)
                    split(c0 + k + 1, 0, k + 1 == small)
                    evac(k)
                t.chunk += n

            def value_chunks(slot, turned, evac):
                for k in range(4):
                    c = t.chunk + k
                    split(c, 1, units=(4, 5))
                    slot(4 * k)
                    split(c, 1, units=(6, 7))
                    if k == 0:
                        turned()
                    slot(4 * k + 1)
                    split(c + 1, 0, units=(0, 1))
                    slot(4 * k + 2)
                    split(c + 1, 0, units=(2, 3))
                    slot(4 * k + 3)
                    evac(8 + k)
                t.chunk += 4

            def gate_chunks(slot, evac):
                for k in range(8):
                    c = t.chunk + k
                    split(c, 1, units=(4, 5, 6))
                    slot(3 * k)
                    split(c, 1, units=(7,))
                    split(c + 1, 0, units=(0, 1))
                    slot(3 * k + 1)
                    split(c + 1, 0, units=(2, 3))
                    slot(3 * k + 2)
                    evac(17 + k)
                t.chunk += 8

            def done(c):
                act.wait_ge(unit_used, c * UNITS + (UNITS + SPLIT))

            def high(n, nh, bank, dst):
                act.wait_ge(group_done, n + 1)
                nc.scalar.copy(dst, tp[bank][:]).then_inc(group_high, 1)

            def high_wide(dH):
                for g in range(GROUPS):
                    high(t.group + g, None, g % 2, dH[:, 2 * g:2 * g + 2])
                t.group += GROUPS

            def norm(ready):
                for q in range(QT):
                    if q == QT - 1:
                        nc.scalar.activation(small[:, 104 + t.norm:105 + t.norm], eps, ACT.Sqrt)
                    ready(q)
                    if q:
                        act.wait_ge(sumsq_done, MT * (QT * t.norm + q))
                    for m in range(MT):
                        nc.scalar.activation(wk[m][:].rearrange("p a s -> p (a s)"), X[:, m, q * NW:(q + 1) * NW], ACT.Square,
                                             accum_out=ssq[:, m, q:q + 1]).then_inc(sumsq_done, 1)
                act.wait_ge(ssum_done, t.norm + 1)
                nc.scalar.activation(std, ss, ACT.Sqrt, bias=eps, scale=1.0 / D).then_inc(std_done, 1)
                t.norm += 1

            def added(q):
                act.wait_ge(acc_free, t.x_ready - MT * (QT - 1 - q))

            def mlp(before=None, after=None, ready=added):
                norm(ready)
                high_wide(xH)
                if before:
                    before()
                c0, f0, g0, q0 = t.chunk, t.fill, t.group, t.square

                def block_of(b, after=None):
                    def turned(c):
                        for g in range(2):
                            high(b * 8 + (g0 + 2 * c + g), None, g, hH[:, 4 * c + 2 * g:4 * c + 2 * g + 2])
                    for c in range(8):
                        split(b * 8 + (c0 + c), 1)
                        if 1 <= c <= 4:
                            turned(c - 1)
                        split(b * 8 + (c0 + c + 1), 0)
                        if c < 4:
                            done(b * 8 + (c0 + c))
                            if c == 0:
                                act.wait_ge(acc_free, b * 16 + (2 * f0 + 4))
                            if c >= 2:
                                act.wait_ge(group_done, b * 8 + (g0 + 2 * (c - 1)))
                            for m in range(MT):
                                nc.scalar.activation(stg[:, c % 2, m], acc[c % 2][m][:], ACT.Relu).then_inc(acc_free, 1)
                        if after:
                            after(c)

                block_of(0, after)
                with act.Fori(1, FB) as b:
                    block_of(b)
                t.chunk += 8 * FB
                t.fill += 8 * FB
                t.group += 8 * FB
                t.square += 8 * FB
                t.x_ready = 4 + 2 * t.fill

            act.wait_ge(const_b, 4)
            act.dma_start(lamv[:], I["a_lambda"].rearrange("o a d -> o (a d)").broadcast_to([P, 4 * DA_HD])).then_inc(lam_in, 16)
            act.dma_start(subg[:], I["a_subln"].broadcast_to([P, DA_VD])).then_inc(lam_in, 16)
            norm(lambda q: act.wait_ge(x_in[q], 16))
            split(0, 0)
            high_wide(xH)
            act.wait_ge(lam_step, 4)
            nc.scalar.activation(lame, lams, ACT.Exp).then_inc(lam_exp, 1)
            g0 = t.group

            def qk_turned(c):
                for g in range(2):
                    act.wait_ge(group_done, g0 + 2 * c + g + 1)
                    dst = qT if c < 4 else kT
                    k = 4 * (c % 4) + 2 * g
                    nc.scalar.copy(dst[:, k:k + 2], tp[g][:]).then_inc(group_free, 1)

            def qk_out(c):
                done(c)
                if c >= 8:
                    for m in range(MT):
                        nc.scalar.copy(va[:, m, (c - 8) * NW:(c - 7) * NW], acc[c % 2][m][:]).then_inc(acc_free, 1)
                    return
                if c >= 2:
                    act.wait_ge(group_done, g0 + 2 * (c - 1))
                for m in range(MT):
                    nc.scalar.copy(stg[:, c % 2, m], acc[c % 2][m][:]).then_inc(acc_free, 1)

            steps(8, qk_out, turned=qk_turned)
            t.group += 16

            def exps(i):
                nk = (i % 2 + 1) * P
                act.wait_ge(nmax_done, i + 1)
                for b in range(2):
                    e = ms[:, i % 2, b, 0:nk]
                    nc.scalar.activation(e, e, ACT.Exp, bias=anm[:, i % 2, b:b + 1], scale=DA_HD ** -0.5,
                                         accum_out=asum[:, i % 2, b:b + 1]).then_inc(exp_done, 1)

            def turned_probs(i):
                act.wait_ge(group_done, t.group + i + 1)
                if i >= 2:
                    act.wait_ge(pv_done, i - 1)
                nk = (i % 2 + 1) * P
                nc.scalar.copy(pT[:, i % 2].rearrange("p k q -> p (k q)")[:, 0:nk], tp[i % 2][:, 0, 0:nk]).then_inc(group_free, 1)

            def outs(i):
                h, qt = i // 2, i % 2
                act.wait_ge(pv_done, i + 1)
                o = oa[:, qt, h * DA_VD:(h + 1) * DA_VD]
                nc.scalar.copy(o, tp[i % 2][:, 1]).then_inc(o_out, 1)
                act.wait_ge(o_out, i + 1)
                if i:
                    act.wait_ge(lam_exp, 1 + i)
                nc.scalar.activation(osq[:], o, ACT.Square, accum_out=oss[:, i:i + 1]).then_inc(lam_exp, 1)

            def slot(p):
                n = p - DA_FIRST
                if 3 <= n < DA_ITEMS + 3:
                    outs(n - 3)
                if 2 <= n < DA_ITEMS + 2:
                    turned_probs(n - 2)
                if 0 <= n < DA_ITEMS:
                    exps(n)

            value_chunks(slot, lambda: qk_turned(7), qk_out)
            t.fill += 12
            for p in range(16, DA_FIRST + DA_ITEMS + 3):
                slot(p)
            t.group += DA_ITEMS
            act.wait_ge(lam_exp, 1 + DA_ITEMS)
            nc.scalar.activation(ostd, oss, ACT.Sqrt, bias=eps, scale=1.0 / DA_VD).then_inc(lam_exp, 1)
            high_wide(xH)
            steps(4, lambda c: None)
            t.fill += 4
            t.x_ready = 4 + 2 * t.fill

            def s5_load():
                act.dma_start(sv[:, 0], I["b_a_re"][0]).then_inc(s5_in, 16)
                act.dma_start(sv[:, 1], I["b_a_im"][0]).then_inc(s5_in, 16)
                act.dma_start(sv[:, 2, 0:1], I["b_log_dt"].rearrange("o g -> g o")).then_inc(s5_in, 16)
                for c, name in enumerate(("b_b_re", "b_b_im")):
                    act.dma_start(sb_b[:, c], I[name][0]).then_inc(s5_in, 16)
                for c, name in enumerate(("b_c_re", "b_c_im")):
                    for twice in range(2):
                        act.dma_start(sb_c[:, c, :, twice], I[name][0].rearrange("(k e) c p -> (e c) k p", e=8)).then_inc(s5_cin, 16)

            def s5_scalars(c):
                if c == 0:
                    act.wait_ge(s5_in, 80)
                    nc.scalar.activation(sv[:, 2, 1:2], sv[:, 2, 0:1], ACT.Exp).then_inc(s5_act, 1)
                if c == 1:
                    act.wait_ge(s5_step, 8)
                    nc.scalar.activation(sv[:, 5], sv[:, 3], ACT.Exp).then_inc(s5_act, 1)
                    nc.scalar.activation(sv[:, 6], sv[:, 7], ACT.Sin).then_inc(s5_act, 1)
                    nc.scalar.activation(sv[:, 8], sv[:, 7], ACT.Sin, scale=0.5).then_inc(s5_act, 1)
                if c == 5:
                    act.wait_ge(s5_step, S5_STEPS)
                    act.dma_start(bb_dram, sb_bb[:]).then_inc(s5_out, 16)

            mlp(before=s5_load, after=s5_scalars)
            norm(added)
            act.wait_ge(s5_out, 16)
            act.dma_start(bbT[:].rearrange("p k c s -> p k (c s)"),
                          bb_dram.rearrange("(k e) c r s -> (e c) k (r s)", e=8)).then_inc(s5_out, 16)
            act.dma_start(skip[:], I["b_d"].broadcast_to([P, D])).then_inc(skip_in, 16)
            for g in range(GROUPS):
                act.wait_ge(group_done, t.group + g + 1)
                nc.scalar.copy(uT[:, 2 * g:2 * g + 2], tp[g % 2][:]).then_inc(group_free, 1)
            t.group += GROUPS
            act.wait_ge(s5_out, 32)

            def gelus(r):
                for m in range(MT):
                    act.wait_ge(acc_free, 2 * (t.fill + r) + 4 + m + 1)
                    y = xn[:, m, r * NW:(r + 1) * NW]
                    nc.scalar.activation(y, y, ACT.Gelu_apprx_tanh).then_inc(gelu_done, 1)

            for r in range(4):
                with act.Fori(0, 4) as k:
                    for q in range(4):
                        act.wait_ge(bu_done, k * 4 + (16 * r + q + 1))
                        act.sem_inc(pad_turn, 1)
                        for g in range(2):
                            nc.scalar.activation(bpad[:, q % 2, :, g], bbT[:, bass.ds(k + 4 * r, 1)].rearrange("p o c s -> p (o c) s"),
                                                 ACT.Copy, scale=pmask[:, 2 * q + g:2 * q + g + 1]).then_inc(pad_done, 1)
                if r >= 2:
                    gelus(r - 2)
            gelus(2)
            gelus(3)
            t.fill += 4
            high_wide(xH)

            c0, f0 = t.chunk, t.fill

            def gate(c):
                if c % 2:
                    return
                done(c0 + c)
                if c:
                    act.wait_ge(glu_added, c)
                for m in range(MT):
                    nc.scalar.activation(stg[:, (c // 2) % 2, m], acc[0][m][:], ACT.Sigmoid).then_inc(acc_free, 1)

            steps(8, gate)
            t.fill += 8
            t.x_ready = 4 + 2 * t.fill
            mlp(ready=lambda q: act.wait_ge(glu_added, MT * (q + 1)))
            norm(added)
            before = MT * QT * (t.norm - 1)
            norm(lambda q: act.wait_ge(xn_done, before + MT * (q + 1)))
            high_wide(xH)
            act.dma_start(mixmu[:], I["rwkv_shift_mix_2"][:, 0:4 * H1].broadcast_to([P, 4 * H1])).then_inc(f_in, 16)
            act.dma_start(lmu[:], I["rwkv_shift_mix_2"][:, 4 * H1:].broadcast_to([P, 2 * LORA])).then_inc(f_in, 16)
            act.dma_start(fbias[:], I["fox_forget_bias_2"].broadcast_to([P, F_HEADS])).then_inc(f_in, 16)
            c0, f0, g0 = t.chunk, t.fill, t.group
            gates = gates_dram.rearrange("g (m p) n -> g p m n", p=P)

            def second_turned(c):
                if c < 4:
                    for g in range(2):
                        act.wait_ge(group_done, g0 + 2 * c + g + 1)
                        dst = fq if c < 2 else fk
                        k = 4 * (c % 2) + 2 * g
                        nc.scalar.copy(dst[:, k:k + 2], tp[g][:]).then_inc(group_free, 1)

            def second_out(c):
                done(c0 + c)
                for m in range(MT):
                    src = acc[c % 2][m][:]
                    if c < 4 or 8 <= c < 16:
                        dst = stg[:, c % 2, m]
                    elif c < 8:
                        dst = (fv if c < 6 else fz)[:, m, (c % 2) * NW:(c % 2 + 1) * NW]
                    elif c > 16:
                        dst = stg[:, c % 2, m]
                    if m == 0:
                        if 2 <= c < 4:
                            act.wait_ge(group_done, g0 + 2 * (c - 1))
                        if 10 <= c < 16:
                            act.wait_ge(shift_out, 2 * (c - 9))
                        if 17 <= c < 19:
                            act.wait_ge(shift_out, 16)
                        if c >= 19:
                            act.wait_ge(gate_out[c % 2], 16 * ((c - 19) // 2 + 1))
                    if c == 16:
                        FACT.mark(f_act, nc.scalar.copy(lo[:, m], src[:, 0:LC]), "lo", m)
                    elif c > 16:
                        nc.scalar.activation(dst, src, ACT.Sigmoid).then_inc(acc_free, 1)
                    else:
                        nc.scalar.copy(dst, src).then_inc(acc_free, 1)
                if c > 16:
                    n = c - 17
                    act.wait_ge(acc_free, 2 * (f0 + 16 + n) + 6)
                    act.dma_start(gates[n // 4][:, :, (n % 4) * NW:(n % 4 + 1) * NW], stg[:, c % 2]).then_inc(gate_out[c % 2], 16)

            steps(17, second_out, turned=second_turned, small=16)
            t.group += 8

            def small_scalars(p):
                if p == 1:
                    act.wait_ge(f_dve, FDVE["ladd", 1])
                    low = lo[:, :, F_HEADS:F_HEADS + LORA]
                    FACT.mark(f_act, nc.scalar.activation(low, low, ACT.Tanh), "tanh")
                    act.wait_ge(f_dve, FDVE["abs",])
                    FACT.mark(f_act, nc.scalar.activation(lf[:, 1], lf[:, 1], ACT.Exp, scale=-1.0), "fe")
                    act.wait_ge(f_act, FACT["fe",])
                    FACT.mark(f_act, nc.scalar.activation(lf[:, 1], lf[:, 1], ACT.Ln, bias=1.0), "fl")
                if p == 2:
                    act.wait_ge(f_pe, FPE["lT",])
                    FACT.mark(f_act, nc.scalar.copy(lT[:], tp[0][0:LORA]), "lT")
                if p == 3:
                    act.wait_ge(f_pe, FPE["cum",])
                    FACT.mark(f_act, nc.scalar.activation(nct[:], tp[1][0:F_HEADS, 0], ACT.Copy, scale=-1.0 / F_SCALE), "nc")

            def fox_exp(i):
                nk = (i % 2 + 1) * P
                act.wait_ge(f_dve, FDVE["fn", i])
                e = fms[:, i % 2, 0:nk]
                FACT.mark(f_act, nc.scalar.activation(e, e, ACT.Exp, bias=fstat[:, 2 + i % 2:3 + i % 2], scale=F_SCALE,
                                                      accum_out=fstat[:, 4 + i % 2:5 + i % 2]), "fe", i)

            def fox_turned(i):
                nk = (i % 2 + 1) * P
                act.wait_ge(f_pe, FPE["ft", i])
                FACT.mark(f_act, nc.scalar.copy(fpT[:, i % 2].rearrange("p k q -> p (k q)")[:, 0:nk], tp[i % 2][:, 0, 0:nk]), "ft", i)

            def fox_out(i):
                h, qt = i // 2, i % 2
                act.wait_ge(f_pe, FPE["fv", i])
                FACT.mark(f_act, nc.scalar.copy(fo[:, qt, h * F_HD:(h + 1) * F_HD], tp[i % 2][:, 1, 0:F_HD]), "fv", i)

            def slot(p):
                small_scalars(p)
                n = p - 3
                if 3 <= n < F_ITEMS + 3:
                    fox_out(n - 3)
                if 2 <= n < F_ITEMS + 2:
                    fox_turned(n - 2)
                if 0 <= n < F_ITEMS:
                    fox_exp(n)
                if n == F_ITEMS + 3:
                    for m in range(MT):
                        FACT.mark(f_act, nc.scalar.activation(fk[:, 4 * m:4 * m + 4].rearrange("p a s -> p (a s)"), fz[:, m],
                                                              ACT.Sigmoid), "sz", m)

            gate_chunks(slot, second_out)
            t.fill += 24

            def high_half(k0):
                for g in range(4):
                    high(t.group + g, None, g % 2, xH[:, k0 + 2 * g:k0 + 2 * g + 2])
                t.group += 4
            high_half(0)

            B = [acc[0][0], acc[0][1], acc[1][0], acc[1][1], tp[0], tp[1], wk[0], wk[1]]
            B = [b[:] if n < 4 else b[:].rearrange("p a s -> p (a s)") for n, b in enumerate(B)]

            def bcast(name, dst, s):
                act.dma_start(dst, I[name].broadcast_to([P, H1])).then_inc(s, 16)

            def end(m):
                act.wait_ge(r_dve, RDVE["vs", m])
                RACT.mark(r_act, nc.scalar.activation(rsm[:, 5], rsm[:, 4], ACT.Sqrt, bias=gn_eps, scale=1.0 / R_HD), "sd", m)
                RACT.mark(r_act, nc.scalar.activation(zs[:], zb[:, m], ACT.Sigmoid), "sz", m)

            act.wait_ge(group_free, t.group + 2)
            def load_kk():
                bcast("rwkv_k_k_2", kkp[:], r_kk_in)
                bcast("rwkv_k_a_2", kap[:], r_kk_in)

            def load_low():
                act.dma_start(lw2[:, 0], I["rwkv_w2_2"][0]).then_inc(r_low_in, 16)
                act.dma_start(lw2[:, 1], I["rwkv_a2_2"][0]).then_inc(r_low_in, 16)

            load_low()
            load_kk()
            for m in range(MT):
                if m:
                    act.wait_ge(r_dve, RDVE["O", m - 1, 1])
                bcast("rwkv_w0_2", w0p[:], r_in)
                bcast("rwkv_a0_2", a0p[:], r_in)
                act.dma_start(rkp[:], I["rwkv_r_k_2"].rearrange("o h n -> o (h n)").broadcast_to([P, H1])).then_inc(r_in, 16)
                act.wait_ge(r_dve, RDVE["kks", m])
                RACT.mark(r_act, nc.scalar.activation(rsm[:, 1], rsm[:, 0], ACT.Sqrt), "sqrt", m)
                act.wait_ge(r_dve, RDVE["linw", m, 1])
                RACT.mark(r_act, nc.scalar.activation(sg[:], sg[:], ACT.Sigmoid), "sigw", m)
                act.wait_ge(r_dve, RDVE["lina", m, 1])
                RACT.mark(r_act, nc.scalar.activation(sa[:], sa[:], ACT.Sigmoid), "siga", m)
                if m:
                    end(m - 1)
                    act.wait_ge(r_dve, RDVE["ob", m - 1])
                act.wait_ge(r_pe, RPE["cum", m])
                for name, dst, bank, sc in (("E0", E0, 0, 1.0), ("E1", E1, 2, 1.0), ("E2", E2, 2, -1.0), ("E3", E3, 4, 1.0)):
                    nc.scalar.activation(dst[:, 0:NW], B[bank], ACT.Exp, scale=sc)
                    RACT.mark(r_act, nc.scalar.activation(dst[:, NW:], B[bank + 1], ACT.Exp, scale=sc), name, m)
                RACT.mark(r_act, nc.scalar.activation(lamT[:].rearrange("p a c -> p (a c)"), B[6][:, 0:2 * R_PAIRS], ACT.Exp), "lam", m)
                for i in range(8):
                    dst = (kkrT if i < 4 else bkT)[:, 4 * (i % 2):4 * (i % 2) + 4, (i // 2) % 2]
                    act.wait_ge(r_pe, RPE["T", m, i])
                    RACT.mark(r_act, nc.scalar.copy(dst, B[i].rearrange("p (a t) -> p a t", a=4)), "T", m, i)
                for g in range(2):
                    half = slice(g * NW, (g + 1) * NW)
                    act.wait_ge(r_pe, RPE["AV", m, g])
                    RACT.mark(r_act, nc.scalar.copy(AV[:].rearrange("p a s -> p (a s)"), B[6]), "AV", m, g)
                    if g and m < MT - 1:
                        load_kk()
                    act.wait_ge(r_pe, RPE["U", m, g])
                    RACT.mark(r_act, nc.scalar.mul(nU[:, half], B[7], -1.0), "U", m, g)
                    act.wait_ge(r_pe, RPE["W", m, g])
                    RACT.mark(r_act, nc.scalar.mul(nW[:, half], B[6], -1.0), "W", m, g)
                    act.wait_ge(r_pe, RPE["Y", m, g])
                    RACT.mark(r_act, nc.scalar.copy(yy[:, m, half], B[1]), "Y", m, g)
                if m < MT - 1:
                    act.wait_ge(r_pe, RPE["N", m, 1])
                    load_low()
                act.wait_ge(r_pe, RPE["O", m, 1])
                bcast("rwkv_ln_w_2", lnw[:], r_in2)
                bcast("rwkv_ln_b_2", lnb[:], r_in2)
            end(MT - 1)
            high_half(8)

            for par in range(2):
                act.wait_ge(gate_out[par], 64)
            act.wait_ge(r_dve, RDVE["ob", 1])
            t0 = t.fill

            def load_gates(c):
                if c >= 2:
                    act.wait_ge(mix_done, 2 * (c - 1))
                for g in range(2):
                    act.dma_start(gg[:, c % 2, g], gates[g][:, :, c * NW:(c + 1) * NW]).then_inc(gates_in[c % 2], 16)

            load_gates(0)
            g0 = t.group

            def mixed_high(c):
                for g in range(2):
                    high(g0 + 2 * c + g, None, g, hH[:, 4 * c + 2 * g:4 * c + 2 * g + 2])

            steps(4, lambda c: load_gates(c + 1) if c < 3 else None, turned=mixed_high)
            t.fill += 8
            c0 = t.chunk
            split(c0, 1)
            mixed_high(3)
            for c in range(1, 4):
                split(c0 + c, 0)
                split(c0 + c, 1)
            t.fill += 4
            t.x_ready = 4 + 2 * t.fill
            norm(added)

        @block.vector
        def _(dve):
            t = Tally()

            def split(c, half, small=False, units=None):
                for j in units or range(half * HALF, half * HALF + HALF):
                    dve.wait_ge(high_done, c * UNITS + (j + 1))
                    n = LC if small else NW
                    nc.vector.tensor_tensor(wL[:, j % SPLIT, :, 0:n], raw[:, j % RAW, :, 0:n],
                                            wH[:, j % SPLIT, :, 0:n].bitcast(F32), ALU.subtract).then_inc(split_done, 1)

            def steps(n, evac, turned=None, small=None):
                c0 = t.chunk
                for k in range(n):
                    split(c0 + k, 1, k == small)
                    if k == small:
                        t.extra = 16 * UNITS // RAW
                    if turned is not None and k:
                        turned(k - 1)
                    split(c0 + k + 1, 0, k + 1 == small)
                    evac(k)
                t.chunk += n

            def value_chunks(slot, turned, evac):
                for k in range(4):
                    c = t.chunk + k
                    split(c, 1, units=(4, 5))
                    slot(4 * k)
                    split(c, 1, units=(6, 7))
                    if k == 0:
                        turned()
                    slot(4 * k + 1)
                    split(c + 1, 0, units=(0, 1))
                    slot(4 * k + 2)
                    split(c + 1, 0, units=(2, 3))
                    slot(4 * k + 3)
                    evac(8 + k)
                t.chunk += 4

            def gate_chunks(slot, evac):
                for k in range(8):
                    c = t.chunk + k
                    split(c, 1, units=(4, 5, 6))
                    slot(3 * k)
                    split(c, 1, units=(7,))
                    split(c + 1, 0, units=(0, 1))
                    slot(3 * k + 1)
                    split(c + 1, 0, units=(2, 3))
                    slot(3 * k + 2)
                    evac(17 + k)
                t.chunk += 8

            def done(c):
                dve.wait_ge(unit_used, c * UNITS + (UNITS + SPLIT))

            def low(nh, bank, dH, dL):
                dve.wait_ge(group_high, nh + 1)
                nc.vector.tensor_tensor(dL, tp[bank][:], dH.bitcast(F32), ALU.subtract).then_inc(group_free, 1)

            def low_of(g):
                low(t.high + g, g % 2, xH[:, 2 * g:2 * g + 2], xL[:, 2 * g:2 * g + 2])

            def low_wide():
                for g in range(GROUPS):
                    low_of(g)
                t.high += GROUPS
                t.group += GROUPS

            def norm(dst=xn, out_sem=None, lows=False):
                dve.wait_ge(sumsq_done, MT * QT * (t.norm + 1))
                nc.vector.tensor_reduce(ss, ssq, AX, ALU.add).then_inc(ssum_done, 1)
                dve.wait_ge(std_done, t.norm + 1)
                nc.vector.reciprocal(rstd, std).then_inc(rstd_done, 1)
                dve.wait_ge(rstd_done, t.norm + 1)
                if t.norm:
                    dve.wait_ge(gain_in, 16 * t.norm)
                else:
                    dve.wait_ge(gain_first, 16)
                for q in range(QT):
                    cols = slice(q * NW, (q + 1) * NW)
                    for m in range(MT):
                        nc.vector.scalar_tensor_tensor(dst[:, m, cols], X[:, m, cols], rstd[:, m:m + 1], gain[:, cols],
                                                       ALU.mult, ALU.mult).then_inc(out_sem or xn_done, 1)
                    if lows and q:
                        low_of(2 * q - 2)
                        low_of(2 * q - 1)
                if lows:
                    low_of(2 * QT - 2)
                    low_of(2 * QT - 1)
                    t.high += GROUPS
                    t.group += GROUPS
                t.norm += 1

            def add_to_x(c, par, cols):
                done(c)
                for m in range(MT):
                    nc.vector.tensor_tensor(X[:, m, cols], X[:, m, cols], acc[par][m][:], ALU.add).then_inc(acc_free, 1)

            def mlp(after=None):
                norm(lows=True)
                c0, f0, h0, q0 = t.chunk, t.fill, t.high, t.square

                def block_of(b, after=None):
                    def turned(c):
                        for g in range(2):
                            k = 4 * c + 2 * g
                            low(b * 8 + (h0 + 2 * c + g), g, hH[:, k:k + 2], hL[:, k:k + 2])
                    for c in range(8):
                        split(b * 8 + (c0 + c), 1)
                        if 1 <= c <= 4:
                            turned(c - 1)
                        split(b * 8 + (c0 + c + 1), 0)
                        if c < 4:
                            for m in range(MT):
                                dve.wait_ge(acc_free, b * 16 + (2 * (f0 + c) + 4 + m + 1))
                                r = stg[:, c % 2, m]
                                nc.vector.tensor_tensor(r, r, r, ALU.mult).then_inc(stg_done, 1)
                        else:
                            add_to_x(b * 8 + (c0 + c), c % 2, slice((c - 4) * NW, (c - 3) * NW))
                        if after:
                            after(c)

                block_of(0, after)
                with dve.Fori(1, FB) as b:
                    block_of(b)
                t.chunk += 8 * FB
                t.fill += 8 * FB
                t.high += 8 * FB
                t.group += 8 * FB
                t.square += 8 * FB

            nc.vector.sem_inc(split_done, RAW)
            nc.vector.sem_inc(acc_free, 4)
            nc.vector.sem_inc(group_free, 2)
            dve.wait_ge(const_b, 4)
            norm()
            split(0, 0)
            low_wide()
            dve.wait_ge(lam_in, 32)
            lv = lamv[:].rearrange("p (a b) d -> p a b d", b=2)
            nc.vector.tensor_tensor(lamp[:], lv[:, :, 0], lv[:, :, 1], ALU.mult).then_inc(lam_step, 1)
            nc.vector.tensor_scalar(subg[:], subg[:], 1.0 - LAMBDA_INIT, None, ALU.mult).then_inc(lam_step, 1)
            dve.wait_ge(lam_step, 2)
            nc.vector.tensor_reduce(lams, lamp[:], AX, ALU.add).then_inc(lam_step, 1)
            nc.vector.memset(ac1, 0.0).then_inc(lam_step, 1)
            dve.wait_ge(lam_exp, 1)
            nc.vector.tensor_tensor(nlam, lame[:, 1:2], lame[:, 0:1], ALU.subtract).then_inc(lam_step, 1)
            dve.wait_ge(lam_step, 5)
            nc.vector.tensor_scalar(nlam, nlam, -LAMBDA_INIT, None, ALU.add).then_inc(lam_step, 1)
            steps(8, lambda c: None)
            t.group += 16

            def masks(i):
                nk = (i % 2 + 1) * P
                m = ms[:, i % 2, :, 0:nk]
                dve.wait_ge(score_done, i + 1)
                if i >= 2:
                    dve.wait_ge(prob_done, i - 1)
                if nk > P:
                    nc.vector.tensor_copy(ms[:, i % 2, :, 0:P], wk[i % 2][:, :, 0:P]).then_inc(mask_done, 1)
                nc.vector.tensor_tensor(ms[:, i % 2, :, nk - P:nk], wk[i % 2][:, :, nk - P:nk],
                                        dmask[:].unsqueeze(1).broadcast_to([P, 2, P]), ALU.add).then_inc(mask_done, 1)
                dve.wait_ge(mask_done, masked(i))
                nc.vector.tensor_reduce(amx[:, i % 2], m, AX, ALU.max).then_inc(max_done, 1)
                dve.wait_ge(max_done, i + 1)
                nc.vector.tensor_scalar(anm[:, i % 2], amx[:, i % 2], -DA_HD ** -0.5, None, ALU.mult).then_inc(nmax_done, 1)

            def probs(i):
                nk = (i % 2 + 1) * P
                e = ms[:, i % 2]
                n = 3 * i
                dve.wait_ge(exp_done, 2 * i + 2)
                nc.vector.reciprocal(ars[:, i % 2], asum[:, i % 2]).then_inc(coef_step, 1)
                dve.wait_ge(coef_step, n + 1)
                nc.vector.tensor_tensor(ac1[:, i % 2:i % 2 + 1], ars[:, i % 2, 1:2], nlam, ALU.mult).then_inc(coef_step, 1)
                dve.wait_ge(coef_step, n + 2)
                nc.vector.tensor_scalar(e[:, 1, 0:nk], e[:, 1, 0:nk], ac1[:, i % 2:i % 2 + 1], None, ALU.mult).then_inc(coef_step, 1)
                dve.wait_ge(coef_step, n + 3)
                if i >= 2:
                    dve.wait_ge(group_done, t.group + i - 1)
                nc.vector.scalar_tensor_tensor(pd[:, i % 2, 0:nk], e[:, 0, 0:nk], ars[:, i % 2, 0:1], e[:, 1, 0:nk],
                                               ALU.mult, ALU.add).then_inc(prob_done, 1)

            def slot(p):
                n = p - DA_FIRST
                if 1 <= n <= DA_ITEMS:
                    probs(n - 1)
                if 0 <= n < DA_ITEMS:
                    masks(n)

            value_chunks(slot, lambda: None, lambda c: None)
            t.fill += 12
            for p in range(16, DA_FIRST + DA_ITEMS + 1):
                slot(p)
            t.group += DA_ITEMS
            dve.wait_ge(lam_exp, DA_ITEMS + 2)
            nc.vector.reciprocal(orstd, ostd).then_inc(lam_step, 1)
            dve.wait_ge(lam_step, 7)
            for i in range(DA_ITEMS):
                h, qt = i // 2, i % 2
                o = oa[:, qt, h * DA_VD:(h + 1) * DA_VD]
                nc.vector.scalar_tensor_tensor(o, o, orstd[:, i:i + 1], subg[:], ALU.mult, ALU.mult).then_inc(o_norm, 1)
                if qt and h >= 2:
                    low_of(h - 2)
            low_of(GROUPS - 2)
            low_of(GROUPS - 1)
            t.high += GROUPS
            t.group += GROUPS
            c0 = t.chunk
            steps(4, lambda c: add_to_x(c0 + c, c % 2, slice(c * NW, (c + 1) * NW)))
            t.fill += 4

            n = [0]

            def link(ins):
                n[0] += 1
                ins.then_inc(s5_step, 1)
                dve.wait_ge(s5_step, n[0])

            are, aim, dt = sv[:, 0], sv[:, 1], sv[:, 2, 1:2]

            def angles():
                dve.wait_ge(s5_act, 1)
                link(nc.vector.tensor_scalar(sv[:, 3], are, dt, None, ALU.mult))
                link(nc.vector.tensor_scalar(sv[:, 4], aim, dt, None, ALU.mult))
                link(nc.vector.tensor_scalar(sv[:, 7], sv[:, 4], 1 / (2 * math.pi), ROUND, ALU.mult, ALU.add))
                link(nc.vector.tensor_scalar(sv[:, 9], sv[:, 7], -ROUND, None, ALU.add))
                link(nc.vector.scalar_tensor_tensor(sv[:, 4], sv[:, 9], -TWO_PI_A, sv[:, 4], ALU.mult, ALU.add))
                link(nc.vector.scalar_tensor_tensor(sv[:, 4], sv[:, 9], -TWO_PI_B, sv[:, 4], ALU.mult, ALU.add))
                link(nc.vector.scalar_tensor_tensor(sv[:, 4], sv[:, 9], -TWO_PI_C, sv[:, 4], ALU.mult, ALU.add))
                link(nc.vector.tensor_scalar(sv[:, 7], sv[:, 4], PI_BELOW, -PI_BELOW, ALU.min, ALU.max))

            def factors():
                dve.wait_ge(s5_act, 4)
                sn, cs, mag = sv[:, 6], sv[:, 10], sv[:, 5]
                link(nc.vector.tensor_tensor(sv[:, 9], sv[:, 8], sv[:, 8], ALU.mult))
                link(nc.vector.tensor_scalar(cs, sv[:, 9], -2.0, 1.0, ALU.mult, ALU.add))
                link(nc.vector.tensor_tensor(sv[:, 11], mag, cs, ALU.mult))
                link(nc.vector.tensor_scalar(sv[:, 11], sv[:, 11], -1.0, None, ALU.add))
                link(nc.vector.tensor_tensor(sv[:, 12], mag, sn, ALU.mult))
                link(nc.vector.tensor_tensor(sv[:, 13], are, are, ALU.mult))
                link(nc.vector.tensor_tensor(sv[:, 14], aim, aim, ALU.mult))
                link(nc.vector.tensor_tensor(sv[:, 13], sv[:, 13], sv[:, 14], ALU.add))
                link(nc.vector.reciprocal(sv[:, 14], sv[:, 13]))
                for o, op, p0, q0 in ((15, ALU.add, (11, 0), (12, 1)), (16, ALU.subtract, (12, 0), (11, 1))):
                    link(nc.vector.tensor_tensor(sv[:, 17], sv[:, p0[0]], sv[:, p0[1]], ALU.mult))
                    link(nc.vector.tensor_tensor(sv[:, 18], sv[:, q0[0]], sv[:, q0[1]], ALU.mult))
                    link(nc.vector.tensor_tensor(sv[:, o], sv[:, 17], sv[:, 18], op))
                    link(nc.vector.tensor_tensor(sv[:, o], sv[:, o], sv[:, 14], ALU.mult))
                link(nc.vector.tensor_tensor(sv[:, 17], cs, cs, ALU.mult))
                link(nc.vector.tensor_tensor(sv[:, 18], sn, sn, ALU.mult))
                link(nc.vector.tensor_tensor(sv[:, 17], sv[:, 17], sv[:, 18], ALU.add))
                link(nc.vector.tensor_scalar(sv[:, 17], sv[:, 17], -0.5, 1.5, ALU.mult, ALU.add))
                for twice in range(2):
                    link(nc.vector.tensor_copy(pks[:, 0, twice], mag))
                    link(nc.vector.tensor_tensor(pks[:, 1, twice], cs, sv[:, 17], ALU.mult))
                    link(nc.vector.tensor_tensor(pks[:, 2, twice], sn, sv[:, 17], ALU.mult))
                assert n[0] == S5_PHASES

            def input_matrices(c):
                wide = [P, S5_P, S5_C]
                cr, ci = sv[:, 15].unsqueeze(2).broadcast_to(wide), sv[:, 16].unsqueeze(2).broadcast_to(wide)
                o = sb_bb[:, :, c].rearrange("p c s -> p s c")
                link(nc.vector.tensor_tensor(o, cr, sb_b[:, c], ALU.mult))
                link(nc.vector.tensor_tensor(sb_t[:], ci, sb_b[:, 1 - c], ALU.mult))
                link(nc.vector.tensor_tensor(o, o, sb_t[:], ALU.add if c else ALU.subtract))

            def phases():
                dve.wait_ge(s5_turn, 1)
                for g in range(2):
                    half = slice(64 * g, 64 * g + 64)
                    src = wk[0][half].rearrange("p a s -> p (a s)")[:, 0:3 * P].rearrange("p (v s g) -> p v s g", v=3, g=2)
                    nc.vector.tensor_copy(srs[half], src[:, :, :, g]).then_inc(s5_back, 1)

            def output_matrices(b):
                dve.wait_ge(s5_pool, 1)
                dve.wait_ge(s5_turn, b + 2)
                for g in range(2):
                    half = slice(64 * g, 64 * g + 64)
                    src = wk[b % 2][half].rearrange("p a s -> p (a s)").rearrange("p (s g c) -> p s g c", g=2, c=S5_C)
                    s0 = (b % 4) * 16
                    nc.vector.tensor_scalar(cpad[half, s0:s0 + 16, b // 4, g], src[:, :, g], -1.0 if b >= 4 else 1.0,
                                            None, ALU.mult).then_inc(s5_back, 1)

            def s5_vectors(c):
                if c == 0:
                    angles()
                if c == 1:
                    factors()
                if c == 2:
                    input_matrices(0)
                if c == 3:
                    input_matrices(1)
                    phases()
                if c >= 4:
                    for b in range(2 * (c - 4), 2 * (c - 4) + 2):
                        output_matrices(b)

            mlp(after=s5_vectors)
            for b in range(2):
                dve.wait_ge(tab_out[b], 16 * (S5_PAIRS // TG // 2))
            norm()
            dve.wait_ge(xn_done, MT * QT * t.norm)
            dve.wait_ge(group_done, t.group + GROUPS)
            t.group += GROUPS
            nc.vector.sem_inc(rot_done, 4)

            def rotate(s, q):
                b = q % 2
                dve.wait_ge(bu_done, s + 3)
                for c in range(2):
                    nc.vector.tensor_tensor(rot[b][:, c], wk[b][:], tab[:, q // TG, q % TG, c:c + 1].broadcast_to([P, 2, S]),
                                            ALU.mult).then_inc(rot_done, 1)

            def combine(s, q):
                b = q % 2
                dve.wait_ge(rot_done, s * 2 + 6)
                nc.vector.tensor_tensor(vv[:, b, 0], rot[b][:, 0, 0], rot[b][:, 1, 1], ALU.add).then_inc(v_done, 1)
                nc.vector.tensor_tensor(vv[:, b, 1], rot[b][:, 0, 1], rot[b][:, 1, 0], ALU.subtract).then_inc(v_done, 1)

            def scan(s, q):
                b = q % 2
                dve.wait_ge(v_done, s * 2 + 2)
                dve.wait_ge(zc_done, s + 1)
                for c in range(2):
                    nc.vector.tensor_tensor_scan(zz[:, b, c], srs[:, 0, bass.ds(s, 1)].broadcast_to([P, S]), vv[:, b, c],
                                                 0.0, ALU.mult, ALU.add).then_inc(scan_done, 1)

            def times_sin(s, q):
                b = q % 2
                dve.wait_ge(scan_done, s * 2 + 2)
                dve.wait_ge(y_done, s + 1)
                nc.vector.tensor_tensor(zs5[:, b], zz[:, b], tab[:, q // TG, q % TG, 1:2].broadcast_to([P, 2, S]),
                                        ALU.mult).then_inc(zs_done, 1)

            def pairs_of(r, i, final=False):
                for q in range(2 * TG):
                    s = i * (2 * TG) + (16 * r + q)
                    nxt = not (final and q == 2 * TG - 1)
                    q1 = (q + 1) % (2 * TG)
                    if nxt:
                        if q1 % TG == 0:
                            dve.wait_ge(tab_in[q1 // TG], i * 16 + (32 * r + (16 if q1 else 32)))
                        rotate(s + 1, q1)
                    scan(s, q)
                    if nxt:
                        combine(s + 1, q1)
                    times_sin(s, q)

            def add_outputs(r):
                dve.wait_ge(y_done, 16 * (r + 1) + 2)
                for m in range(MT):
                    y = xn[:, m, r * NW:(r + 1) * NW]
                    nc.vector.tensor_tensor(y, y, acc[r % 2][m][:], ALU.add).then_inc(acc_free, 1)

            dve.wait_ge(tab_in[0], 16)
            rotate(0, 0)
            combine(0, 0)
            for r in range(4):
                if r < 3:
                    with dve.Fori(0, 2) as i:
                        pairs_of(r, i)
                else:
                    pairs_of(r, 0)
                    pairs_of(r, 1, final=True)
                if r == 0:
                    dve.wait_ge(skip_in, 16)
                    for m in range(MT):
                        nc.vector.tensor_tensor(xn[:, m], xn[:, m], skip[:], ALU.mult).then_inc(skip_done, 1)
                    dve.wait_ge(skip_done, 2)
                else:
                    add_outputs(r - 1)
            add_outputs(3)
            t.fill += 4
            low_wide()
            c0, f0 = t.chunk, t.fill

            def glu(c):
                if not c % 2:
                    return
                done(c0 + c)
                for m in range(MT):
                    g = stg[:, (c // 2) % 2, m]
                    cols = slice((c // 2) * NW, (c // 2 + 1) * NW)
                    dve.wait_ge(acc_free, 2 * (f0 + c - 1) + 6 + m)
                    nc.vector.tensor_tensor(g, g, acc[1][m][:], ALU.mult).then_inc(acc_free, 1)
                    dve.wait_ge(acc_free, 2 * (f0 + c) + 4 + m + 1)
                    nc.vector.tensor_tensor(X[:, m, cols], X[:, m, cols], g, ALU.add).then_inc(glu_added, 1)

            steps(8, glu)
            t.fill += 8
            mlp()
            dve.wait_ge(mask_step, MASK_STEPS)
            norm(X)
            norm(lows=True)
            c0, f0 = t.chunk, t.fill
            dve.wait_ge(f_in, 48)

            def second_turned(c):
                if not 8 <= c < 16:
                    return
                n = c - 8
                dst = (rr, kr, vr, zb)[n // 2]
                dve.wait_ge(shift_done, n + 1)
                if n:
                    dve.wait_ge(shift_out, 2 * n)
                for m in range(MT):
                    nc.vector.tensor_tensor(shtmp[:, m], wk[m][:].rearrange("p a s -> p (a s)"), mixmu[:, n * NW:(n + 1) * NW],
                                            ALU.mult).then_inc(shift_mul, 1)
                for m in range(MT):
                    dve.wait_ge(shift_mul, 2 * n + m + 1)
                    nc.vector.tensor_tensor(dst[:, m, (n % 2) * NW:(n % 2 + 1) * NW], shtmp[:, m], stg[:, c % 2, m],
                                            ALU.add).then_inc(shift_out, 1)

            steps(17, lambda c: None, turned=second_turned, small=16)
            t.fill += 24
            t.group += 8

            def small_vectors(p):
                if p == 0:
                    for m in range(MT):
                        dve.wait_ge(f_act, FACT["lo", m])
                        FDVE.mark(f_dve, nc.vector.tensor_tensor(lf[:, 0, m], lo[:, m, 0:F_HEADS], fbias[:], ALU.add), "bias", m)
                    dve.wait_ge(f_pe, FPE["shift", 0])
                    for m in range(MT):
                        bank = wk[m][:].rearrange("p a s -> p (a s)")[:, 0:2 * LORA]
                        FDVE.mark(f_dve, nc.vector.tensor_tensor(ltmp[:, m], bank, lmu[:], ALU.mult), "lmul", m)
                        dve.wait_ge(f_dve, FDVE["lmul", m])
                        u = lo[:, m, F_HEADS:]
                        FDVE.mark(f_dve, nc.vector.tensor_tensor(u, ltmp[:, m], u, ALU.add), "ladd", m)
                    FDVE.mark(f_dve, nc.vector.scalar_tensor_tensor(lf[:, 1], lf[:, 0], -1.0, lf[:, 0], ALU.mult, ALU.max), "abs")
                    FDVE.mark(f_dve, nc.vector.tensor_scalar(lf[:, 2], lf[:, 0], 0.0, None, ALU.min), "min")
                if p == 2:
                    dve.wait_ge(f_act, FACT["fl",])
                    dve.wait_ge(f_dve, FDVE["min",])
                    FDVE.mark(f_dve, nc.vector.tensor_tensor(lf[:, 2], lf[:, 2], lf[:, 1], ALU.subtract), "lf")

            def fox_mask(i):
                nk = (i % 2 + 1) * P
                dve.wait_ge(f_pe, FPE["fs", i])
                if i >= 2:
                    dve.wait_ge(f_dve, FDVE["fp", i - 2])
                if nk > P:
                    FDVE.mark(f_dve, nc.vector.tensor_copy(fms[:, i % 2, 0:P], wk[i % 2][:, 0, 0:P]), "fc", i)
                FDVE.mark(f_dve, nc.vector.tensor_tensor(fms[:, i % 2, nk - P:nk], wk[i % 2][:, 0, nk - P:nk], cmask[:], ALU.add), "fm", i)
                dve.wait_ge(f_dve, FDVE["fm", i])
                FDVE.mark(f_dve, nc.vector.tensor_reduce(fstat[:, i % 2:i % 2 + 1], fms[:, i % 2, 0:nk], AX, ALU.max), "fx", i)
                dve.wait_ge(f_dve, FDVE["fx", i])
                FDVE.mark(f_dve, nc.vector.tensor_scalar(fstat[:, 2 + i % 2:3 + i % 2], fstat[:, i % 2:i % 2 + 1], -F_SCALE, None,
                                                         ALU.mult), "fn", i)

            def fox_prob(i):
                nk = (i % 2 + 1) * P
                dve.wait_ge(f_act, FACT["fe", i])
                FDVE.mark(f_dve, nc.vector.reciprocal(fstat[:, 6 + i % 2:7 + i % 2], fstat[:, 4 + i % 2:5 + i % 2]), "fr", i)
                dve.wait_ge(f_dve, FDVE["fr", i])
                if i >= 2:
                    dve.wait_ge(f_pe, FPE["ft", i - 2])
                FDVE.mark(f_dve, nc.vector.tensor_scalar(fpd[:, i % 2, 0:nk], fms[:, i % 2, 0:nk], fstat[:, 6 + i % 2:7 + i % 2], None,
                                                         ALU.mult), "fp", i)

            def slot(p):
                small_vectors(p)
                n = p - 3
                if 1 <= n <= F_ITEMS:
                    fox_prob(n - 1)
                if 0 <= n < F_ITEMS:
                    fox_mask(n)

            gate_chunks(slot, lambda c: None)
            for m in range(MT):
                sz = fk[:, 4 * m:4 * m + 4].rearrange("p a s -> p (a s)")
                dve.wait_ge(f_act, FACT["sz", m])
                FDVE.mark(f_dve, nc.vector.tensor_tensor(sz, sz, fz[:, m], ALU.mult), "oz", m)
                dve.wait_ge(f_dve, FDVE["oz", m])
                FDVE.mark(f_dve, nc.vector.tensor_tensor(fo[:, m], fo[:, m], sz, ALU.mult), "og", m)

            def low_half(k0):
                for g in range(4):
                    low(t.high + g, g % 2, xH[:, k0 + 2 * g:k0 + 2 * g + 2], xL[:, k0 + 2 * g:k0 + 2 * g + 2])
                t.high += 4
                t.group += 4
            low_half(0)

            B = [acc[0][0], acc[0][1], acc[1][0], acc[1][1], tp[0], tp[1], wk[0], wk[1]]
            B = [b[:] if n < 4 else b[:].rearrange("p a s -> p (a s)") for n, b in enumerate(B)]
            hd = lambda t: t.rearrange("p (h n) -> p h n", n=R_HD)
            wide = lambda t: t.unsqueeze(2).broadcast_to([P, R_HEADS, R_HD])
            over = lambda t, n: t.unsqueeze(1).broadcast_to([P, n, P])
            four = lambda b: b.rearrange("p (a t) -> p a t", a=4)
            TT = nc.vector.tensor_tensor

            def step(ins, *name):
                RDVE.mark(r_dve, ins, *name)

            def own(*name):
                dve.wait_ge(r_dve, RDVE[name])

            nc.vector.memset(ST[:, 0], 0.0).then_inc(shift_mul, 1)
            def end(m):
                y = yy[:, m]
                own("O", m, 1)
                step(nc.vector.tensor_reduce(rsm[:, 3], hd(y), AX, ALU.add), "mu", m)
                own("mu", m)
                step(nc.vector.tensor_scalar(rsm[:, 3], rsm[:, 3], -1.0 / R_HD, None, ALU.mult), "nm", m)
                own("nm", m)
                step(TT(hd(y), hd(y), wide(rsm[:, 3]), ALU.add), "yc", m)
                own("yc", m)
                step(TT(y2[:], y, y, ALU.mult), "y2", m)
                own("y2", m)
                step(nc.vector.tensor_reduce(rsm[:, 4], hd(y2[:]), AX, ALU.add), "vs", m)
                dve.wait_ge(r_act, RACT["sd", m])
                step(nc.vector.reciprocal(rsm[:, 7], rsm[:, 5]), "sr", m)
                own("sr", m)
                step(TT(hd(y), hd(y), wide(rsm[:, 7]), ALU.mult), "yn", m)
                dve.wait_ge(r_in2, 32 * (m + 1))
                own("yn", m)
                step(TT(y, y, lnw[:], ALU.mult), "yw", m)
                own("yw", m)
                step(TT(y, y, lnb[:], ALU.add), "yb", m)
                step(TT(hd(y2[:]), hd(vr[:, m]), wide(rsm[:, 6]), ALU.mult), "bv", m)
                own("bv", m)
                step(TT(y, y, y2[:], ALU.add), "yv", m)
                dve.wait_ge(r_act, RACT["sz", m])
                step(TT(zb[:, m], zb[:, m], zs[:], ALU.mult), "zz", m)
                own("zz", m)
                step(TT(zb[:, m], zb[:, m], y, ALU.mult), "ob", m)

            for m in range(MT):
                dve.wait_ge(r_kk_in, 32 * (m + 1))
                step(TT(kk[:], kr[:, m], kkp[:], ALU.mult), "kk0", m)
                own("kk0", m)
                step(TT(tmp[:], kk[:], kk[:], ALU.mult), "kk2", m)
                own("kk2", m)
                step(nc.vector.tensor_reduce(rsm[:, 0], hd(tmp[:]), AX, ALU.add), "kks", m)
                dve.wait_ge(r_act, RACT["sqrt", m])
                step(nc.vector.tensor_scalar(rsm[:, 1], rsm[:, 1], L2_EPS, None, ALU.max), "kkm", m)
                own("kkm", m)
                step(nc.vector.reciprocal(rsm[:, 2], rsm[:, 1]), "kkr", m)
                own("kkr", m)
                step(TT(hd(kk[:]), hd(kk[:]), wide(rsm[:, 2]), ALU.mult), "kk", m)
                dve.wait_ge(r_pe, RPE["lin", m])
                dve.wait_ge(r_in, 48 * (m + 1))
                for name, dst, par, b0 in (("linw", sg, w0p, 0), ("lina", sa, a0p, 2)):
                    for q in range(2):
                        cols = slice(q * NW, (q + 1) * NW)
                        step(TT(dst[:, cols], B[b0 + q], par[:, cols], ALU.add), name, m, q)
                if m:
                    end(m - 1)
                dve.wait_ge(r_act, RACT["siga", m])
                step(nc.vector.scalar_tensor_tensor(tmp[:], sa[:], -1.0, kap[:], ALU.add, ALU.mult), "ka", m)
                own("ka", m)
                step(nc.vector.scalar_tensor_tensor(kr[:, m], tmp[:], 1.0, kr[:, m], ALU.add, ALU.mult), "k'", m)
                step(TT(bb[:], kk[:], sa[:], ALU.mult), "b", m)
                own("b", m)
                step(TT(tmp[:], rr[:, m], kr[:, m], ALU.mult), "bo0", m)
                own("bo0", m)
                step(TT(tmp[:], tmp[:], rkp[:], ALU.mult), "bo1", m)
                own("bo1", m)
                step(nc.vector.tensor_reduce(rsm[:, 6], hd(tmp[:]), AX, ALU.add), "bon", m)
                dve.wait_ge(r_act, RACT["E3", m])
                step(TT(kkh[:], kk[:], E0[:], ALU.mult), "kkh", m)
                step(TT(rr[:, m], rr[:, m], E1[:], ALU.mult), "rh", m)
                own("kkh", m)
                step(TT(kk[:], bb[:], E2[:], ALU.mult), "bh", m)
                step(TT(sg[:], kr[:, m], E2[:], ALU.mult), "kh", m)
                step(TT(bt[:], bb[:], E3[:], ALU.mult), "bt", m)
                own("kh", m)
                step(TT(kr[:, m], kr[:, m], E3[:], ALU.mult), "kt", m)
                own("kt", m)
                for g in range(2):
                    dve.wait_ge(r_pe, RPE["T", m, 7])
                    for h in range(8):
                        dve.wait_ge(r_pe, RPE["A", m, g, h])
                        step(TT(A4[:, h].rearrange("p (v e) t -> p v e t", v=2), B[h].rearrange("p (v e t) -> p v e t", v=2, e=2),
                                mask2[:].unsqueeze(1).broadcast_to([P, 2, 2, P]), ALU.mult), "A", m, g, h)
                    dve.wait_ge(r_pe, RPE["L", m, g])
                    X4 = XA[:].rearrange("p (a e) s -> p a e s", e=2)
                    for e in range(2):
                        step(TT(X4[:, :, e], four(B[e]), over(level[:, 0], 4), ALU.mult), "x0", m, g, e)
                    own("A", m, g, 7)
                    step(TT(XT[:], A4[:, :, 0], over(level[:, 1], 8), ALU.mult), "xt0", m, g)
                    own("xt0", m, g)
                    step(TT(XA[:], XA[:], over(ident[:], 8), ALU.add), "X", m, g, 0)
                    step(TT(XT[:], XT[:], over(ident[:], 8), ALU.add), "XT", m, g, 0)
                    for lv in range(1, LEVELS + 1):
                        for k in range(2):
                            h4 = slice(4 * k, 4 * k + 4)
                            dve.wait_ge(r_pe, RPE["Q", m, g, lv, k])
                            step(TT(QQ[:, h4], four(B[k]), over(level[:, lv + 1], 4), ALU.mult), "Q", m, g, lv, k)
                        for k in range(2):
                            h4 = slice(4 * k, 4 * k + 4)
                            dve.wait_ge(r_pe, RPE["XQ", m, g, lv, k])
                            if lv < LEVELS:
                                step(TT(XA[:, h4], XA[:, h4], four(B[2 + k]), ALU.subtract), "X", m, g, lv, k)
                            step(TT(XT[:, h4], XT[:, h4], four(B[4 + k]), ALU.subtract), "XT", m, g, lv, k)
                    dve.wait_ge(r_pe, RPE["R", m, g])
                    dst = kkrT[:, 4 * g:4 * g + 4, 1]
                    step(TT(dst, dst, four(B[0]), ALU.add), "R", m, g)
                for name, dst, b0 in (("M", MM, 0), ("N", NN, 2)):
                    for c in range(2):
                        dve.wait_ge(r_pe, RPE[name, m, c])
                        for q in range(2):
                            step(TT(dst[:, c, 4 * q:4 * q + 4], four(B[4 * c + b0 + q]), over(same[:], 4), ALU.mult), name, m, c, q)
                for c in range(2):
                    new = ST[:, 1 - c]
                    if c:
                        own("S", m, 0)
                    if c or m:
                        dve.wait_ge(r_pe, RPE["O", m, 0] if c else RPE["O", m - 1, 1])
                    else:
                        dve.wait_ge(shift_mul, 17)
                    step(TT(new, ST[:, c], lamT[:, :, c:c + 1].broadcast_to([P, R_PAIRS, P]), ALU.mult), "sl", m, c)
                    dve.wait_ge(r_pe, RPE["S", m, c])
                    own("sl", m, c)
                    for q in range(2):
                        part = ST[:, 1 - c, 4 * q:4 * q + 4]
                        step(TT(part, part, four(B[q]), ALU.add), "sb", m, c, q)
                    own("sb", m, c, 1)
                    step(TT(new, new, NN[:, c], ALU.add), "S", m, c)
                dve.wait_ge(r_pe, RPE["O", m, 1])
                dve.wait_ge(r_act, RACT["Y", m, 1])
                for q in range(2):
                    cols = slice(q * NW, (q + 1) * NW)
                    step(TT(yy[:, m, cols], yy[:, m, cols], B[2 + q], ALU.add), "O", m, q)
            end(MT - 1)
            low_half(8)

            c0, f0, h0 = t.chunk, t.fill, t.high

            def mixed_low(c):
                for g in range(2):
                    k = 4 * c + 2 * g
                    low(h0 + 2 * c + g, g, hH[:, k:k + 2], hL[:, k:k + 2])

            def gated(c, g):
                dve.wait_ge(unit_used, (c0 + c) * UNITS + ((g + 1) * HALF + SPLIT))
                dve.wait_ge(gates_in[c % 2], 32 * (c // 2 + 1))
                for m in range(MT):
                    v = gg[:, c % 2, g, m]
                    TT(v, v, acc[g][m][:], ALU.mult).then_inc(acc_free, 1)

            def mixed(c):
                if c >= 2:
                    dve.wait_ge(group_done, t.group + 2 * (c - 1))
                gated(c, 1)
                dve.wait_ge(acc_free, 2 * (f0 + 2 * c) + 8)
                for m in range(MT):
                    TT(stg[:, c % 2, m], gg[:, c % 2, 0, m], gg[:, c % 2, 1, m], ALU.add).then_inc(mix_done, 1)

            for c in range(4):
                split(c0 + c, 1)
                if c:
                    mixed_low(c - 1)
                gated(c, 0)
                split(c0 + c + 1, 0)
                mixed(c)
            t.chunk += 4
            t.fill += 8
            t.high += 8
            t.group += 8
            c0 = t.chunk
            split(c0, 1)
            mixed_low(3)
            for c in range(4):
                if c < 3:
                    split(c0 + c + 1, 0)
                add_to_x(c0 + c, c % 2, slice(c * NW, (c + 1) * NW))
                if c < 3:
                    split(c0 + c + 1, 1)
            norm(out_sem=fin_done)


_INS = ['x', 'norm_mix', 'norm_mlp', 'norm_final', 'a_w_in', 'a_lambda', 'a_subln', 'a_w_out',
        'b_a_re', 'b_a_im', 'b_log_dt', 'b_b_re', 'b_b_im', 'b_c_re', 'b_c_im', 'b_d', 'b_w_glu',
        'mlp_w1', 'mlp_w2', 'norm_gain_2', 'w_in_2', 'fox_forget_bias_2', 'rwkv_shift_mix_2',
        'rwkv_w0_2', 'rwkv_w2_2', 'rwkv_a0_2', 'rwkv_a2_2', 'rwkv_k_k_2', 'rwkv_k_a_2',
        'rwkv_r_k_2', 'rwkv_ln_w_2', 'rwkv_ln_b_2', 'w_proj_fox_2', 'w_proj_rwkv_2', 'w_out_2',
        'final_norm_gain_2']


def kernel(**inputs):
    import numpy as _np
    import concourse.bacc as _bacc
    from concourse import mybir as _mybir
    from concourse.bass_utils import run_bass_kernel_spmd as _run

    nc = _bacc.Bacc("TRN2", target_bir_lowering=False, num_devices=1)
    arrays, args = {}, {}
    for name in _INS:
        a = _np.ascontiguousarray(inputs[name])
        arrays[f"in_{name}_dram"] = a
        args[name] = nc.dram_tensor(f"in_{name}_dram", a.shape, _mybir.dt.from_np(a.dtype), kind="ExternalInput").ap()
    out = nc.dram_tensor("out_0_dram", (1, S, D), F32, kind="ExternalOutput").ap()
    build(nc, args, out)
    r = _run(nc, [arrays], core_ids=[0])
    return r.results[0]["out_0_dram"]
```
